# Optimizing a Trainium2 kernel written in Bass

```python
import math
import jax, jax.numpy as jnp
from jax import lax
import numpy as np

D_MODEL = 2048
BATCH = 1
SEQ = 256
DEPTH = 1

GLA_HEADS = 4
GLA_DK = (D_MODEL // 2) // GLA_HEADS
GLA_DV = D_MODEL // GLA_HEADS
GLA_K_WIDTH = GLA_HEADS * GLA_DK
GLA_V_WIDTH = GLA_HEADS * GLA_DV
GLA_GATE_RANK = 16
GLA_GATE_NORMALIZER = 16.0
GLA_CHUNK = 64

DIFF_HEAD_DIM = 128
DIFF_HEADS = D_MODEL // (2 * DIFF_HEAD_DIM)
DIFF_V_DIM = 2 * DIFF_HEAD_DIM
DIFF_QK_WIDTH = DIFF_HEADS * 2 * DIFF_HEAD_DIM
DIFF_V_WIDTH = DIFF_HEADS * DIFF_V_DIM
ATTN_BLOCK = 128
ROPE_THETA = 500000.0
ROPE_DIM = DIFF_HEAD_DIM // 4

FFN_HIDDEN = 5632
CONV_WIDTH = 3
EPS = 1e-6
SUBLN_EPS = 1e-5

IN_SPLITS = [GLA_K_WIDTH, GLA_K_WIDTH, GLA_V_WIDTH, GLA_GATE_RANK, GLA_V_WIDTH,
             DIFF_QK_WIDTH, DIFF_QK_WIDTH, DIFF_V_WIDTH, D_MODEL, D_MODEL]
IN_WIDTH = int(sum(IN_SPLITS))
IN_SPLIT_POINTS = [int(i) for i in np.cumsum(IN_SPLITS)[:-1]]

kernel_name = "hybrid_gla_diffattn_convffn"

def rms_norm(x, g, eps=EPS):
    xf = x.astype(jnp.float32)
    y = xf * lax.rsqrt(jnp.mean(xf * xf, axis=-1, keepdims=True) + eps)
    return (y * g.astype(jnp.float32)).astype(x.dtype)

def lambda_init_fn(layer_idx):
    return 0.8 - 0.6 * math.exp(-0.3 * layer_idx)

def rope_partial(x, positions):
    inv_freq = ROPE_THETA ** (-jnp.arange(0, ROPE_DIM, 2, dtype=jnp.float32) / ROPE_DIM)
    ang = positions.astype(jnp.float32)[:, :, None] * inv_freq
    cos = jnp.cos(ang)[:, :, None, :]
    sin = jnp.sin(ang)[:, :, None, :]
    xr = x[..., :ROPE_DIM].astype(jnp.float32)
    x1, x2 = xr[..., :ROPE_DIM // 2], xr[..., ROPE_DIM // 2:]
    rot = jnp.concatenate([x1 * cos - x2 * sin, x2 * cos + x1 * sin], axis=-1)
    return jnp.concatenate([rot.astype(x.dtype), x[..., ROPE_DIM:]], axis=-1)

def gla_chunked(q, k, v, log_decay):
    B, T, H, dk = q.shape
    dv = v.shape[-1]
    C = GLA_CHUNK
    N = T // C

    def to_chunks(a):
        return a.reshape(B, N, C, H, a.shape[-1]).transpose(0, 3, 1, 2, 4)

    qf = to_chunks(q.astype(jnp.float32) * (dk ** -0.5))
    kf = to_chunks(k.astype(jnp.float32))
    vf = to_chunks(v.astype(jnp.float32))
    b = jnp.cumsum(to_chunks(log_decay.astype(jnp.float32)), axis=3)
    b_last = b[:, :, :, -1:, :]

    q_dec = qf * jnp.exp(b)
    k_inv = kf * jnp.exp(-b)
    k_tail = kf * jnp.exp(b_last - b)

    causal = jnp.tril(jnp.ones((C, C), dtype=bool))
    A = jnp.einsum('bhncd,bhnsd->bhncs', q_dec, k_inv)
    A = jnp.where(causal, A, 0.0)
    o_intra = jnp.einsum('bhncs,bhnse->bhnce', A, vf)

    chunk_kv = jnp.einsum('bhncd,bhnce->bhnde', k_tail, vf)
    chunk_decay = jnp.exp(b_last[:, :, :, 0, :])

    def step(S, inp):
        kv_n, dec_n = inp
        return S * dec_n[..., None] + kv_n, S

    S0 = jnp.zeros((B, H, dk, dv), jnp.float32)
    _, S_in = lax.scan(step, S0, (jnp.moveaxis(chunk_kv, 2, 0), jnp.moveaxis(chunk_decay, 2, 0)))
    S_in = jnp.moveaxis(S_in, 0, 2)
    o_inter = jnp.einsum('bhncd,bhnde->bhnce', q_dec, S_in)

    o = o_intra + o_inter
    return o.transpose(0, 2, 3, 1, 4).reshape(B, T, H, dv)

def diff_attention(q, k, v, lam):
    B, T, H2, d = q.shape
    H = H2 // 2
    NB = T // ATTN_BLOCK
    qh = jnp.transpose(q, (0, 2, 1, 3)).astype(jnp.float32) * (d ** -0.5)
    kh = jnp.transpose(k, (0, 2, 1, 3)).astype(jnp.float32)
    vh = jnp.transpose(v, (0, 2, 1, 3)).astype(jnp.float32)
    q_blocks = qh.reshape(B, H2, NB, ATTN_BLOCK, d).transpose(2, 0, 1, 3, 4)
    key_idx = jnp.arange(T)

    def attend(args):
        qb, blk = args
        s = jnp.einsum('bhqd,bhkd->bhqk', qb, kh)
        q_idx = blk * ATTN_BLOCK + jnp.arange(ATTN_BLOCK)
        s = jnp.where(key_idx[None, :] <= q_idx[:, None], s, -jnp.inf)
        p = jax.nn.softmax(s, axis=-1).reshape(B, H, 2, ATTN_BLOCK, T)
        a = p[:, :, 0] - lam * p[:, :, 1]
        return jnp.einsum('bhqk,bhke->bhqe', a, vh)

    o = lax.map(attend, (q_blocks, jnp.arange(NB)))
    return o.transpose(1, 0, 3, 2, 4).reshape(B, T, H, v.shape[-1])

def causal_depthwise_conv(a, w, bias):
    T = a.shape[1]
    a_pad = jnp.pad(a, ((0, 0), (CONV_WIDTH - 1, 0), (0, 0)))
    out = bias
    for j in range(CONV_WIDTH):
        out = out + a_pad[:, j:j + T, :] * w[j]
    return out

def setup_inputs(seed: int = 0) -> dict:
    key = jax.random.key(seed)
    ks = jax.random.split(key, 24)
    f32 = jnp.float32
    nrm = lambda k, shape, scale: jax.random.normal(k, shape, f32) * scale
    L = DEPTH
    return {
        "x": nrm(ks[0], (BATCH, SEQ, D_MODEL), 1.0),
        "positions": jnp.broadcast_to(jnp.arange(SEQ, dtype=jnp.int32), (BATCH, SEQ)),
        "norm1_g": 1.0 + nrm(ks[1], (L, D_MODEL), 0.02),
        "w_in": nrm(ks[2], (L, D_MODEL, IN_WIDTH), D_MODEL ** -0.5),
        "w_gk_up": nrm(ks[3], (L, GLA_GATE_RANK, GLA_K_WIDTH), GLA_GATE_RANK ** -0.5),
        "b_gk": nrm(ks[4], (L, GLA_K_WIDTH), 0.01),
        "gla_norm_g": 1.0 + nrm(ks[5], (L, GLA_DV), 0.02),
        "q_norm_g": 1.0 + nrm(ks[6], (L, DIFF_HEAD_DIM), 0.02),
        "k_norm_g": 1.0 + nrm(ks[7], (L, DIFF_HEAD_DIM), 0.02),
        "lambda_q1": nrm(ks[8], (L, DIFF_HEAD_DIM), 0.1),
        "lambda_k1": nrm(ks[9], (L, DIFF_HEAD_DIM), 0.1),
        "lambda_q2": nrm(ks[10], (L, DIFF_HEAD_DIM), 0.1),
        "lambda_k2": nrm(ks[11], (L, DIFF_HEAD_DIM), 0.1),
        "subln_g": 1.0 + nrm(ks[12], (L, DIFF_V_DIM), 0.02),
        "w_branch": nrm(ks[13], (L, GLA_V_WIDTH + DIFF_V_WIDTH, D_MODEL), GLA_V_WIDTH ** -0.5),
        "w_out": nrm(ks[14], (L, D_MODEL, D_MODEL), D_MODEL ** -0.5),
        "norm2_g": 1.0 + nrm(ks[15], (L, D_MODEL), 0.02),
        "w_ffn_up": nrm(ks[16], (L, D_MODEL, 2 * FFN_HIDDEN), D_MODEL ** -0.5),
        "conv_w": nrm(ks[17], (L, CONV_WIDTH, FFN_HIDDEN), CONV_WIDTH ** -0.5),
        "conv_b": nrm(ks[18], (L, FFN_HIDDEN), 0.01),
        "w_ffn_down": nrm(ks[19], (L, FFN_HIDDEN, D_MODEL), FFN_HIDDEN ** -0.5),
    }

def reference(x, positions, norm1_g, w_in, w_gk_up, b_gk, gla_norm_g, q_norm_g, k_norm_g,
              lambda_q1, lambda_k1, lambda_q2, lambda_k2, subln_g, w_branch, w_out,
              norm2_g, w_ffn_up, conv_w, conv_b, w_ffn_down):
    B, T, _ = x.shape
    for l in range(DEPTH):
        lambda_init = lambda_init_fn(l)
        h = rms_norm(x, norm1_g[l])
        u = h @ w_in[l]
        (g_q, g_k, g_v, g_lr, g_out, d_q, d_k, d_v, m_gla, m_diff) = jnp.split(u, IN_SPLIT_POINTS, axis=-1)

        gk = (g_lr @ w_gk_up[l] + b_gk[l]).astype(jnp.float32)
        log_decay = jax.nn.log_sigmoid(gk) / GLA_GATE_NORMALIZER
        o_gla = gla_chunked(g_q.reshape(B, T, GLA_HEADS, GLA_DK),
                            g_k.reshape(B, T, GLA_HEADS, GLA_DK),
                            g_v.reshape(B, T, GLA_HEADS, GLA_DV),
                            log_decay.reshape(B, T, GLA_HEADS, GLA_DK)).astype(x.dtype)
        o_gla = rms_norm(o_gla, gla_norm_g[l]) * jax.nn.silu(g_out.reshape(B, T, GLA_HEADS, GLA_DV))
        o_gla = o_gla.reshape(B, T, GLA_V_WIDTH)

        q = rms_norm(d_q.reshape(B, T, 2 * DIFF_HEADS, DIFF_HEAD_DIM), q_norm_g[l])
        k = rms_norm(d_k.reshape(B, T, 2 * DIFF_HEADS, DIFF_HEAD_DIM), k_norm_g[l])
        q = rope_partial(q, positions)
        k = rope_partial(k, positions)
        lam = (jnp.exp(jnp.sum(lambda_q1[l].astype(jnp.float32) * lambda_k1[l].astype(jnp.float32)))
               - jnp.exp(jnp.sum(lambda_q2[l].astype(jnp.float32) * lambda_k2[l].astype(jnp.float32)))
               + lambda_init)
        o_diff = diff_attention(q, k, d_v.reshape(B, T, DIFF_HEADS, DIFF_V_DIM), lam).astype(x.dtype)
        o_diff = rms_norm(o_diff, subln_g[l], SUBLN_EPS) * (1.0 - lambda_init)
        o_diff = o_diff.reshape(B, T, DIFF_V_WIDTH)

        y_gla = o_gla @ w_branch[l][:GLA_V_WIDTH]
        y_diff = o_diff @ w_branch[l][GLA_V_WIDTH:]
        mixed = jax.nn.sigmoid(m_gla) * y_gla + jax.nn.sigmoid(m_diff) * y_diff
        x = x + mixed @ w_out[l]

        h2 = rms_norm(x, norm2_g[l])
        up = h2 @ w_ffn_up[l]
        a, val = up[..., :FFN_HIDDEN], up[..., FFN_HIDDEN:]
        a = causal_depthwise_conv(a, conv_w[l], conv_b[l])
        x = x + (jax.nn.silu(a) * val) @ w_ffn_down[l]
    return x


_drawn_inputs = setup_inputs


def setup_inputs(seed=0):
    import zlib

    import numpy as np

    out = dict(_drawn_inputs(seed))
    spreads = {}
    factors = {'norm1_g': 2.693,
     'b_gk': 8.0,
     'gla_norm_g': 8.0,
     'q_norm_g': 6.256,
     'k_norm_g': 6.292,
     'lambda_k1': 2.879,
     'subln_g': 6.972,
     'norm2_g': 4.053,
     'conv_b': 8.0}
    for name, (base, spread) in spreads.items():
        noise = np.random.default_rng([zlib.crc32(name.encode()), seed]).standard_normal(out[name].shape)
        drawn = base * np.exp(spread * noise) if base else spread * noise
        out[name] = __import__('jax').numpy.asarray(drawn.astype(out[name].dtype))
    for name, factor in factors.items():
        out[name] = (out[name] * factor).astype(out[name].dtype)
    return out
```

```python
import math
from contextlib import ExitStack

import numpy as np

import concourse.bass as bass
from concourse import mybir

F32 = mybir.dt.float32
F32R = mybir.dt.float32r
I32 = mybir.dt.int32
U32 = mybir.dt.uint32
ALU = mybir.AluOpType
ACT = mybir.ActivationFunctionType
AX = mybir.AxisListType

P = 128
T = 256
TT = T // P
D = 2048
KT = D // P
NB = 512
CHUNK_KT = 4
PIECE_KT = 2

GLA_HEADS = 4
GLA_DK = 256
GLA_DV = 512
GLA_RANK = 16
GLA_NORMALIZER = 16.0
C = 64
DIFF_PAIRS = 4
DH = 128
ROPE = 32
ROPE_THETA = 500000.0
FFN = 5632
FFN_GROUPS = FFN // NB
GROUPS = D // NB
EPS = 1e-6
SUBLN_EPS = 1e-5
LAMBDA_INIT = 0.8 - 0.6 * math.exp(-0.3 * 0)

C_GV = 2 * GLA_HEADS * GLA_DK
C_LR = C_GV + GLA_HEADS * GLA_DV
C_GOUT = C_LR + GLA_RANK
C_DQ = C_GOUT + D
C_DK = C_DQ + D
C_DV = C_DK + D
C_MG = C_DV + D
C_MD = C_MG + D

BLOCK = 8
GLA0, GLA_N = 0, 3 * BLOCK
DIFF0, DIFF_N = GLA0 + GLA_HEADS * GLA_N, 3 * BLOCK
BR0, BR_N = DIFF0 + DIFF_PAIRS * DIFF_N, 4 * BLOCK
OUT0 = BR0 + GROUPS * BR_N
FFN0 = OUT0 + 4 * BLOCK
FFN_N = 3 * BLOCK
LAST = FFN_GROUPS - 1
END0 = FFN0 + FFN_GROUPS * FFN_N - BLOCK


def ffn_base(f):
    return f * FFN_N + (FFN0 - BLOCK)


def two_pi_pieces(n):
    left, out = 2.0 * math.pi, []
    for _ in range(n - 1):
        step = 2.0 ** (math.floor(math.log2(left)) - 6)
        out.append(math.floor(left / step) * step)
        left -= out[-1]
    return out + [float(np.float32(left))]


TWO_PI = two_pi_pieces(5)
ROUND = 1.5 * 2.0 ** 23


def hybrid_block_kernel(nc, x, positions, norm1_g, w_in, w_gk_up, b_gk, gla_norm_g, q_norm_g, k_norm_g,
                        lambda_q1, lambda_k1, lambda_q2, lambda_k2, subln_g, w_branch, w_out,
                        norm2_g, w_ffn_up, conv_w, conv_b, w_ffn_down, out):
    with ExitStack() as ctx:
        KB = 1024
        base = -(-nc.sbuf_base // 64) * 64

        def at(name, offset, shape, dt=F32):
            return nc.alloc_sbuf_tensor_at(name, [P] + shape, dt, offset=base + int(offset))

        def sem(name):
            return ctx.enter_context(nc.semaphore(name))

        raw = at("raw", 0, [4, CHUNK_KT, NB])
        whi = at("whi", 32 * KB, [4, PIECE_KT, NB], F32R)
        wlo = at("wlo", 48 * KB, [4, PIECE_KT, NB], F32R)
        hT_hi = at("hT_hi", 64 * KB, [KT, T], F32R)
        hT_lo = at("hT_lo", 80 * KB, [KT, T], F32R)
        glaT_hi = at("glaT_hi", 96 * KB, [KT, T], F32R)
        glaT_lo = at("glaT_lo", 112 * KB, [KT, T], F32R)
        resid = at("resid", 96 * KB, [TT, D])
        normed = at("normed", 112 * KB, [TT, D])
        diffT_hi = at("diffT_hi", 128 * KB, [KT, T], F32R)
        diffT_lo = at("diffT_lo", 144 * KB, [KT, T], F32R)
        mixT_hi = at("mixT_hi", 160 * KB, [KT, T], F32R)
        mixT_lo = at("mixT_lo", 176 * KB, [KT, T], F32R)
        wlr_raw = at("wlr_raw", 128 * KB, [KT, P])
        wlr_hi = at("wlr_hi", 136 * KB, [KT, P], F32R)
        wlr_lo = at("wlr_lo", 144 * KB, [KT, P], F32R)
        gkx = at("gkx", 152 * KB, [8, T])
        g_exp = at("g_exp", 128 * KB, [TT * NB])
        g_silu = at("g_silu", 132 * KB, [TT, NB])
        g_on = at("g_on", 136 * KB, [TT, NB])
        g_og = at("g_og", 140 * KB, [TT, NB])
        g_v = at("g_v", 144 * KB, [TT, NB])
        g_junk = at("g_junk", 148 * KB, [TT, NB])
        o = 160 * KB
        dec = at("dec", o, [2, T])
        gmin = at("gmin", o + 2 * KB, [2, T])
        cum = at("cum", o + 4 * KB, [2, T])
        e_pos = at("e_pos", o + 6 * KB, [2, T])
        e_neg = at("e_neg", o + 8 * KB, [2, T])
        e_tail = at("e_tail", o + 10 * KB, [2, 2, C])
        e_tile = at("e_tile", o + 11 * KB, [2, P])
        e_q3 = at("e_q3", o + 12 * KB, [2, C])
        q_dec = at("q_dec", o + 12.5 * KB, [2, T])
        k_inv = at("k_inv", o + 14.5 * KB, [2, T])
        k_mix = at("k_mix", o + 16.5 * KB, [2, T])
        k_tile = at("k_tile", o + 18.5 * KB, [2, P])
        q_3 = at("q_3", o + 19.5 * KB, [2, C])
        AT = at("AT", o + 20 * KB, [3, P])
        reset = at("reset", o + 21.5 * KB, [T])
        rows = at("rows", o + 22.5 * KB, [3, P])
        wup = at("wup", o + 24 * KB, [GLA_HEADS * GLA_DK])
        lam_v = at("lam_v", o + 28 * KB, [4, P])
        qk_g = at("qk_g", o + 30 * KB, [2, P])
        lam_p = at("lam_p", o + 31 * KB, [2, P])
        sq = at("sq", o, [8, DH])
        rot = at("rot", o + 4 * KB, [4, 8, ROPE // 2])
        qT = at("qT", o + 6 * KB, [4, T])
        kT = at("kT", o + 10 * KB, [4, T])
        d_v = at("d_v", o + 14 * KB, [TT, NB])
        prob = at("prob", o + 18 * KB, [4, 3 * P])
        att = at("att", o + 24 * KB, [2, 3 * P])
        attT = at("attT", o + 27 * KB, [2, 3 * P])
        o = 192 * KB
        lrT = at("lrT", o, [T])
        qn = at("qn", o, [TT, 4, DH])
        kn = at("kn", o + 4 * KB, [TT, 4, DH])
        gate_g = at("gate_g", o, [4, T])
        gate_d = at("gate_d", o + 4 * KB, [4, T])
        d_on = at("d_on", o + 8 * KB, [TT, NB])
        o += 12 * KB
        ident = at("ident", o, [P])
        keep = at("keep", o + 512, [P])
        causal = at("causal", o + 1024, [T])
        cols = at("cols", o + 2048, [224])
        rope_t = at("rope_t", o + 2048 + 896, [6, TT, ROPE // 2])
        small = at("small", o + 2048 + 896 + 768, [44])
        assert base + o + 2048 + 896 + 768 + 176 <= nc.sbuf_usable_end
        xn2 = at("xn2", 128 * KB, [TT, D])
        conv = at("conv", 144 * KB, [4, T])
        hid_hi = at("hid_hi", 148 * KB, [4, T], F32R)
        hid_lo = at("hid_lo", 152 * KB, [4, T], F32R)
        last_hi = at("last_hi", 156 * KB, [4, T], F32R)
        last_lo = at("last_lo", 128 * KB, [4, T], F32R)

        V_N1, V_N2, V_BGK, V_GLA, V_SUB, V_CW0 = 0, 16, 32, 40, 44, 46
        V_CW1, V_CW2, V_CB = 90, 134, 178
        ss_x, rs_x = small[:, 0:2], small[:, 2:4]
        eps_c, sub_eps_c = small[:, 4:5], small[:, 5:6]
        one_c, zero_c = small[:, 6:7], small[:, 7:8]
        neg_lam = small[:, 8:9]
        lam2 = small[:, 9:11]
        pos_i = small[:, 11:13]
        inv_f = small[:, 13:29]
        ss_out = small[:, 29:37]
        tiny = at("tiny", 31.5 * KB + 160 * KB, [96])
        bl = tiny[:, 0:8]
        bl01 = tiny[:, 8:10]
        g_ss, g_rs = tiny[:, 10:12], tiny[:, 12:14]
        dq_ss, dq_rs = tiny[:, 14:22], tiny[:, 22:30]
        dk_ss, dk_rs = tiny[:, 30:38], tiny[:, 38:46]
        s_max, s_nmax = tiny[:, 46:54], tiny[:, 54:62]
        p_sum, p_inv = tiny[:, 62:70], tiny[:, 70:78]
        p_lam = tiny[:, 78:82]
        o_ss, o_rs = tiny[:, 82:86], tiny[:, 86:90]

        acc_a, acc_b, acc_c, mix = (ctx.enter_context(nc.psum_tensor(n, [P, 2 * NB], F32))
                                    for n in ("acc_a", "acc_b", "acc_c", "mix"))

        def stage(pair):
            b = pair % 6
            return (acc_b, acc_c, mix)[b // 2][:, (b % 2) * NB:(b % 2 + 1) * NB]

        raw_landed = [sem(f"raw_landed{i}") for i in range(4)]
        keys_landed = [sem(f"keys_landed{i}") for i in range(4)]
        hi_ready = sem("hi_ready")
        lo_ready = sem("lo_ready")
        pieces_used = sem("pieces_used")
        x_landed = [sem("x_landed0"), sem("x_landed1")]
        wlr_landed, small_landed = sem("wlr_landed"), sem("small_landed")
        resid_landed = sem("resid_landed")
        out_stored = sem("out_stored")
        consts_ready, const_step = sem("consts_ready"), sem("const_step")
        cols_T, cols_ready = sem("cols_T"), sem("cols_ready")
        scale_ready = sem("scale_ready")
        wlr_hi_ready, wlr_lo_ready = sem("wlr_hi_ready"), sem("wlr_lo_ready")
        sumsq_act, sumsq_dve = sem("sumsq_act"), sem("sumsq_dve")
        norm_ln, norm_rs = sem("norm_ln"), sem("norm_rs")
        normed_act, normed_dve = sem("normed_act"), sem("normed_dve")
        norm_T, norm_hi, norm_lo = sem("norm_T"), sem("norm_hi"), sem("norm_lo")
        lr_done, lr_ready, gk_done, gkx_ready = sem("lr_done"), sem("lr_ready"), sem("gk_done"), sem("gkx_ready")
        rope_step, rope_arg, rope_sin, rope_ready = sem("rope_step"), sem("rope_arg"), sem("rope_sin"), sem("rope_ready")
        lam_dot, lam_exp, lam_ready = sem("lam_dot"), sem("lam_exp"), sem("lam_ready")
        gk_abs, gk_exp, gk_ln = sem("gk_abs"), sem("gk_exp"), sem("gk_ln")
        gk_min, gk_gate, cum_ready, bl_ready = sem("gk_min"), sem("gk_gate"), sem("cum_ready"), sem("bl_ready")
        bl_scaled = sem("bl_scaled")
        e_ready, operands_ready, A_done = sem("e_ready"), sem("operands_ready"), sem("A_done")
        AT_ready, gv_ready, go_done = sem("AT_ready"), sem("gv_ready"), sem("go_done")
        go_sumsq, go_ln, go_rs, go_normed = sem("go_sumsq"), sem("go_ln"), sem("go_rs"), sem("go_normed")
        gout_exp, gout_one, gout_inv, gout_silu = sem("gout_exp"), sem("gout_one"), sem("gout_inv"), sem("gout_silu")
        og_ready, og_T, glaT_hi_ready, glaT_lo_ready = sem("og_ready"), sem("og_T"), sem("glaT_hi_ready"), sem("glaT_lo_ready")
        q_sq, q_ss, q_ln, q_rs, q_normed = (sem("q_" + n) for n in ("sq", "ss", "ln", "rs", "normed"))
        k_sq, k_ss, k_ln, k_rs, k_normed = (sem("k_" + n) for n in ("sq", "ss", "ln", "rs", "normed"))
        q_scaled, q_turned, q_roped = sem("q_scaled"), sem("q_turned"), sem("q_roped")
        k_scaled, k_turned, k_roped = sem("k_scaled"), sem("k_turned"), sem("k_roped")
        q_T, k_T, qT_ready, kT_ready, dv_ready = sem("q_T"), sem("k_T"), sem("qT_ready"), sem("kT_ready"), sem("dv_ready")
        scores_done = [sem("scores01_done"), sem("scores23_done")]
        max_found = [sem("max01_found"), sem("max23_found")]
        max_ready = [sem("max01_ready"), sem("max23_ready")]
        exp_ready = [sem("exp01_ready"), sem("exp23_ready")]
        sums_inv, sums_lam, att_second, att_ready = sem("sums_inv"), sem("sums_lam"), sem("att_second"), sem("att_ready")
        att_T, attT_ready, pv_done = sem("att_T"), sem("attT_ready"), sem("pv_done")
        do_sumsq, do_ln, do_rs, do_normed = sem("do_sumsq"), sem("do_ln"), sem("do_rs"), sem("do_normed")
        do_T, diffT_hi_ready, diffT_lo_ready = sem("do_T"), sem("diffT_hi_ready"), sem("diffT_lo_ready")
        gates_ready, yg_gated, yd_gated, mixed_ready = sem("gates_ready"), sem("yg_gated"), sem("yd_gated"), sem("mixed_ready")
        mixT_hi_ready, mixT_lo_ready = sem("mixT_hi_ready"), sem("mixT_lo_ready")
        x1_ready, x1_sumsq = sem("x1_ready"), sem("x1_sumsq")
        conv_first, conv_second, conv_ready, conv_silu = sem("conv_first"), sem("conv_second"), sem("conv_ready"), sem("conv_silu")
        hid_ready, hid_hi_ready, hid_lo_ready, down_added = sem("hid_ready"), sem("hid_hi_ready"), sem("hid_lo_ready"), sem("down_added")

        x_v = x[0].rearrange("(t p) n -> p t n", p=P)
        out_v = out[0].rearrange("(t p) n -> p t n", p=P)
        w_in_v = w_in[0].rearrange("(k p) n -> p k n", p=P)
        w_br_v = w_branch[0].rearrange("(k p) n -> p k n", p=P)
        w_out_v = w_out[0].rearrange("(k p) n -> p k n", p=P)
        w_up_v = w_ffn_up[0].rearrange("(k p) n -> p k n", p=P)
        w_down_v = w_ffn_down[0].rearrange("(g k p) n -> p g k n", k=4, p=P)

        block = ctx.enter_context(nc.Block())

        @block.sync
        def _(sp):
            def load(first, j, src, width=NB):
                slot = j % 4
                if isinstance(first, int):
                    if first // 2 + j >= 4:
                        sp.wait_ge(lo_ready, first + 2 * j - 6)
                else:
                    split = sp.snap(sp.to_reg(first + 2 * j - 6))
                    sp.wait_ge(x_landed[0], 16)
                    sp.wait_ge(lo_ready, split)
                sp.dma_start(raw[:, slot, :, 0:width], src).then_inc(raw_landed[slot], 16)

            def load_block(first, b, view, col, k0=0):
                for q in range(4):
                    load(first, 4 * b + q, view[:, k0 + 4 * q:k0 + 4 * q + 4, bass.ds(col, NB)])

            def gla(h):
                first = GLA_N * h + GLA0
                for q in range(4):
                    if isinstance(h, int) and q == 1:
                        sp.dma_start(wlr_raw[:, :, :], w_in_v[:, :, C_LR:C_LR + P]).then_inc(wlr_landed, 16)
                    load(first, q, w_in_v[:, 4 * q:4 * q + 4, bass.ds(h * GLA_DK, GLA_DK)], GLA_DK)
                    sp.dma_start(raw[:, q, :, GLA_DK:2 * GLA_DK],
                                 w_in_v[:, 4 * q:4 * q + 4, bass.ds(h * GLA_DK + GLA_HEADS * GLA_DK, GLA_DK)])\
                      .then_inc(keys_landed[q], 16)
                load_block(first, 1, w_in_v, h * NB + C_GV)
                load_block(first, 2, w_in_v, h * NB + C_GOUT)

            def diff(i):
                first = DIFF_N * i + DIFF0
                load_block(first, 0, w_in_v, i * NB + C_DQ)
                load_block(first, 1, w_in_v, i * NB + C_DK)
                load_block(first, 2, w_in_v, i * NB + C_DV)

            def branch(g):
                first = BR_N * g + BR0
                load_block(first, 0, w_in_v, g * NB + C_MG)
                load_block(first, 1, w_in_v, g * NB + C_MD)
                load_block(first, 2, w_br_v, g * NB)
                load_block(first, 3, w_br_v, g * NB, KT)

            def down(first, b, f):
                for q in range(4):
                    load(first, 4 * b + q, w_down_v[:, bass.ds(f, 1), :, q * NB:(q + 1) * NB].rearrange("p g k n -> p (g k) n"))

            sp.dma_start(resid[:, 0], x_v[:, 0]).then_inc(x_landed[0], 16)
            sp.dma_start(resid[:, 1], x_v[:, 1]).then_inc(x_landed[1], 16)
            sp.wait_ge(small_landed, 17 * 16)
            gla(0)
            with sp.Fori(1, GLA_HEADS) as h:
                gla(h)
            with sp.Fori(0, DIFF_PAIRS) as i:
                diff(i)
            with sp.Fori(0, GROUPS) as g:
                branch(g)
            load_block(OUT0, 0, w_out_v, 0)
            sp.wait_ge(pieces_used, OUT0 - BLOCK)
            sp.dma_start(resid[:, :, :], x_v).then_inc(resid_landed, 16)
            for b in range(1, 4):
                load_block(OUT0, b, w_out_v, b * NB)
            load_block(FFN0, 0, w_up_v, 0)
            load_block(FFN0, 1, w_up_v, FFN)
            with sp.Fori(1, LAST) as f:
                load_block(ffn_base(f), 0, w_up_v, f * NB)
                down(ffn_base(f), 1, f - 1)
                load_block(ffn_base(f), 2, w_up_v, f * NB + FFN)
            load_block(ffn_base(LAST), 0, w_up_v, LAST * NB)
            load_block(ffn_base(LAST), 1, w_up_v, LAST * NB + FFN)
            down(ffn_base(LAST), 2, LAST - 1)
            down(END0, 0, FFN_GROUPS - 1)
            for q in range(4):
                sp.wait_ge(down_added, 4 * (FFN_GROUPS - 1) + q + 1)
                sp.dma_start(out_v[:, :, q * NB:(q + 1) * NB], resid[:, :, q * NB:(q + 1) * NB]).then_inc(out_stored, 16)
            sp.wait_ge(out_stored, 4 * 16)

        @block.scalar
        def _(act):
            def fn(o_, i_, f, **kw):
                return nc.scalar.activation(o_, i_, f, **kw)

            def split_hi(first, j, keys=None):
                slot = j % 4
                if j % 2 == 0:
                    act.wait_ge(raw_landed[(j // 2) % 4], (first + 8 * (j // 8) + 8) * 2)
                    if keys is not None:
                        act.wait_ge(keys_landed[j // 2], keys)
                if not (isinstance(first, int) and first + j < 4):
                    act.wait_ge(pieces_used, first + j - 3)
                fn(whi[:, slot], raw[:, (j // 2) % 4, 2 * (j % 2):2 * (j % 2) + 2], ACT.Copy).then_inc(hi_ready, 1)

            def rsqrt(src, dst, width, eps, ready, ln_sem, rs_sem, n):
                act.wait_ge(ready, n)
                fn(dst, src, ACT.Ln, scale=1.0 / width, bias=eps).then_inc(ln_sem, 1)
                act.wait_ge(ln_sem, n)
                fn(dst, dst, ACT.Exp, scale=-0.5).then_inc(rs_sem, 1)

            def norm_rows(src, dst, sums, n):
                act.wait_ge(norm_rs, n)
                if n == 2:
                    act.wait_ge(pieces_used, FFN0)
                for b in range(4):
                    fn(dst[:, 0, b * NB:(b + 1) * NB], src[:, 0, b * NB:(b + 1) * NB], ACT.Copy,
                       scale=rs_x[:, 0:1]).then_inc(normed_act, 1)

            def norm_pair(pair, col, n):
                act.wait_ge(norm_T, 8 * (n - 1) + pair + 1)
                for k in (2 * pair, 2 * pair + 1):
                    last = fn(hT_hi[:, k], stage(pair)[:, (k % 2) * T:(k % 2 + 1) * T], ACT.Copy,
                              scale=cols[:, col + k:col + k + 1])
                last.then_inc(norm_hi, 1)

            def decay_inputs(j):
                if j == 2:
                    act.wait_ge(wlr_landed, 16)
                    fn(wlr_hi[:, :, :], wlr_raw[:, :, :], ACT.Copy).then_inc(wlr_hi_ready, 1)
                if j == 11:
                    act.wait_ge(lr_done, 1)
                    fn(lrT[0:GLA_RANK, :], mix[0:GLA_RANK, 0:T], ACT.Copy).then_inc(lr_ready, 1)
                if j in (12, 13):
                    act.wait_ge(gk_done, j - 11)
                    for k in range(4 * (j - 12), 4 * (j - 12) + 4):
                        last = fn(gkx[:, k], (acc_c, mix)[k // 4][:, (k % 4) * T:(k % 4 + 1) * T], ACT.Identity,
                                  bias=cols[:, V_BGK + k:V_BGK + k + 1])
                    last.then_inc(gkx_ready, 1)

            def decays(h, n):
                if n is not None:
                    act.wait_ge(gk_gate, n - 1)
                fn(dec[:, :, :], gkx[:, bass.ds(2 * h, 2), :], ACT.Abs).then_inc(gk_abs, 1)
                act.wait_ge(gk_abs, h + 1)
                fn(dec[:, :, :], dec[:, :, :], ACT.Exp, scale=-1.0).then_inc(gk_exp, 1)
                act.wait_ge(gk_exp, h + 1)
                fn(dec[:, :, :], dec[:, :, :], ACT.Ln, bias=one_c).then_inc(gk_ln, 1)

            def exponentials(h, first_head):
                act.wait_ge(bl_ready, h + 1)
                if not first_head:
                    act.wait_ge(operands_ready, h)
                s = 1.0 / GLA_NORMALIZER
                fn(e_pos[:, :, :], cum[:, :, :], ACT.Exp, scale=s)
                fn(e_neg[:, :, :], cum[:, :, :], ACT.Exp, scale=-s)

            def exponentials_tail(h):
                s = 1.0 / GLA_NORMALIZER
                for f in range(2):
                    for c in range(2):
                        fn(e_tail[:, f, c], cum[:, f, 2 * c * C:(2 * c + 1) * C], ACT.Exp, scale=-s,
                           bias=bl[:, 4 * f + 2 * c:4 * f + 2 * c + 1])
                    fn(e_tile[:, f, 0:C], cum[:, f, 0:C], ACT.Exp, scale=-s, bias=bl01[:, f:f + 1])
                    fn(e_tile[:, f, C:P], cum[:, f, C:P], ACT.Exp, scale=-s, bias=bl[:, 4 * f + 1:4 * f + 2])
                    last = fn(e_q3[:, f], cum[:, f, 3 * C:4 * C], ACT.Exp, scale=s, bias=bl[:, 4 * f + 2:4 * f + 3])
                last.then_inc(e_ready, 1)

            def gla(h, tail):
                first = GLA_N * h + GLA0
                first_head = tail is None
                at_decays, at_exp, at_exp_tail = (14, 15, 16) if first_head else (0, 5, 6)
                for j in range(GLA_N):
                    if first_head and j < KT // 2:
                        norm_pair(j, V_N1, 1)
                    split_hi(first, j, 16 * h + 16 if j < BLOCK else None)
                    if first_head:
                        decay_inputs(j)
                    if j == at_decays:
                        if first_head:
                            act.wait_ge(gkx_ready, 2)
                        decays(h, None if first_head else h + 1)
                    if j == at_exp:
                        exponentials(h, first_head)
                    if j == at_exp_tail:
                        exponentials_tail(h)
                    if first_head and j == 9:
                        rope_and_lambda()
                    if j == 19:
                        act.wait_ge(pieces_used, first + 2 * BLOCK)
                        if not first_head:
                            act.wait_ge(go_done, h)
                        fn(g_v[:, :, :], acc_b[:, :].rearrange("p (t n) -> p t n", t=TT), ACT.Copy).then_inc(gv_ready, 1)
                    if j == 22:
                        act.wait_ge(go_done, h + 1)
                        for t, ps in enumerate((mix[:, NB:2 * NB], mix[:, 0:NB])):
                            last = fn(g_junk[:, t], ps, ACT.Square, accum_out=g_ss[:, t:t + 1])
                        last.then_inc(go_sumsq, 1)
                        rsqrt(g_ss, g_rs, GLA_DV, eps_c, go_sumsq, go_ln, go_rs, h + 1)
                    if j == 23:
                        act.wait_ge(go_rs, h + 1)
                        if not first_head:
                            act.wait_ge(og_ready, h)
                        for t, ps in enumerate((mix[:, NB:2 * NB], mix[:, 0:NB])):
                            last = fn(g_on[:, t], ps, ACT.Copy, scale=g_rs[:, t:t + 1])
                        last.then_inc(go_normed, 1)
                    if tail is not None:
                        gla_tail(j, tail)

            def gla_tail(j, n):
                if j == 3:
                    act.wait_ge(pieces_used, GLA_N * n + GLA0)
                    fn(g_exp[:, :], acc_c[:, :], ACT.Exp, scale=-1.0).then_inc(gout_exp, 1)
                if j == 13:
                    act.wait_ge(og_T, n)
                    for f in range(4):
                        last = fn(glaT_hi[:, bass.ds(4 * n - 4 + f, 1), :].rearrange("p a t -> p (a t)"),
                                  mix[:, f * T:(f + 1) * T], ACT.Copy, scale=cols[:, V_GLA + f:V_GLA + f + 1])
                    last.then_inc(glaT_hi_ready, 1)

            def rope_and_lambda():
                nc.scalar.preload_act_table_set("trig_and_small")
                act.wait_ge(rope_arg, 1)
                fn(rope_t[:, 4], rope_t[:, 3], ACT.Sin)
                fn(rope_t[:, 5], rope_t[:, 3], ACT.Sin, scale=0.5).then_inc(rope_sin, 1)
                nc.scalar.preload_act_table_set("natural_log_exp_and_others")
                act.wait_ge(lam_dot, 1)
                fn(lam2, lam2, ACT.Exp).then_inc(lam_exp, 1)

            def diff(i, tail, gtail):
                first = DIFF_N * i + DIFF0
                for j in range(DIFF_N):
                    split_hi(first, j)
                    if tail is not None:
                        diff_tail(j, tail)
                    if gtail is not None:
                        gla_tail(j, gtail)
                    if j == 11:
                        act.wait_ge(pieces_used, first + BLOCK)
                        if gtail is None:
                            act.wait_ge(k_ss, i)
                        fn(sq[:, :, :], acc_a[:, :].rearrange("p (s d) -> p s d", d=DH), ACT.Square).then_inc(q_sq, 1)
                    if j == 12:
                        rsqrt(dq_ss, dq_rs, DH, eps_c, q_ss, q_ln, q_rs, i + 1)
                    if j == 20:
                        act.wait_ge(q_T, i + 1)
                        if gtail is None:
                            act.wait_ge(scores_done[1], i)
                        fn(qT[:, :, :], mix[:, :].rearrange("p (s t) -> p s t", t=T), ACT.Copy).then_inc(qT_ready, 1)
                    if j == 19:
                        act.wait_ge(pieces_used, first + 2 * BLOCK)
                        act.wait_ge(q_ss, i + 1)
                        fn(sq[:, :, :], acc_b[:, :].rearrange("p (s d) -> p s d", d=DH), ACT.Square).then_inc(k_sq, 1)
                    if j == 20:
                        rsqrt(dk_ss, dk_rs, DH, eps_c, k_ss, k_ln, k_rs, i + 1)

            def diff_tail(j, n):
                if j == 1:
                    act.wait_ge(k_T, n)
                    fn(kT[:, :, :], mix[:, :].rearrange("p (s t) -> p s t", t=T), ACT.Copy).then_inc(kT_ready, 1)
                if j == 3:
                    act.wait_ge(pieces_used, DIFF_N * n + DIFF0)
                    fn(d_v[:, :, :], acc_c[:, :].rearrange("p (t n) -> p t n", t=TT), ACT.Copy).then_inc(dv_ready, 1)
                if j in (7, 10):
                    half = (7, 10).index(j)
                    act.wait_ge(max_ready[half], n)
                    for s in (2 * half, 2 * half + 1):
                        for t, a in enumerate((prob[:, s, 0:P], prob[:, s, P:3 * P])):
                            k = 2 * s + t
                            last = fn(a, a, ACT.Exp, scale=DH ** -0.5, bias=s_nmax[:, k:k + 1],
                                      accum_out=p_sum[:, k:k + 1])
                    last.then_inc(exp_ready[half], 1)
                if j == 14:
                    act.wait_ge(att_T, n)
                    for hh in range(2):
                        last = fn(attT[:, hh], mix[:, hh * NB:hh * NB + 3 * P], ACT.Copy)
                    last.then_inc(attT_ready, 1)
                if j == 16:
                    act.wait_ge(pv_done, n)
                    act.wait_ge(k_ss, n)
                    for k in range(4):
                        last = fn(d_on[:, k // 2, (k % 2) * T:(k % 2 + 1) * T], mix[:, k * T:(k + 1) * T], ACT.Square,
                                  accum_out=o_ss[:, k:k + 1])
                    last.then_inc(do_sumsq, 1)
                    rsqrt(o_ss, o_rs, 2 * DH, sub_eps_c, do_sumsq, do_ln, do_rs, n)
                if j == 22:
                    act.wait_ge(do_T, n)
                    for f in range(4):
                        last = fn(diffT_hi[:, bass.ds(4 * n - 4 + f, 1), :].rearrange("p a t -> p (a t)"),
                                  mix[:, f * T:(f + 1) * T], ACT.Copy, scale=cols[:, V_SUB + f % 2:V_SUB + f % 2 + 1])
                    last.then_inc(diffT_hi_ready, 1)

            def branch(g, tail, dtail):
                first = BR_N * g + BR0
                for j in range(BR_N):
                    split_hi(first, j)
                    if dtail is not None:
                        diff_tail(j, dtail)
                    if tail is not None:
                        branch_tail(j, tail)
                    if j == 23:
                        if dtail is not None:
                            nc.scalar.preload_act_table_set("sigmoid_and_others")
                        act.wait_ge(pieces_used, first + 2 * BLOCK)
                        if tail is not None:
                            act.wait_ge(mixT_lo_ready, g)
                        fn(gate_g[:, :, :], acc_a[:, :].rearrange("p (f t) -> p f t", t=T), ACT.Sigmoid)
                        fn(gate_d[:, :, :], acc_b[:, :].rearrange("p (f t) -> p f t", t=T), ACT.Sigmoid).then_inc(gates_ready, 1)

            def branch_tail(j, n):
                if j == 4:
                    act.wait_ge(mixed_ready, n)
                    fn(mixT_hi[:, bass.ds(4 * n - 4, 4), :], gate_g[:, :, :], ACT.Copy).then_inc(mixT_hi_ready, 1)

            def out_sumsq(b):
                act.wait_ge(x1_ready, b + 1)
                if b >= 1:
                    act.wait_ge(x1_sumsq, b)
                for t in range(TT):
                    last = fn(gate_g[:, 2 * t:2 * t + 2].rearrange("p a t -> p (a t)"), resid[:, t, b * NB:(b + 1) * NB],
                              ACT.Square, accum_out=ss_out[:, 4 * t + b:4 * t + b + 1])
                last.then_inc(x1_sumsq, 1)

            def ffn_conv(j, f):
                if j == 11:
                    act.wait_ge(pieces_used, ffn_base(f) + BLOCK if not isinstance(f, int) or f else FFN0 + BLOCK)
                    if not (isinstance(f, int) and f == 0):
                        act.wait_ge(hid_lo_ready, f)
                    for k in range(4):
                        last = fn(conv[:, k], acc_a[:, k * T:(k + 1) * T], ACT.Identity,
                                  scale=cols[:, bass.ds(f * 4 + (V_CW2 + k), 1)],
                                  bias=cols[:, bass.ds(f * 4 + (V_CB + k), 1)])
                    last.then_inc(conv_first, 1)
                if j == 13:
                    act.wait_ge(conv_ready, f + 1)
                    fn(conv[:, :, :], conv[:, :, :], ACT.Silu).then_inc(conv_silu, 1)

            def hidden_hi(n, dst):
                act.wait_ge(hid_ready, n)
                if dst is hid_hi:
                    act.wait_ge(pieces_used, ffn_base(n) - BLOCK)
                fn(dst[:, :, :], conv[:, :, :], ACT.Copy).then_inc(hid_hi_ready, 1)

            nc.scalar.preload_act_table_set("natural_log_exp_and_others")
            for r, c0, v in ((0, V_N1, norm1_g), (0, V_N2, norm2_g), (0, V_BGK, b_gk), (0, V_GLA, gla_norm_g),
                             (0, V_SUB, subln_g), (0, V_CW0, conv_w[:, 0]), (1, V_CW1 - 90, conv_w[:, 1]),
                             (1, V_CW2 - 90, conv_w[:, 2]), (2, 0, conv_b)):
                n = v.shape[-1] // P
                act.dma_start(rows[c0:c0 + n, r, :], v[0].rearrange("(a b) -> a b", b=P)).then_inc(small_landed, 16)
            act.dma_start(wup[0:GLA_RANK, :], w_gk_up[0]).then_inc(small_landed, 16)
            act.dma_start(qk_g[:, 0], q_norm_g.broadcast_to([P, P])).then_inc(small_landed, 16)
            act.dma_start(qk_g[:, 1], k_norm_g.broadcast_to([P, P])).then_inc(small_landed, 16)
            for k, v in enumerate((lambda_q1, lambda_k1, lambda_q2, lambda_k2)):
                act.dma_start(lam_v[:, k], v.broadcast_to([P, P])).then_inc(small_landed, 16)
            act.dma_start(pos_i.bitcast(I32), positions[0].rearrange("(t p) -> p t", p=P),
                          allow_slow_non_contiguous=True).then_inc(small_landed, 16)

            act.wait_ge(x_landed[0], 16)
            fn(normed[:, 0], resid[:, 0], ACT.Square, accum_out=ss_x[:, 0:1]).then_inc(sumsq_act, 1)
            act.wait_ge(consts_ready, 1)
            act.wait_ge(sumsq_dve, 1)
            rsqrt(ss_x, rs_x, D, eps_c, sumsq_act, norm_ln, norm_rs, 1)
            norm_rows(resid, normed, ss_x, 1)
            act.wait_ge(cols_ready, 1)

            gla(0, None)
            with act.Fori(1, GLA_HEADS) as h:
                gla(h, h)
            diff(0, None, GLA_HEADS)
            with act.Fori(1, DIFF_PAIRS) as i:
                diff(i, i, None)
            branch(0, None, DIFF_PAIRS)
            with act.Fori(1, GROUPS) as g:
                branch(g, g, None)
            for j in range(4 * BLOCK):
                split_hi(OUT0, j)
                branch_tail(j, GROUPS)
                if j == 8:
                    nc.scalar.preload_act_table_set("natural_log_exp_and_others")
                if j % 8 == 4 and j > 4:
                    out_sumsq(j // 8 - 1)
            for j in range(2 * BLOCK):
                if 4 <= j < BLOCK:
                    norm_pair(j, V_N2, 2)
                split_hi(FFN0, j)
                if j == 3:
                    out_sumsq(3)
                    rsqrt(ss_x, rs_x, D, eps_c, sumsq_dve, norm_ln, norm_rs, 2)
                    norm_rows(resid, xn2, ss_x, 2)
                    for pair in range(4):
                        norm_pair(pair, V_N2, 2)
                if j == 7:
                    nc.scalar.preload_act_table_set("silu_and_others")
                ffn_conv(j, 0)
            with act.Fori(1, LAST) as f:
                for j in range(FFN_N):
                    split_hi(ffn_base(f), j)
                    if j == 3:
                        hidden_hi(f, hid_hi)
                    ffn_conv(j, f)
            for j in range(FFN_N):
                split_hi(ffn_base(LAST), j)
                if j == 3:
                    hidden_hi(LAST, hid_hi)
                ffn_conv(j, LAST)
                if j == 19:
                    hidden_hi(FFN_GROUPS, last_hi)
            for j in range(BLOCK):
                split_hi(END0, j)

        @block.vector
        def _(dve):
            V = nc.vector

            def split_lo(first, j):
                slot = j % 4
                dve.wait_ge(hi_ready, first + j + 1)
                V.tensor_tensor(wlo[:, slot], raw[:, (j // 2) % 4, 2 * (j % 2):2 * (j % 2) + 2],
                                whi[:, slot].bitcast(F32), ALU.subtract).then_inc(lo_ready, 1)

            def norm_rows(src, dst, n):
                dve.wait_ge(norm_rs, n)
                for b in range(4):
                    V.tensor_scalar(dst[:, 1, b * NB:(b + 1) * NB], src[:, 1, b * NB:(b + 1) * NB], rs_x[:, 1:2], None,
                                    ALU.mult).then_inc(normed_dve, 1)

            def norm_pair(pair, col, n):
                dve.wait_ge(norm_hi, 8 * (n - 1) + pair + 1)
                for k in (2 * pair, 2 * pair + 1):
                    last = V.scalar_tensor_tensor(out=hT_lo[:, k], in0=stage(pair)[:, (k % 2) * T:(k % 2 + 1) * T],
                                                  scalar=cols[:, col + k:col + k + 1], in1=hT_hi[:, k].bitcast(F32),
                                                  op0=ALU.mult, op1=ALU.subtract)
                last.then_inc(norm_lo, 1)

            def rope_and_lambda():
                n_rope = [0]

                def then(ins):
                    n_rope[0] += 1
                    ins.then_inc(rope_step, 1)
                    dve.wait_ge(rope_step, n_rope[0])

                pos, ang, turns, red = (rope_t[:, k] for k in range(4))
                then(V.tensor_copy(pos[:, :, 0], pos_i.bitcast(I32)))
                for t in range(TT):
                    ins = V.tensor_scalar(ang[:, t], inv_f, pos[:, t, 0:1], None, ALU.mult)
                then(ins)
                for unit in (4096.0, 1.0):
                    src = ang
                    then(V.tensor_scalar(turns, src, 1.0 / (2.0 * math.pi * unit), None, ALU.mult))
                    then(V.tensor_scalar(turns, turns, ROUND, None, ALU.add))
                    then(V.tensor_scalar(turns, turns, -ROUND, None, ALU.add))
                    for piece in TWO_PI:
                        then(V.scalar_tensor_tensor(out=ang, in0=turns, scalar=-piece * unit, in1=ang,
                                                    op0=ALU.mult, op1=ALU.add))
                pi = float(np.nextafter(np.float32(math.pi), np.float32(0)))
                V.tensor_scalar(red, ang, pi, -pi, ALU.min, ALU.max).then_inc(rope_arg, 1)
                for k in range(2):
                    ins = V.tensor_tensor_reduce(lam_p[:, k], lam_v[:, 2 * k], lam_v[:, 2 * k + 1], 1.0, 0.0,
                                                 ALU.mult, ALU.add, lam2[:, k:k + 1])
                ins.then_inc(lam_dot, 1)

            def rope_and_lambda_end():
                dve.wait_ge(rope_sin, 1)
                V.scalar_tensor_tensor(out=rope_t[:, 5], in0=rope_t[:, 5], scalar=-2.0, in1=rope_t[:, 5],
                                       op0=ALU.mult, op1=ALU.mult).then_inc(rope_ready, 1)
                dve.wait_ge(rope_ready, 1)
                V.tensor_scalar(rope_t[:, 5], rope_t[:, 5], 1.0, None, ALU.add).then_inc(rope_ready, 1)
                dve.wait_ge(lam_exp, 1)
                V.tensor_tensor(neg_lam, lam2[:, 1:2], lam2[:, 0:1], ALU.subtract).then_inc(lam_ready, 1)
                dve.wait_ge(lam_ready, 1)
                V.tensor_scalar(neg_lam, neg_lam, -LAMBDA_INIT, None, ALU.add).then_inc(lam_ready, 1)

            def cumulate(h, first_head):
                if not first_head:
                    dve.wait_ge(cum_ready, h)
                else:
                    dve.wait_ge(gkx_ready, 2)
                V.tensor_scalar(gmin[:, :, :], gkx[:, bass.ds(2 * h, 2), :], 0.0, None, ALU.min).then_inc(gk_min, 1)
                dve.wait_ge(gk_min, h + 1)
                dve.wait_ge(gk_ln, h + 1)
                V.tensor_tensor(gmin[:, :, :], gmin[:, :, :], dec[:, :, :], ALU.subtract).then_inc(gk_gate, 1)
                dve.wait_ge(gk_gate, h + 1)
                if not first_head:
                    dve.wait_ge(e_ready, h)
                for f in range(2):
                    last = V.tensor_tensor_scan(cum[:, f], reset[:, :], gmin[:, f], 0.0, ALU.mult, ALU.add)
                last.then_inc(cum_ready, 1)
                dve.wait_ge(cum_ready, h + 1)
                V.tensor_scalar(bl.rearrange("p (f c) -> p f c", f=2),
                                cum[:, :, :].rearrange("p f (c t) -> p f c t", t=C)[:, :, :, C - 1],
                                1.0 / GLA_NORMALIZER, None, ALU.mult).then_inc(bl_scaled, 1)
                dve.wait_ge(bl_scaled, h + 1)
                b4 = bl.rearrange("p (f c) -> p f c", f=2)
                V.tensor_tensor(bl01, b4[:, :, 0], b4[:, :, 1], ALU.add).then_inc(bl_ready, 1)

            def gla(h, tail):
                first = GLA_N * h + GLA0
                first_head = tail is None
                qp = acc_a[:, 0:NB].rearrange("p (f t) -> p f t", t=T)
                kp = acc_a[:, NB:2 * NB].rearrange("p (f t) -> p f t", t=T)
                at_cum, at_operands, at_AT = (15, 16, 19) if first_head else (2, 11, 17)
                for j in range(GLA_N):
                    if first_head and j < KT // 2:
                        norm_pair(j, V_N1, 1)
                    split_lo(first, j)
                    if first_head and j == 2:
                        dve.wait_ge(wlr_hi_ready, 1)
                        V.tensor_tensor(wlr_lo[:, :, :], wlr_raw[:, :, :], wlr_hi[:, :, :].bitcast(F32), ALU.subtract)\
                         .then_inc(wlr_lo_ready, 1)
                    if j == at_cum:
                        cumulate(h, first_head)
                    if first_head and j == 7:
                        rope_and_lambda()
                    if j == at_operands:
                        dve.wait_ge(pieces_used, first + BLOCK)
                        dve.wait_ge(e_ready, h + 1)
                        if not first_head:
                            dve.wait_ge(A_done, h)
                        V.scalar_tensor_tensor(out=q_dec[:, :, :], in0=qp, scalar=GLA_DK ** -0.5, in1=e_pos[:, :, :],
                                               op0=ALU.mult, op1=ALU.mult)
                        V.tensor_tensor(k_inv[:, :, :], kp, e_neg[:, :, :], ALU.mult)
                    if j == at_operands + 1:
                        def chunks(a, odd):
                            return a.rearrange("p f (c s t) -> p f c s t", s=2, t=C)[:, :, :, odd]
                        V.tensor_tensor(chunks(k_mix[:, :, :], 0), chunks(kp, 0), e_tail[:, :, :, :], ALU.mult)
                        V.tensor_tensor(chunks(k_mix[:, :, :], 1), chunks(kp, 1), chunks(e_neg[:, :, :], 1), ALU.mult)
                        V.tensor_tensor(k_tile[:, :, :], kp[:, :, 0:P], e_tile[:, :, :], ALU.mult)
                        V.scalar_tensor_tensor(out=q_3[:, :, :], in0=qp[:, :, 3 * C:4 * C], scalar=GLA_DK ** -0.5,
                                               in1=e_q3[:, :, :], op0=ALU.mult, op1=ALU.mult).then_inc(operands_ready, 1)
                    if first_head and j == 14:
                        rope_and_lambda_end()
                    if j == at_AT:
                        dve.wait_ge(A_done, h + 1)
                        if not first_head:
                            dve.wait_ge(go_done, h)
                        V.tensor_copy(AT[:, 2], mix[:, 2 * P:3 * P])
                        dve.wait_ge(consts_ready, 1)
                        for t in range(TT):
                            last = V.copy_predicated(AT[:, t], keep[:, :].bitcast(U32), mix[:, t * P:(t + 1) * P])
                        last.then_inc(AT_ready, 1)
                    if tail is not None:
                        gla_tail(j, tail)

            def gla_tail(j, n):
                if j == 3:
                    dve.wait_ge(gout_exp, n)
                    V.tensor_scalar(g_exp[:, :], g_exp[:, :], 1.0, None, ALU.add).then_inc(gout_one, 1)
                if j == 4:
                    dve.wait_ge(gout_one, n)
                    V.reciprocal(g_exp[:, :], g_exp[:, :]).then_inc(gout_inv, 1)
                if j == 5:
                    dve.wait_ge(gout_inv, n)
                    V.tensor_tensor(g_silu[:, :, :].rearrange("p t n -> p (t n)"), acc_c[:, :], g_exp[:, :],
                                    ALU.mult).then_inc(gout_silu, 1)
                if j == 13:
                    dve.wait_ge(glaT_hi_ready, n)
                    for f in range(4):
                        last = V.scalar_tensor_tensor(
                            out=glaT_lo[:, bass.ds(4 * n - 4 + f, 1), :].rearrange("p a t -> p (a t)"),
                            in0=mix[:, f * T:(f + 1) * T], scalar=cols[:, V_GLA + f:V_GLA + f + 1],
                            in1=glaT_hi[:, bass.ds(4 * n - 4 + f, 1), :].rearrange("p a t -> p (a t)").bitcast(F32),
                            op0=ALU.mult, op1=ALU.subtract)
                    last.then_inc(glaT_lo_ready, 1)

            def head_sums(sq_sem, out_ss, done, n):
                dve.wait_ge(sq_sem, n)
                V.tensor_reduce(out_ss, sq[:, :, :], AX.X, ALU.add).then_inc(done, 1)

            def head_scale(acc, dst, rs, rs_sem, done, n, free_sem, free_n):
                dve.wait_ge(rs_sem, n)
                if free_n is not None:
                    dve.wait_ge(free_sem, free_n)
                V.tensor_tensor(dst[:, :, :, :].rearrange("p t s d -> p (t s) d"),
                                acc[:, :].rearrange("p (s d) -> p s d", d=DH),
                                rs.unsqueeze(2).broadcast_to([P, 8, DH]), ALU.mult).then_inc(done, 1)

            def diff(i, tail, gtail):
                first = DIFF_N * i + DIFF0
                for j in range(DIFF_N):
                    split_lo(first, j)
                    if tail is not None:
                        diff_tail(j, tail)
                    if gtail is not None:
                        gla_tail(j, gtail)
                    if j == 11:
                        head_sums(q_sq, dq_ss, q_ss, i + 1)
                    if j == 13:
                        head_scale(acc_a, qn, dq_rs, q_rs, q_normed, i + 1, q_T, i if gtail is None else None)
                    if j == 19:
                        head_sums(k_sq, dk_ss, k_ss, i + 1)
                    if j == 21:
                        head_scale(acc_b, kn, dk_rs, k_rs, k_normed, i + 1, k_T, i if gtail is None else None)

            def diff_tail(j, n):
                if j in (5, 8):
                    half = (5, 8).index(j)
                    dve.wait_ge(consts_ready, 1)
                    dve.wait_ge(scores_done[half], n)
                    for s in (2 * half, 2 * half + 1):
                        ps = mix[:, (s % 2) * NB:(s % 2) * NB + 3 * P]
                        for t, (a, b) in enumerate(((0, P), (P, 3 * P))):
                            k = 2 * s + t
                            last = V.tensor_tensor_reduce(prob[:, s, a:b], ps[:, a:b], causal[:, T - (b - a):T], 1.0, -3.0e38,
                                                          ALU.add, ALU.max, s_max[:, k:k + 1])
                    last.then_inc(max_found[half], 1)
                    dve.wait_ge(max_found[half], n)
                    V.tensor_scalar(s_nmax[:, 4 * half:4 * half + 4], s_max[:, 4 * half:4 * half + 4], -DH ** -0.5, None,
                                    ALU.mult).then_inc(max_ready[half], 1)
                if j == 11:
                    dve.wait_ge(exp_ready[0], n)
                    dve.wait_ge(exp_ready[1], n)
                    V.reciprocal(p_inv, p_sum).then_inc(sums_inv, 1)
                    dve.wait_ge(sums_inv, n)
                    V.tensor_scalar(p_lam.rearrange("p (h t) -> p h t", h=2),
                                    p_inv.rearrange("p (h s t) -> p h s t", h=2, s=2)[:, :, 1], neg_lam, None,
                                    ALU.mult).then_inc(sums_lam, 1)
                    dve.wait_ge(sums_lam, n)
                    spans = [(hh, t, a, b) for hh in range(2) for t, (a, b) in enumerate(((0, P), (P, 3 * P)))]
                    for hh, t, a, b in spans:
                        last = V.tensor_scalar(prob[:, 2 * hh + 1, a:b], prob[:, 2 * hh + 1, a:b],
                                               p_lam[:, 2 * hh + t:2 * hh + t + 1], None, ALU.mult)
                    last.then_inc(att_second, 1)
                    dve.wait_ge(att_second, n)
                    for hh, t, a, b in spans:
                        k = 4 * hh + t
                        last = V.scalar_tensor_tensor(out=att[:, hh, a:b], in0=prob[:, 2 * hh, a:b], scalar=p_inv[:, k:k + 1],
                                                      in1=prob[:, 2 * hh + 1, a:b], op0=ALU.mult, op1=ALU.add)
                    last.then_inc(att_ready, 1)
                if j == 17:
                    dve.wait_ge(do_rs, n)
                    for hh in range(2):
                        last = V.tensor_tensor(d_on[:, :, hh * T:(hh + 1) * T],
                                               mix[:, hh * NB:(hh + 1) * NB].rearrange("p (t e) -> p t e", t=TT),
                                               o_rs[:, 2 * hh:2 * hh + 2].unsqueeze(2).broadcast_to([P, TT, T]), ALU.mult)
                    last.then_inc(do_normed, 1)
                if j == 22:
                    dve.wait_ge(diffT_hi_ready, n)
                    for f in range(4):
                        last = V.scalar_tensor_tensor(
                            out=diffT_lo[:, bass.ds(4 * n - 4 + f, 1), :].rearrange("p a t -> p (a t)"),
                            in0=mix[:, f * T:(f + 1) * T], scalar=cols[:, V_SUB + f % 2:V_SUB + f % 2 + 1],
                            in1=diffT_hi[:, bass.ds(4 * n - 4 + f, 1), :].rearrange("p a t -> p (a t)").bitcast(F32),
                            op0=ALU.mult, op1=ALU.subtract)
                    last.then_inc(diffT_lo_ready, 1)

            def branch(g, tail, dtail):
                first = BR_N * g + BR0
                for j in range(BR_N):
                    split_lo(first, j)
                    if dtail is not None:
                        diff_tail(j, dtail)
                    if tail is not None:
                        branch_tail(j, tail)
                    if j == 27:
                        dve.wait_ge(pieces_used, first + 3 * BLOCK)
                        dve.wait_ge(gates_ready, g + 1)
                        V.tensor_tensor(gate_g[:, :, :], acc_c[:, :].rearrange("p (f t) -> p f t", t=T), gate_g[:, :, :],
                                        ALU.mult).then_inc(yg_gated, 1)

            def branch_tail(j, n):
                if j == 3:
                    dve.wait_ge(pieces_used, BR_N * n + BR0)
                    V.tensor_tensor(gate_d[:, :, :], mix[:, :].rearrange("p (f t) -> p f t", t=T), gate_d[:, :, :],
                                    ALU.mult).then_inc(yd_gated, 1)
                    dve.wait_ge(yg_gated, n)
                    dve.wait_ge(yd_gated, n)
                    V.tensor_tensor(gate_g[:, :, :], gate_g[:, :, :], gate_d[:, :, :], ALU.add).then_inc(mixed_ready, 1)
                if j == 4:
                    dve.wait_ge(mixT_hi_ready, n)
                    V.tensor_tensor(mixT_lo[:, bass.ds(4 * n - 4, 4), :], gate_g[:, :, :],
                                    mixT_hi[:, bass.ds(4 * n - 4, 4), :].bitcast(F32), ALU.subtract).then_inc(mixT_lo_ready, 1)

            def add_x(b):
                dve.wait_ge(pieces_used, OUT0 + (b + 1) * BLOCK)
                dve.wait_ge(resid_landed, 16)
                dst = resid[:, :, b * NB:(b + 1) * NB]
                V.tensor_tensor(dst, (acc_a, acc_b)[b % 2][:, :].rearrange("p (t n) -> p t n", t=TT), dst,
                                ALU.add).then_inc(x1_ready, 1)

            def ffn_conv(j, f):
                if j == 11:
                    dve.wait_ge(conv_first, f + 1)
                    for k in range(4):
                        last = V.scalar_tensor_tensor(out=conv[:, k, 1:T], in0=acc_a[:, k * T:(k + 1) * T - 1],
                                                      scalar=cols[:, bass.ds(f * 4 + (V_CW1 + k), 1)], in1=conv[:, k, 1:T],
                                                      op0=ALU.mult, op1=ALU.add)
                    last.then_inc(conv_second, 1)
                if j == 12:
                    dve.wait_ge(conv_second, f + 1)
                    for k in range(4):
                        last = V.scalar_tensor_tensor(out=conv[:, k, 2:T], in0=acc_a[:, k * T:(k + 1) * T - 2],
                                                      scalar=cols[:, bass.ds(f * 4 + (V_CW0 + k), 1)], in1=conv[:, k, 2:T],
                                                      op0=ALU.mult, op1=ALU.add)
                    last.then_inc(conv_ready, 1)

            def hidden(n, done, hi, lo):
                dve.wait_ge(conv_silu, n)
                dve.wait_ge(pieces_used, done)
                V.tensor_tensor(conv[:, :, :], acc_b[:, :].rearrange("p (f t) -> p f t", t=T), conv[:, :, :],
                                ALU.mult).then_inc(hid_ready, 1)
                dve.wait_ge(hid_hi_ready, n)
                V.tensor_tensor(lo[:, :, :], conv[:, :, :], hi[:, :, :].bitcast(F32), ALU.subtract)\
                 .then_inc(hid_lo_ready, 1)

            def add_down(first, q, n):
                dve.wait_ge(pieces_used, first + 2 * (q + 1))
                dst = resid[:, :, q * NB:(q + 1) * NB]
                V.tensor_tensor(dst, (acc_c, mix)[q % 2][:, :].rearrange("p (t n) -> p t n", t=TT), dst,
                                ALU.add).then_inc(down_added, 1)

            dve.wait_ge(x_landed[1], 16)
            V.tensor_tensor_reduce(normed[:, 1], resid[:, 1], resid[:, 1], 1.0, 0.0, ALU.mult, ALU.add,
                                   ss_x[:, 1:2]).then_inc(sumsq_dve, 1)
            dve.wait_ge(cols_T, 1)
            V.tensor_copy(cols[:, 0:90], mix[:, 0:90])
            V.tensor_copy(cols[:, 90:222], mix[:, 90:222]).then_inc(scale_ready, 1)
            dve.wait_ge(scale_ready, 1)
            V.tensor_scalar(cols[:, V_SUB:V_SUB + 2], cols[:, V_SUB:V_SUB + 2], 1.0 - LAMBDA_INIT, None,
                            ALU.mult).then_inc(cols_ready, 1)
            norm_rows(resid, normed, 1)

            gla(0, None)
            with dve.Fori(1, GLA_HEADS) as h:
                gla(h, h)
            diff(0, None, GLA_HEADS)
            with dve.Fori(1, DIFF_PAIRS) as i:
                diff(i, i, None)
            branch(0, None, DIFF_PAIRS)
            with dve.Fori(1, GROUPS) as g:
                branch(g, g, None)
            for j in range(4 * BLOCK):
                split_lo(OUT0, j)
                branch_tail(j, GROUPS)
                if j % 8 == 3 and j > 3:
                    add_x(j // 8 - 1)
            for j in range(2 * BLOCK):
                if 4 <= j < BLOCK:
                    norm_pair(j, V_N2, 2)
                split_lo(FFN0, j)
                if j == 3:
                    add_x(3)
                    dve.wait_ge(x1_sumsq, 4)
                    V.tensor_reduce(ss_x, ss_out.rearrange("p (t b) -> p t b", t=TT), AX.X, ALU.add).then_inc(sumsq_dve, 1)
                    norm_rows(resid, xn2, 2)
                    for pair in range(4):
                        norm_pair(pair, V_N2, 2)
                ffn_conv(j, 0)
            with dve.Fori(1, LAST) as f:
                for j in range(FFN_N):
                    split_lo(ffn_base(f), j)
                    if j == 3:
                        hidden(f, ffn_base(f), hid_hi, hid_lo)
                    ffn_conv(j, f)
                    if j in (13, 15, 17, 19):
                        add_down(ffn_base(f) + BLOCK, (j - 13) // 2, f)
            for j in range(FFN_N):
                split_lo(ffn_base(LAST), j)
                if j == 3:
                    hidden(LAST, ffn_base(LAST), hid_hi, hid_lo)
                ffn_conv(j, LAST)
                if j == 19:
                    hidden(FFN_GROUPS, ffn_base(LAST) + 2 * BLOCK, last_hi, last_lo)
                if j in (21, 23):
                    add_down(ffn_base(LAST) + 2 * BLOCK, (j - 21) // 2, LAST)
            for j in range(BLOCK):
                split_lo(END0, j)
                if j in (1, 3):
                    add_down(ffn_base(LAST) + 2 * BLOCK, (j + 3) // 2, LAST)
                if j in (5, 7):
                    add_down(END0, (j - 5) // 2, FFN_GROUPS)
            add_down(END0, 2, FFN_GROUPS)
            add_down(END0, 3, FFN_GROUPS)

        @block.gpsimd
        def _(pool):
            G = nc.gpsimd
            G.memset(ident[:, :], 0.0)
            G.memset(keep[:, :], 1.0)
            G.memset(causal[:, :], 0.0)
            G.memset(AT[:, :, :], 0.0)
            G.memset(reset[:, :], 1.0)
            G.memset(cols[:, :], 0.0)
            G.memset(eps_c, EPS)
            G.memset(sub_eps_c, SUBLN_EPS)
            G.memset(one_c, 1.0)
            for k in range(ROPE // 2):
                f = float(np.float32(ROPE_THETA) ** (-np.float32(2 * k) / np.float32(ROPE)))
                last = G.memset(inv_f[:, k:k + 1], f)
            last.then_inc(const_step, 1)
            pool.wait_ge(const_step, 1)
            G.affine_select(out=ident[:, :], in_=ident[:, :], compare_op=ALU.not_equal, fill=1.0, base=0,
                            pattern=[[-1, P]], channel_multiplier=1)
            G.affine_select(out=keep[:, :], in_=keep[:, :], compare_op=ALU.is_ge, fill=0.0, base=0,
                            pattern=[[1, P]], channel_multiplier=-1)
            G.affine_select(out=causal[:, P:T], in_=causal[:, P:T], compare_op=ALU.is_ge, fill=-1.0e30, base=0,
                            pattern=[[-1, P]], channel_multiplier=1)
            G.memset(reset[:, :].rearrange("p (c t) -> p c t", t=C)[:, :, 0:1], 0.0).then_inc(consts_ready, 1)

            def gla_tail(n):
                pool.wait_ge(go_normed, n)
                pool.wait_ge(gout_silu, n)
                if not (isinstance(n, int) and n == 1):
                    pool.wait_ge(og_T, n - 1)
                G.tensor_tensor(g_og[:, :, :], g_on[:, :, :], g_silu[:, :, :], ALU.mult).then_inc(og_ready, 1)

            def turn(buf, which, normed_sem, scaled, turned, roped, n):
                v = buf[:, :, :, :].rearrange("p t s d -> p (t s) d")
                pool.wait_ge(normed_sem, n)
                G.tensor_tensor(v, v, qk_g[:, which].unsqueeze(1).broadcast_to([P, 8, DH]), ALU.mult).then_inc(scaled, 1)
                pool.wait_ge(scaled, n)
                H = ROPE // 2
                sin = rope_t[:, 4].unsqueeze(2).broadcast_to([P, TT, 4, H])
                cos = rope_t[:, 5].unsqueeze(2).broadcast_to([P, TT, 4, H])
                x1, x2 = buf[:, :, :, 0:H], buf[:, :, :, H:2 * H]
                r = [rot[:, k].rearrange("p (t s) h -> p t s h", t=TT) for k in range(4)]
                G.tensor_tensor(r[0], x1, cos, ALU.mult)
                G.tensor_tensor(r[1], x2, sin, ALU.mult)
                G.tensor_tensor(r[2], x2, cos, ALU.mult)
                G.tensor_tensor(r[3], x1, sin, ALU.mult).then_inc(turned, 1)
                pool.wait_ge(turned, n)
                G.tensor_tensor(x1, r[0], r[1], ALU.subtract)
                G.tensor_tensor(x2, r[2], r[3], ALU.add).then_inc(roped, 1)

            def diff(n):
                turn(qn, 0, q_normed, q_scaled, q_turned, q_roped, n)
                pool.wait_ge(q_roped, n)
                turn(kn, 1, k_normed, k_scaled, k_turned, k_roped, n)
                pool.wait_ge(k_roped, n)

            gla_tail(1)
            with pool.Fori(2, GLA_HEADS + 1) as n:
                gla_tail(n)
            pool.wait_ge(small_landed, 17 * 16)
            pool.wait_ge(rope_ready, 2)
            with pool.Fori(1, DIFF_PAIRS + 1) as n:
                diff(n)

        @block.tensor
        def _(pe):
            mm = nc.tensor.matmul

            def features(first, j, b, acc, a_hi, a_lo):
                slot, k0 = j % 4, 2 * (j - b * BLOCK)
                pe.wait_ge(lo_ready, first + j + 1)
                for k in range(PIECE_KT):
                    for f in range(4):
                        dst = acc[:, f * T:(f + 1) * T]
                        hi, lo = (w[:, slot, k, f * P:(f + 1) * P] for w in (whi, wlo))
                        kt = k0 + k
                        mm(dst, hi, a_hi[:, kt], start=(kt == 0 and f % 2 == 0), stop=False, skip_group_check=True)
                        mm(dst, hi, a_lo[:, kt], start=False, stop=False, skip_group_check=True)
                        last = mm(dst, lo, a_hi[:, kt], start=False, stop=(kt == KT - 1), skip_group_check=True)
                last.then_inc(pieces_used, 1)

            def tokens(first, j, k0, n_kt, acc, a_hi, a_lo):
                slot = j % 4
                pe.wait_ge(lo_ready, first + j + 1)
                for k in range(PIECE_KT):
                    kt = k0 + k
                    for t in range(TT):
                        dst = acc[:, t * NB:(t + 1) * NB]
                        hi, lo = a_hi[:, kt, t * P:(t + 1) * P], a_lo[:, kt, t * P:(t + 1) * P]
                        mm(dst, hi, whi[:, slot, k], start=(kt == 0), stop=False)
                        mm(dst, hi, wlo[:, slot, k], start=False, stop=False)
                        last = mm(dst, lo, whi[:, slot, k], start=False, stop=(kt == n_kt - 1))
                last.then_inc(pieces_used, 1)

            def transpose(dst, src, n=P):
                return nc.tensor.transpose(dst, src, ident[0:n, 0:n])

            def norm_transposes(src, pair, n):
                pe.wait_ge(normed_act, 4 * (n - 1) + pair // 2 + 1)
                pe.wait_ge(normed_dve, 4 * (n - 1) + pair // 2 + 1)
                if pair >= 6:
                    pe.wait_ge(norm_lo, 8 * (n - 1) + pair - 5)
                for k in range(2):
                    for t in range(TT):
                        col = (2 * pair + k) * P
                        last = transpose(stage(pair)[:, k * T + t * P:k * T + (t + 1) * P], src[:, t, col:col + P])
                last.then_inc(norm_T, 1)

            def normed_block(src, j, n):
                if j == 0:
                    for pair in range(6):
                        norm_transposes(src, pair, n)
                if j in (1, 2):
                    norm_transposes(src, j + 5, n)
                if j < BLOCK:
                    pe.wait_ge(norm_lo, 8 * (n - 1) + j + 1)

            def decay_inputs(j):
                if j == 8:
                    pe.wait_ge(wlr_lo_ready, 1)
                    for k in range(KT):
                        mm(mix[:, 0:T], wlr_hi[:, k], hT_hi[:, k], start=(k == 0), stop=False)
                        mm(mix[:, 0:T], wlr_hi[:, k], hT_lo[:, k], start=False, stop=False)
                        last = mm(mix[:, 0:T], wlr_lo[:, k], hT_hi[:, k], start=False, stop=(k == KT - 1))
                    last.then_inc(lr_done, 1)
                if j == 10:
                    pe.wait_ge(lr_ready, 1)
                    for k in range(8):
                        last = mm((acc_c, mix)[k // 4][:, (k % 4) * T:(k % 4 + 1) * T], wup[0:GLA_RANK, k * P:(k + 1) * P],
                                  lrT[0:GLA_RANK, :], start=True, stop=True)
                        if k % 4 == 3:
                            last.then_inc(gk_done, 1)

            def gla(h, tail):
                first = GLA_N * h + GLA0
                first_head = tail is None
                at_A, at_o = (17, 20) if first_head else (13, 18)
                for j in range(GLA_N):
                    if tail is not None:
                        gla_tail(j, tail)
                    if first_head:
                        normed_block(normed, j, 1)
                        decay_inputs(j)
                        if j == 2 * BLOCK:
                            pe.wait_ge(gkx_ready, 1)
                    if j == at_A:
                        pe.wait_ge(operands_ready, h + 1)
                        if not first_head:
                            pe.wait_ge(glaT_lo_ready, h)
                        for dst, key, query in (
                                (0, k_inv[:, :, 0:P], q_dec[:, :, 0:C]), (C, k_mix[:, :, 0:P], q_dec[:, :, C:2 * C]),
                                (2 * C, k_inv[:, :, P:T], q_dec[:, :, 2 * C:3 * C]),
                                (3 * C, k_mix[:, :, P:T], q_dec[:, :, 3 * C:4 * C]),
                                (4 * C, k_tile[:, :, :], q_dec[:, :, 2 * C:3 * C]), (5 * C, k_tile[:, :, :], q_3[:, :, :])):
                            for f in range(2):
                                last = mm(mix[:, dst:dst + C], key[:, f], query[:, f], start=(f == 0), stop=(f == 1))
                        last.then_inc(A_done, 1)
                    if j == at_o:
                        pe.wait_ge(AT_ready, h + 1)
                        pe.wait_ge(gv_ready, h + 1)
                        mm(mix[:, NB:2 * NB], AT[:, 0], g_v[:, 0], start=True, stop=True)
                        mm(mix[:, 0:NB], AT[:, 1], g_v[:, 1], start=True, stop=False)
                        mm(mix[:, 0:NB], AT[:, 2], g_v[:, 0], start=False, stop=True).then_inc(go_done, 1)
                    if j < BLOCK:
                        if j == 0 and not first_head:
                            pe.wait_ge(operands_ready, h)
                        features(first, j, 0, acc_a, hT_hi, hT_lo)
                    elif j < 2 * BLOCK:
                        if j == BLOCK and not first_head:
                            pe.wait_ge(gv_ready, h)
                        tokens(first, j, 2 * (j - BLOCK), KT, acc_b, hT_hi, hT_lo)
                    else:
                        if j == 2 * BLOCK and not first_head:
                            pe.wait_ge(gout_silu, h)
                        tokens(first, j, 2 * (j - 2 * BLOCK), KT, acc_c, hT_hi, hT_lo)

            def gla_tail(j, n):
                if j == 9:
                    pe.wait_ge(og_ready, n)
                    for f in range(4):
                        for t in range(TT):
                            last = transpose(mix[:, f * T + t * P:f * T + (t + 1) * P], g_og[:, t, f * P:(f + 1) * P])
                    last.then_inc(og_T, 1)

            def head_transposes(src):
                for s in range(4):
                    for t in range(TT):
                        last = transpose(mix[:, s * T + t * P:s * T + (t + 1) * P], src[:, t, s])
                return last

            def diff(i, tail, gtail):
                first = DIFF_N * i + DIFF0
                for j in range(DIFF_N):
                    if tail is not None:
                        diff_tail(j, tail, True, i)
                    if gtail is not None:
                        gla_tail(j, gtail)
                    if j == 17:
                        pe.wait_ge(q_roped, i + 1)
                        if tail is not None:
                            pe.wait_ge(do_normed, i)
                        else:
                            pe.wait_ge(glaT_lo_ready, GLA_HEADS)
                        head_transposes(qn).then_inc(q_T, 1)
                    if j == 22:
                        pe.wait_ge(k_roped, i + 1)
                        pe.wait_ge(qT_ready, i + 1)
                        if tail is not None:
                            pe.wait_ge(diffT_lo_ready, i)
                        head_transposes(kn).then_inc(k_T, 1)
                    b = j // BLOCK
                    if j == 0:
                        pe.wait_ge(operands_ready if gtail is not None else q_normed, GLA_HEADS if gtail is not None else i)
                    if j == BLOCK:
                        pe.wait_ge(gv_ready if gtail is not None else k_normed, GLA_HEADS if gtail is not None else i)
                    if j == 2 * BLOCK:
                        pe.wait_ge(gout_silu if gtail is not None else dv_ready, GLA_HEADS if gtail is not None else i)
                    tokens(first, j, 2 * (j - b * BLOCK), KT, (acc_a, acc_b, acc_c)[b], hT_hi, hT_lo)

            def diff_tail(j, n, more, i):
                if j in (2, 5):
                    half = (2, 5).index(j)
                    if half == 0:
                        pe.wait_ge(qT_ready, n)
                        pe.wait_ge(kT_ready, n)
                    else:
                        pe.wait_ge(max_found[0], n)
                    for s in (2 * half, 2 * half + 1):
                        ps = mix[:, (s % 2) * NB:(s % 2) * NB + 3 * P]
                        mm(ps[:, 0:P], qT[:, s, 0:P], kT[:, s, 0:P], start=True, stop=True)
                        last = mm(ps[:, P:3 * P], qT[:, s, P:T], kT[:, s, :], start=True, stop=True)
                    last.then_inc(scores_done[half], 1)
                if j == 11:
                    pe.wait_ge(att_ready, n)
                    for hh in range(2):
                        for k in range(3):
                            last = transpose(mix[:, hh * NB + k * P:hh * NB + (k + 1) * P], att[:, hh, k * P:(k + 1) * P])
                    last.then_inc(att_T, 1)
                if j == 13:
                    pe.wait_ge(attT_ready, n)
                    pe.wait_ge(dv_ready, n)
                    for hh in range(2):
                        v = d_v[:, :, hh * T:(hh + 1) * T]
                        mm(mix[:, hh * NB:hh * NB + T], attT[:, hh, 0:P], v[:, 0], start=True, stop=True)
                        mm(mix[:, hh * NB + T:hh * NB + 2 * T], attT[:, hh, P:2 * P], v[:, 0], start=True, stop=False)
                        last = mm(mix[:, hh * NB + T:hh * NB + 2 * T], attT[:, hh, 2 * P:3 * P], v[:, 1],
                                  start=False, stop=True)
                    last.then_inc(pv_done, 1)
                if j == 19:
                    pe.wait_ge(do_normed, n)
                    if more:
                        pe.wait_ge(qT_ready, i + 1)
                    for f in range(4):
                        for t in range(TT):
                            last = transpose(mix[:, f * T + t * P:f * T + (t + 1) * P], d_on[:, t, f * P:(f + 1) * P])
                    last.then_inc(do_T, 1)

            def branch(g, tail, dtail):
                first = BR_N * g + BR0
                for j in range(BR_N):
                    if dtail is not None:
                        diff_tail(j, dtail, False, None)
                    b = j // BLOCK
                    if j == 0:
                        pe.wait_ge(q_normed if dtail is not None else gates_ready, DIFF_PAIRS if dtail is not None else g)
                    if j == BLOCK and dtail is not None:
                        pe.wait_ge(k_normed, DIFF_PAIRS)
                    if j == 2 * BLOCK:
                        pe.wait_ge(dv_ready if dtail is not None else yg_gated, DIFF_PAIRS if dtail is not None else g)
                    if j == 3 * BLOCK:
                        if dtail is not None:
                            pe.wait_ge(diffT_lo_ready, DIFF_PAIRS)
                        else:
                            pe.wait_ge(yd_gated, g)
                    a_hi, a_lo = ((hT_hi, hT_lo), (hT_hi, hT_lo), (glaT_hi, glaT_lo), (diffT_hi, diffT_lo))[b]
                    features(first, j, b, (acc_a, acc_b, acc_c, mix)[b], a_hi, a_lo)

            pe.wait_ge(consts_ready, 1)
            pe.wait_ge(small_landed, 17 * 16)
            transpose(mix[:, 0:90], rows[0:90, 0, :], 90)
            transpose(mix[:, 90:178], rows[0:88, 1, :], 88)
            transpose(mix[:, 178:222], rows[0:44, 2, :], 44).then_inc(cols_T, 1)
            pe.wait_ge(cols_ready, 1)

            gla(0, None)
            with pe.Fori(1, GLA_HEADS) as h:
                gla(h, h)
            diff(0, None, GLA_HEADS)
            with pe.Fori(1, DIFF_PAIRS) as i:
                diff(i, i, None)
            branch(0, None, DIFF_PAIRS)
            with pe.Fori(1, GROUPS) as g:
                branch(g, g, None)
            for j in range(4 * BLOCK):
                b = j // BLOCK
                if j == 0:
                    pe.wait_ge(gates_ready, GROUPS)
                    pe.wait_ge(mixT_lo_ready, GROUPS - 1)
                if j == 6:
                    pe.wait_ge(mixT_lo_ready, GROUPS)
                if j in (2 * BLOCK, 3 * BLOCK):
                    pe.wait_ge(x1_ready, b - 1)
                tokens(OUT0, j, 2 * (j - b * BLOCK), KT, (acc_a, acc_b)[b % 2], mixT_hi, mixT_lo)
            for j in range(2 * BLOCK):
                normed_block(xn2, j, 2)
                features(FFN0, j, j // BLOCK, (acc_a, acc_b)[j // BLOCK], hT_hi, hT_lo)

            def down(first, j, q_first, n, a_hi, a_lo):
                q, k0 = (j - q_first) // 2, 2 * (j % 2)
                if j == q_first:
                    pe.wait_ge(hid_lo_ready, n)
                if j % 2 == 0 and (q >= 2 or a_hi is last_hi):
                    pe.wait_ge(down_added, 4 * n - 5 + q)
                tokens(first, j, k0, 4, (acc_c, mix)[q % 2], a_hi, a_lo)

            with pe.Fori(1, LAST) as f:
                for j in range(FFN_N):
                    if j == 0:
                        pe.wait_ge(conv_ready, f)
                    if j < BLOCK:
                        features(ffn_base(f), j, 0, acc_a, hT_hi, hT_lo)
                    elif j < 2 * BLOCK:
                        down(ffn_base(f), j, BLOCK, f, hid_hi, hid_lo)
                    else:
                        features(ffn_base(f), j, 2, acc_b, hT_hi, hT_lo)
            for j in range(FFN_N):
                if j == 0:
                    pe.wait_ge(conv_ready, LAST)
                if j == BLOCK:
                    pe.wait_ge(hid_ready, LAST)
                if j < 2 * BLOCK:
                    features(ffn_base(LAST), j, j // BLOCK, (acc_a, acc_b)[j // BLOCK], hT_hi, hT_lo)
                else:
                    down(ffn_base(LAST), j, 2 * BLOCK, LAST, hid_hi, hid_lo)
            for j in range(BLOCK):
                down(END0, j, 0, FFN_GROUPS, last_hi, last_lo)


_INS = ["x", "positions", "norm1_g", "w_in", "w_gk_up", "b_gk", "gla_norm_g", "q_norm_g", "k_norm_g",
        "lambda_q1", "lambda_k1", "lambda_q2", "lambda_k2", "subln_g", "w_branch", "w_out", "norm2_g",
        "w_ffn_up", "conv_w", "conv_b", "w_ffn_down"]


def kernel(**inputs):
    import numpy as _np
    import concourse.bacc as _bacc
    from concourse import mybir as _mybir
    from concourse.bass_utils import run_bass_kernel_spmd as _run

    nc = _bacc.Bacc("TRN2", target_bir_lowering=False, num_devices=1)
    arrays, args = {}, []
    for name in _INS:
        a = _np.ascontiguousarray(inputs[name])
        arrays[f"in_{name}_dram"] = a
        args.append(nc.dram_tensor(f"in_{name}_dram", a.shape, _mybir.dt.from_np(a.dtype), kind="ExternalInput").ap())
    out = nc.dram_tensor("out_0_dram", (1, T, D), F32, kind="ExternalOutput").ap()
    hybrid_block_kernel(nc, *args, out)
    r = _run(nc, [arrays], core_ids=[0])
    return r.results[0]["out_0_dram"]
```

```python
import math
from contextlib import ExitStack

import numpy as np

import concourse.bass as bass
from concourse import mybir

F32 = mybir.dt.float32
F32R = mybir.dt.float32r
I32 = mybir.dt.int32
U32 = mybir.dt.uint32
ALU = mybir.AluOpType
ACT = mybir.ActivationFunctionType
AX = mybir.AxisListType

P = 128
T = 256
TT = T // P
D = 2048
KT = D // P
NB = 512
CHUNK_KT = 4
PIECE_KT = 2
HB = NB // 2

GLA_HEADS = 4
GLA_DK = 256
GLA_DV = 512
GLA_RANK = 16
GLA_NORMALIZER = 16.0
C = 64
DIFF_PAIRS = 4
DH = 128
ROPE = 32
ROPE_THETA = 500000.0
FFN = 5632
FFN_GROUPS = FFN // NB
GROUPS = D // NB
EPS = 1e-6
SUBLN_EPS = 1e-5
LAMBDA_INIT = 0.8 - 0.6 * math.exp(-0.3 * 0)

C_GV = 2 * GLA_HEADS * GLA_DK
C_LR = C_GV + GLA_HEADS * GLA_DV
C_GOUT = C_LR + GLA_RANK
C_DQ = C_GOUT + D
C_DK = C_DQ + D
C_DV = C_DK + D
C_MG = C_DV + D
C_MD = C_MG + D

BLOCK = 8
HALF = BLOCK // 2
GLA0, GLA_N = 0, 3 * BLOCK
DIFF0, DIFF_N = GLA0 + GLA_HEADS * GLA_N, 3 * BLOCK
BR0, BR_N = DIFF0 + DIFF_PAIRS * DIFF_N, 4 * BLOCK
OUT0 = BR0 + GROUPS * BR_N
FFN0 = OUT0 + 4 * BLOCK
FFN_N = 3 * BLOCK
LAST = FFN_GROUPS - 1
END0 = FFN0 + FFN_GROUPS * FFN_N - BLOCK


BR_HALVES = 8
FFN_HALF0 = GROUPS * BR_HALVES


def ffn_base(f):
    return f * FFN_N + (FFN0 - BLOCK)


def two_pi_pieces(n):
    left, out = 2.0 * math.pi, []
    for _ in range(n - 1):
        step = 2.0 ** (math.floor(math.log2(left)) - 6)
        out.append(math.floor(left / step) * step)
        left -= out[-1]
    return out + [float(np.float32(left))]


TWO_PI = two_pi_pieces(5)
ROUND = 1.5 * 2.0 ** 23


def hybrid_block_kernel(nc, x, positions, norm1_g, w_in, w_gk_up, b_gk, gla_norm_g, q_norm_g, k_norm_g,
                        lambda_q1, lambda_k1, lambda_q2, lambda_k2, subln_g, w_branch, w_out,
                        norm2_g, w_ffn_up, conv_w, conv_b, w_ffn_down, out):
    with ExitStack() as ctx:
        KB = 1024
        base = -(-nc.sbuf_base // 64) * 64

        def at(name, offset, shape, dt=F32):
            return nc.alloc_sbuf_tensor_at(name, [P] + shape, dt, offset=base + int(offset))

        def sem(name):
            return ctx.enter_context(nc.semaphore(name))

        raw = at("raw", 0, [4, CHUNK_KT, NB])
        whi = at("whi", 32 * KB, [4, PIECE_KT, NB], F32R)
        wlo = at("wlo", 48 * KB, [4, PIECE_KT, NB], F32R)
        hT = at("hT", 64 * KB, [KT, 2, T], F32R)
        glaT = at("glaT", 96 * KB, [KT, 2, T], F32R)
        resid = at("resid", 96 * KB, [TT, D])
        normed = at("normed", 112 * KB, [TT, D])
        diffT = at("diffT", 128 * KB, [KT, 2, T], F32R)
        mixT_hi = at("mixT_hi", 160 * KB, [KT, T], F32R)
        mixT_lo = at("mixT_lo", 176 * KB, [KT, T], F32R)
        wlr_raw = at("wlr_raw", 128 * KB, [KT, P])
        wlr_hi = at("wlr_hi", 136 * KB, [KT, P], F32R)
        wlr_lo = at("wlr_lo", 96 * KB, [KT, P], F32R)
        gkx = at("gkx", 152 * KB, [8, T])
        g_exp = at("g_exp", 128 * KB, [TT * NB])
        g_silu = at("g_silu", 132 * KB, [TT, NB])
        g_on = at("g_on", 136 * KB, [TT, NB])
        g_og = at("g_og", 140 * KB, [TT, NB])
        g_v = at("g_v", 144 * KB, [TT, NB])
        q_sum = at("q_sum", 148 * KB, [2, T])
        k_sum = at("k_sum", 150 * KB, [2, T])
        o = 160 * KB
        dec = at("dec", o, [2, T])
        gmin = at("gmin", o + 2 * KB, [2, T])
        cum = at("cum", o + 4 * KB, [2, T])
        e_pos = at("e_pos", o + 6 * KB, [2, T])
        e_neg = at("e_neg", o + 8 * KB, [2, T])
        e_tail = at("e_tail", o + 10 * KB, [2, 2, C])
        e_tile = at("e_tile", o + 11 * KB, [2, P])
        e_q3 = at("e_q3", o + 12 * KB, [2, C])
        q_dec = at("q_dec", o + 12.5 * KB, [2, T])
        k_inv = at("k_inv", o + 14.5 * KB, [2, T])
        k_mix = at("k_mix", o + 16.5 * KB, [2, T])
        k_tile = at("k_tile", o + 18.5 * KB, [2, P])
        q_3 = at("q_3", o + 19.5 * KB, [2, C])
        AT = at("AT", o + 20 * KB, [3, P])
        reset = at("reset", o + 21.5 * KB, [T])
        rows = at("rows", o + 22.5 * KB, [3, P])
        wup = at("wup", o + 24 * KB, [GLA_HEADS * GLA_DK])
        lam_v = at("lam_v", o + 28 * KB, [4, P])
        qk_g = at("qk_g", o + 30 * KB, [2, P])
        lam_p = at("lam_p", o + 31 * KB, [2, P])
        sq = at("sq", o, [8, DH])
        rot = at("rot", o + 4 * KB, [4, 8, ROPE // 2])
        qT = at("qT", o + 6 * KB, [4, T])
        kT = at("kT", o + 10 * KB, [4, T])
        d_v = at("d_v", o + 14 * KB, [TT, NB])
        prob = at("prob", o + 18 * KB, [4, 3 * P])
        att = at("att", o + 24 * KB, [2, 3 * P])
        attT = at("attT", o + 27 * KB, [2, 3 * P])
        o = 192 * KB
        lrT = at("lrT", o, [T])
        qn = at("qn", o, [TT, 4, DH])
        kn = at("kn", o + 4 * KB, [TT, 4, DH])
        gate_g = at("gate_g", o, [4, T])
        gate_d = at("gate_d", o + 4 * KB, [4, T])
        d_on = at("d_on", o + 8 * KB, [TT, NB])
        y_sum = at("y_sum", o + 8 * KB, [2, 2, T])
        o += 12 * KB
        ident = at("ident", o, [P])
        keep = at("keep", o + 512, [P])
        causal = at("causal", o + 1024, [T])
        cols = at("cols", o + 2048, [224])
        rope_t = at("rope_t", o + 2048 + 896, [6, TT, ROPE // 2])
        small = at("small", o + 2048 + 896 + 768, [44])
        assert base + o + 2048 + 896 + 768 + 176 <= nc.sbuf_usable_end
        xn2 = at("xn2", 128 * KB, [TT, D])
        up_sum = at("up_sum", 112 * KB, [4, T])
        conv = at("conv", 144 * KB, [4, T])
        hid_hi = at("hid_hi", 148 * KB, [4, T], F32R)
        hid_lo = at("hid_lo", 152 * KB, [4, T], F32R)
        last_hi = at("last_hi", 156 * KB, [4, T], F32R)
        last_lo = at("last_lo", 128 * KB, [4, T], F32R)

        V_N1, V_N2, V_BGK, V_GLA, V_SUB, V_CW0 = 0, 16, 32, 40, 44, 46
        V_CW1, V_CW2, V_CB = 90, 134, 178
        ss_x, rs_x = small[:, 0:2], small[:, 2:4]
        eps_c, sub_eps_c = small[:, 4:5], small[:, 5:6]
        one_c, zero_c = small[:, 6:7], small[:, 7:8]
        neg_lam = small[:, 8:9]
        lam2 = small[:, 9:11]
        pos_i = small[:, 11:13]
        inv_f = small[:, 13:29]
        ss_out = small[:, 29:37]
        tiny = at("tiny", 31.5 * KB + 160 * KB, [96])
        bl = tiny[:, 0:8]
        bl01 = tiny[:, 8:10]
        g_ss, g_rs = tiny[:, 10:12], tiny[:, 12:14]
        dq_ss, dq_rs = tiny[:, 14:22], tiny[:, 22:30]
        dk_ss, dk_rs = tiny[:, 30:38], tiny[:, 38:46]
        s_max, s_nmax = tiny[:, 46:54], tiny[:, 54:62]
        p_sum, p_inv = tiny[:, 62:70], tiny[:, 70:78]
        p_lam = tiny[:, 78:82]
        o_ss, o_rs = tiny[:, 82:86], tiny[:, 86:90]

        acc_a, acc_b, acc_c, mix = (ctx.enter_context(nc.psum_tensor(n, [P, 2 * NB], F32))
                                    for n in ("acc_a", "acc_b", "acc_c", "mix"))

        def stage(pair):
            b = pair % 6
            return (acc_b, acc_c, mix)[b // 2][:, (b % 2) * NB:(b % 2 + 1) * NB]

        raw_landed = [sem(f"raw_landed{i}") for i in range(4)]
        hi_ready = sem("hi_ready")
        lo_ready = sem("lo_ready")
        pieces_used = sem("pieces_used")
        x_landed = [sem("x_landed0"), sem("x_landed1")]
        wlr_landed, small_landed = sem("wlr_landed"), sem("small_landed")
        resid_landed = sem("resid_landed")
        out_stored = sem("out_stored")
        consts_ready, const_step = sem("consts_ready"), sem("const_step")
        cols_T, cols_ready = sem("cols_T"), sem("cols_ready")
        scale_ready = sem("scale_ready")
        wlr_hi_ready, wlr_lo_ready = sem("wlr_hi_ready"), sem("wlr_lo_ready")
        sumsq_act, sumsq_dve = sem("sumsq_act"), sem("sumsq_dve")
        norm_ln, norm_rs = sem("norm_ln"), sem("norm_rs")
        normed_act, normed_dve = sem("normed_act"), sem("normed_dve")
        norm_T, norm_hi, norm_lo = sem("norm_T"), sem("norm_hi"), sem("norm_lo")
        lr_done, lr_ready, gk_done, gkx_ready = sem("lr_done"), sem("lr_ready"), sem("gk_done"), sem("gkx_ready")
        rope_step, rope_arg, rope_sin, rope_ready = sem("rope_step"), sem("rope_arg"), sem("rope_sin"), sem("rope_ready")
        lam_dot, lam_exp, lam_ready = sem("lam_dot"), sem("lam_exp"), sem("lam_ready")
        gk_abs, gk_exp, gk_ln = sem("gk_abs"), sem("gk_exp"), sem("gk_ln")
        gk_min, gk_gate, cum_ready, bl_ready = sem("gk_min"), sem("gk_gate"), sem("cum_ready"), sem("bl_ready")
        bl_scaled = sem("bl_scaled")
        e_ready, operands_ready, A_done = sem("e_ready"), sem("operands_ready"), sem("A_done")
        AT_ready, gv_ready, go_done = sem("AT_ready"), sem("gv_ready"), sem("go_done")
        go_sumsq, go_ln, go_rs, go_normed = sem("go_sumsq"), sem("go_ln"), sem("go_rs"), sem("go_normed")
        gout_exp, gout_one, gout_inv, gout_silu = sem("gout_exp"), sem("gout_one"), sem("gout_inv"), sem("gout_silu")
        og_ready, og_T, glaT_hi_ready, glaT_lo_ready = sem("og_ready"), sem("og_T"), sem("glaT_hi_ready"), sem("glaT_lo_ready")
        q_sq, q_ss, q_ln, q_rs, q_normed = (sem("q_" + n) for n in ("sq", "ss", "ln", "rs", "normed"))
        k_sq, k_ss, k_ln, k_rs, k_normed = (sem("k_" + n) for n in ("sq", "ss", "ln", "rs", "normed"))
        q_scaled, q_turned, q_roped = sem("q_scaled"), sem("q_turned"), sem("q_roped")
        k_scaled, k_turned, k_roped = sem("k_scaled"), sem("k_turned"), sem("k_roped")
        q_T, k_T, qT_ready, kT_ready, dv_ready = sem("q_T"), sem("k_T"), sem("qT_ready"), sem("kT_ready"), sem("dv_ready")
        scores_done = [sem("scores01_done"), sem("scores23_done")]
        max_found = [sem("max01_found"), sem("max23_found")]
        max_ready = [sem("max01_ready"), sem("max23_ready")]
        exp_ready = [sem("exp01_ready"), sem("exp23_ready")]
        sums_inv, sums_lam, att_second, att_ready = sem("sums_inv"), sem("sums_lam"), sem("att_second"), sem("att_ready")
        att_T, attT_ready, pv_done = sem("att_T"), sem("attT_ready"), sem("pv_done")
        do_sumsq, do_ln, do_rs, do_normed = sem("do_sumsq"), sem("do_ln"), sem("do_rs"), sem("do_normed")
        do_T, diffT_hi_ready, diffT_lo_ready = sem("do_T"), sem("diffT_hi_ready"), sem("diffT_lo_ready")
        q_summed, k_summed = sem("q_summed"), sem("k_summed")
        halves_summed = sem("halves_summed")
        gates_ready, y_gated, mixed_ready = sem("gates_ready"), sem("y_gated"), sem("mixed_ready")
        mixT_hi_ready, mixT_lo_ready = sem("mixT_hi_ready"), sem("mixT_lo_ready")
        x1_ready, x1_sumsq = sem("x1_ready"), sem("x1_sumsq")
        conv_first, conv_second, conv_ready, conv_silu = sem("conv_first"), sem("conv_second"), sem("conv_ready"), sem("conv_silu")
        hid_ready, hid_hi_ready, hid_lo_ready, down_added = sem("hid_ready"), sem("hid_hi_ready"), sem("hid_lo_ready"), sem("down_added")

        x_v = x[0].rearrange("(t p) n -> p t n", p=P)
        out_v = out[0].rearrange("(t p) n -> p t n", p=P)
        w_in_v = w_in[0].rearrange("(k p) n -> p k n", p=P)
        w_br_v = w_branch[0].rearrange("(k p) n -> p k n", p=P)
        w_out_v = w_out[0].rearrange("(k p) n -> p k n", p=P)
        w_up_v = w_ffn_up[0].rearrange("(k p) n -> p k n", p=P)
        w_down_v = w_ffn_down[0].rearrange("(g k p) n -> p g k n", k=4, p=P)

        block = ctx.enter_context(nc.Block())

        @block.sync
        def _(sp):
            def load(first, j, src, half=False):
                slot = j % 4
                if isinstance(first, int):
                    if first // 2 + j >= 4:
                        sp.wait_ge(lo_ready, first + 2 * j - 6)
                else:
                    split = sp.snap(sp.to_reg(first + 2 * j - 6))
                    sp.wait_ge(x_landed[0], 16)
                    sp.wait_ge(lo_ready, split)
                dst = raw[:, slot]
                if half:
                    dst = dst.rearrange("p k (a n) -> p (k a) n", n=HB)
                sp.dma_start(dst, src).then_inc(raw_landed[slot], 16)

            def load_block(first, b, view, col, k0=0):
                for q in range(4):
                    load(first, 4 * b + q, view[:, k0 + 4 * q:k0 + 4 * q + 4, bass.ds(col, NB)])

            def load_half(first, half, view, col, k0=0):
                for c in range(2):
                    load(first, 2 * half + c, view[:, k0 + 8 * c:k0 + 8 * c + 8, bass.ds(col, HB)], True)

            def load_features(first, b, view, col, k0=0):
                for i in range(2):
                    load_half(first, 2 * b + i, view, col + i * HB, k0)

            def gla(h):
                first = GLA_N * h + GLA0
                load_half(first, 0, w_in_v, h * GLA_DK)
                if isinstance(h, int):
                    sp.dma_start(wlr_raw[:, :, :], w_in_v[:, :, C_LR:C_LR + P]).then_inc(wlr_landed, 16)
                load_half(first, 1, w_in_v, h * GLA_DK + GLA_HEADS * GLA_DK)
                load_block(first, 1, w_in_v, h * NB + C_GV)
                load_block(first, 2, w_in_v, h * NB + C_GOUT)

            def diff(i):
                first = DIFF_N * i + DIFF0
                load_block(first, 0, w_in_v, i * NB + C_DQ)
                load_block(first, 1, w_in_v, i * NB + C_DK)
                load_block(first, 2, w_in_v, i * NB + C_DV)

            def branch(g):
                first = BR_N * g + BR0
                load_features(first, 0, w_in_v, g * NB + C_MG)
                load_features(first, 1, w_in_v, g * NB + C_MD)
                load_features(first, 2, w_br_v, g * NB)
                load_features(first, 3, w_br_v, g * NB, KT)

            def down(first, b, f):
                for q in range(4):
                    load(first, 4 * b + q, w_down_v[:, bass.ds(f, 1), :, q * NB:(q + 1) * NB].rearrange("p g k n -> p (g k) n"))

            sp.dma_start(resid[:, 0], x_v[:, 0]).then_inc(x_landed[0], 16)
            sp.dma_start(resid[:, 1], x_v[:, 1]).then_inc(x_landed[1], 16)
            sp.wait_ge(small_landed, 17 * 16)
            gla(0)
            with sp.Fori(1, GLA_HEADS) as h:
                gla(h)
            with sp.Fori(0, DIFF_PAIRS) as i:
                diff(i)
            with sp.Fori(0, GROUPS) as g:
                branch(g)
            load_block(OUT0, 0, w_out_v, 0)
            sp.wait_ge(pieces_used, OUT0 - BLOCK)
            sp.dma_start(resid[:, :, :], x_v).then_inc(resid_landed, 16)
            for b in range(1, 4):
                load_block(OUT0, b, w_out_v, b * NB)
            load_features(FFN0, 0, w_up_v, 0)
            load_features(FFN0, 1, w_up_v, FFN)
            with sp.Fori(1, LAST) as f:
                load_features(ffn_base(f), 0, w_up_v, f * NB)
                down(ffn_base(f), 1, f - 1)
                load_features(ffn_base(f), 2, w_up_v, f * NB + FFN)
            load_features(ffn_base(LAST), 0, w_up_v, LAST * NB)
            load_features(ffn_base(LAST), 1, w_up_v, LAST * NB + FFN)
            down(ffn_base(LAST), 2, LAST - 1)
            down(END0, 0, FFN_GROUPS - 1)
            for q in range(4):
                sp.wait_ge(down_added, 4 * (FFN_GROUPS - 1) + q + 1)
                sp.dma_start(out_v[:, :, q * NB:(q + 1) * NB], resid[:, :, q * NB:(q + 1) * NB]).then_inc(out_stored, 16)
            sp.wait_ge(out_stored, 4 * 16)

        @block.scalar
        def _(act):
            def fn(o_, i_, f, **kw):
                return nc.scalar.activation(o_, i_, f, **kw)

            def split_hi(first, j):
                slot = j % 4
                if j % 2 == 0:
                    act.wait_ge(raw_landed[(j // 2) % 4], (first + 8 * (j // 8) + 8) * 2)
                if not (isinstance(first, int) and first + j < 4):
                    act.wait_ge(pieces_used, first + j - 3)
                fn(whi[:, slot], raw[:, (j // 2) % 4, 2 * (j % 2):2 * (j % 2) + 2], ACT.Copy).then_inc(hi_ready, 1)

            def rsqrt(src, dst, width, eps, ready, ln_sem, rs_sem, n):
                act.wait_ge(ready, n)
                fn(dst, src, ACT.Ln, scale=1.0 / width, bias=eps).then_inc(ln_sem, 1)
                act.wait_ge(ln_sem, n)
                fn(dst, dst, ACT.Exp, scale=-0.5).then_inc(rs_sem, 1)

            def norm_rows(src, dst, sums, n):
                act.wait_ge(norm_rs, n)
                if n == 2:
                    act.wait_ge(pieces_used, FFN0)
                for b in range(4):
                    fn(dst[:, 0, b * NB:(b + 1) * NB], src[:, 0, b * NB:(b + 1) * NB], ACT.Copy,
                       scale=rs_x[:, 0:1]).then_inc(normed_act, 1)

            def norm_pair(pair, col, n):
                act.wait_ge(norm_T, 8 * (n - 1) + pair + 1)
                for k in (2 * pair, 2 * pair + 1):
                    last = fn(hT[:, k, 0], stage(pair)[:, (k % 2) * T:(k % 2 + 1) * T], ACT.Copy,
                              scale=cols[:, col + k:col + k + 1])
                last.then_inc(norm_hi, 1)

            def decay_inputs(j):
                if j == 2:
                    act.wait_ge(wlr_landed, 16)
                    fn(wlr_hi[:, :, :], wlr_raw[:, :, :], ACT.Copy).then_inc(wlr_hi_ready, 1)
                if j == 11:
                    act.wait_ge(lr_done, 1)
                    fn(lrT[0:GLA_RANK, :], mix[0:GLA_RANK, 0:T], ACT.Copy).then_inc(lr_ready, 1)
                if j in (12, 13):
                    act.wait_ge(gk_done, j - 11)
                    for k in range(4 * (j - 12), 4 * (j - 12) + 4):
                        last = fn(gkx[:, k], (acc_c, mix)[k // 4][:, (k % 4) * T:(k % 4 + 1) * T], ACT.Identity,
                                  bias=cols[:, V_BGK + k:V_BGK + k + 1])
                    last.then_inc(gkx_ready, 1)

            def decays(h, n):
                if n is not None:
                    act.wait_ge(gk_gate, n - 1)
                fn(dec[:, :, :], gkx[:, bass.ds(2 * h, 2), :], ACT.Abs).then_inc(gk_abs, 1)
                act.wait_ge(gk_abs, h + 1)
                fn(dec[:, :, :], dec[:, :, :], ACT.Exp, scale=-1.0).then_inc(gk_exp, 1)
                act.wait_ge(gk_exp, h + 1)
                fn(dec[:, :, :], dec[:, :, :], ACT.Ln, bias=one_c).then_inc(gk_ln, 1)

            def exponentials(h, first_head):
                act.wait_ge(bl_ready, h + 1)
                if not first_head:
                    act.wait_ge(operands_ready, h)
                s = 1.0 / GLA_NORMALIZER
                fn(e_pos[:, :, :], cum[:, :, :], ACT.Exp, scale=s)
                fn(e_neg[:, :, :], cum[:, :, :], ACT.Exp, scale=-s)

            def exponentials_tail(h):
                s = 1.0 / GLA_NORMALIZER
                for f in range(2):
                    for c in range(2):
                        fn(e_tail[:, f, c], cum[:, f, 2 * c * C:(2 * c + 1) * C], ACT.Exp, scale=-s,
                           bias=bl[:, 4 * f + 2 * c:4 * f + 2 * c + 1])
                    fn(e_tile[:, f, 0:C], cum[:, f, 0:C], ACT.Exp, scale=-s, bias=bl01[:, f:f + 1])
                    fn(e_tile[:, f, C:P], cum[:, f, C:P], ACT.Exp, scale=-s, bias=bl[:, 4 * f + 1:4 * f + 2])
                    last = fn(e_q3[:, f], cum[:, f, 3 * C:4 * C], ACT.Exp, scale=s, bias=bl[:, 4 * f + 2:4 * f + 3])
                last.then_inc(e_ready, 1)

            def gla(h, tail):
                first = GLA_N * h + GLA0
                first_head = tail is None
                at_decays, at_exp, at_exp_tail = (14, 15, 16) if first_head else (0, 5, 6)
                for j in range(GLA_N):
                    if first_head and j < HALF:
                        norm_pair(2 * j, V_N1, 1)
                        norm_pair(2 * j + 1, V_N1, 1)
                    split_hi(first, j)
                    if first_head:
                        decay_inputs(j)
                    if j == at_decays:
                        if first_head:
                            act.wait_ge(gkx_ready, 2)
                        decays(h, None if first_head else h + 1)
                    if j == at_exp:
                        exponentials(h, first_head)
                    if j == at_exp_tail:
                        exponentials_tail(h)
                    if first_head and j == 9:
                        rope_and_lambda()
                    if j == 19:
                        act.wait_ge(pieces_used, first + 2 * BLOCK)
                        if not first_head:
                            act.wait_ge(go_done, h)
                        fn(g_v[:, :, :], acc_a[:, :].rearrange("p (t n) -> p t n", t=TT), ACT.Copy).then_inc(gv_ready, 1)
                    if j == 22:
                        act.wait_ge(go_done, h + 1)
                        if not first_head:
                            act.wait_ge(og_ready, h)
                        for t, ps in enumerate((mix[:, NB:2 * NB], mix[:, 0:NB])):
                            last = fn(g_on[:, t], ps, ACT.Square, accum_out=g_ss[:, t:t + 1])
                        last.then_inc(go_sumsq, 1)
                        rsqrt(g_ss, g_rs, GLA_DV, eps_c, go_sumsq, go_ln, go_rs, h + 1)
                    if j == 23:
                        act.wait_ge(go_rs, h + 1)
                        for t, ps in enumerate((mix[:, NB:2 * NB], mix[:, 0:NB])):
                            last = fn(g_on[:, t], ps, ACT.Copy, scale=g_rs[:, t:t + 1])
                        last.then_inc(go_normed, 1)
                    if tail is not None:
                        gla_tail(j, tail)

            def gla_tail(j, n):
                if j == 3:
                    act.wait_ge(pieces_used, GLA_N * n + GLA0)
                    fn(g_exp[:, :], acc_c[:, :], ACT.Exp, scale=-1.0).then_inc(gout_exp, 1)
                if j == 13:
                    act.wait_ge(og_T, n)
                    for f in range(4):
                        last = fn(glaT[:, bass.ds(4 * n - 4 + f, 1), 0].rearrange("p a t -> p (a t)"),
                                  mix[:, f * T:(f + 1) * T], ACT.Copy, scale=cols[:, V_GLA + f:V_GLA + f + 1])
                    last.then_inc(glaT_hi_ready, 1)

            def rope_and_lambda():
                nc.scalar.preload_act_table_set("trig_and_small")
                act.wait_ge(rope_arg, 1)
                fn(rope_t[:, 4], rope_t[:, 3], ACT.Sin)
                fn(rope_t[:, 5], rope_t[:, 3], ACT.Sin, scale=0.5).then_inc(rope_sin, 1)
                nc.scalar.preload_act_table_set("natural_log_exp_and_others")
                act.wait_ge(lam_dot, 1)
                fn(lam2, lam2, ACT.Exp).then_inc(lam_exp, 1)

            def diff(i, tail, gtail):
                first = DIFF_N * i + DIFF0
                for j in range(DIFF_N):
                    split_hi(first, j)
                    if tail is not None:
                        diff_tail(j, tail)
                    if gtail is not None:
                        gla_tail(j, gtail)
                    if j == 11:
                        act.wait_ge(pieces_used, first + BLOCK)
                        if gtail is None:
                            act.wait_ge(k_ss, i)
                        fn(sq[:, :, :], acc_a[:, :].rearrange("p (s d) -> p s d", d=DH), ACT.Square).then_inc(q_sq, 1)
                    if j == 12:
                        rsqrt(dq_ss, dq_rs, DH, eps_c, q_ss, q_ln, q_rs, i + 1)
                    if j == 20:
                        act.wait_ge(q_T, i + 1)
                        if gtail is None:
                            act.wait_ge(scores_done[1], i)
                        fn(qT[:, :, :], mix[:, :].rearrange("p (s t) -> p s t", t=T), ACT.Copy).then_inc(qT_ready, 1)
                    if j == 19:
                        act.wait_ge(pieces_used, first + 2 * BLOCK)
                        act.wait_ge(q_ss, i + 1)
                        fn(sq[:, :, :], acc_b[:, :].rearrange("p (s d) -> p s d", d=DH), ACT.Square).then_inc(k_sq, 1)
                    if j == 20:
                        rsqrt(dk_ss, dk_rs, DH, eps_c, k_ss, k_ln, k_rs, i + 1)

            def diff_tail(j, n):
                if j == 1:
                    act.wait_ge(k_T, n)
                    fn(kT[:, :, :], mix[:, :].rearrange("p (s t) -> p s t", t=T), ACT.Copy).then_inc(kT_ready, 1)
                if j == 3:
                    act.wait_ge(pieces_used, DIFF_N * n + DIFF0)
                    fn(d_v[:, :, :], acc_c[:, :].rearrange("p (t n) -> p t n", t=TT), ACT.Copy).then_inc(dv_ready, 1)
                if j in (7, 10):
                    half = (7, 10).index(j)
                    act.wait_ge(max_ready[half], n)
                    for s in (2 * half, 2 * half + 1):
                        for t, a in enumerate((prob[:, s, 0:P], prob[:, s, P:3 * P])):
                            k = 2 * s + t
                            last = fn(a, a, ACT.Exp, scale=DH ** -0.5, bias=s_nmax[:, k:k + 1],
                                      accum_out=p_sum[:, k:k + 1])
                    last.then_inc(exp_ready[half], 1)
                if j == 14:
                    act.wait_ge(att_T, n)
                    for hh in range(2):
                        last = fn(attT[:, hh], mix[:, hh * NB:hh * NB + 3 * P], ACT.Copy)
                    last.then_inc(attT_ready, 1)
                if j == 16:
                    act.wait_ge(pv_done, n)
                    act.wait_ge(k_ss, n)
                    for k in range(4):
                        last = fn(d_on[:, k // 2, (k % 2) * T:(k % 2 + 1) * T], mix[:, k * T:(k + 1) * T], ACT.Square,
                                  accum_out=o_ss[:, k:k + 1])
                    last.then_inc(do_sumsq, 1)
                    rsqrt(o_ss, o_rs, 2 * DH, sub_eps_c, do_sumsq, do_ln, do_rs, n)
                if j == 22:
                    act.wait_ge(do_T, n)
                    for f in range(4):
                        last = fn(diffT[:, bass.ds(4 * n - 4 + f, 1), 0].rearrange("p a t -> p (a t)"),
                                  mix[:, f * T:(f + 1) * T], ACT.Copy, scale=cols[:, V_SUB + f % 2:V_SUB + f % 2 + 1])
                    last.then_inc(diffT_hi_ready, 1)

            def branch(g, tail, dtail):
                first = BR_N * g + BR0
                for j in range(BR_N):
                    split_hi(first, j)
                    if dtail is not None:
                        diff_tail(j, dtail)
                    if tail is not None:
                        branch_tail(j, tail)
                    if j == 23:
                        if dtail is not None:
                            nc.scalar.preload_act_table_set("sigmoid_and_others")
                        act.wait_ge(halves_summed, BR_HALVES * g + 4)
                        fn(gate_g[:, :, :], gate_g[:, :, :], ACT.Sigmoid)
                        fn(gate_d[:, :, :], gate_d[:, :, :], ACT.Sigmoid).then_inc(gates_ready, 1)

            def branch_tail(j, n):
                if j == 4:
                    act.wait_ge(mixed_ready, n)
                    fn(mixT_hi[:, bass.ds(4 * n - 4, 4), :], gate_g[:, :, :], ACT.Copy).then_inc(mixT_hi_ready, 1)

            def out_sumsq(b):
                act.wait_ge(x1_ready, b + 1)
                if b >= 1:
                    act.wait_ge(x1_sumsq, b)
                for t in range(TT):
                    last = fn(gate_g[:, 2 * t:2 * t + 2].rearrange("p a t -> p (a t)"), resid[:, t, b * NB:(b + 1) * NB],
                              ACT.Square, accum_out=ss_out[:, 4 * t + b:4 * t + b + 1])
                last.then_inc(x1_sumsq, 1)

            def ffn_conv(j, f):
                if j in (8, 12):
                    half = (8, 12).index(j)
                    act.wait_ge(halves_summed, 4 * f + (FFN_HALF0 + half + 1))
                    if not (isinstance(f, int) and f == 0):
                        act.wait_ge(hid_lo_ready, f)
                    for k in (2 * half, 2 * half + 1):
                        last = fn(conv[:, k], up_sum[:, k], ACT.Identity,
                                  scale=cols[:, bass.ds(f * 4 + (V_CW2 + k), 1)],
                                  bias=cols[:, bass.ds(f * 4 + (V_CB + k), 1)])
                    last.then_inc(conv_first, 1)
                if j in (11, 15):
                    half = (11, 15).index(j)
                    act.wait_ge(conv_ready, 2 * f + (half + 1))
                    a = conv[:, 2 * half:2 * half + 2]
                    fn(a, a, ACT.Silu).then_inc(conv_silu, 1)

            def hidden_hi(n, dst):
                act.wait_ge(hid_ready, n)
                if dst is hid_hi:
                    act.wait_ge(pieces_used, ffn_base(n) - BLOCK)
                fn(dst[:, :, :], conv[:, :, :], ACT.Copy).then_inc(hid_hi_ready, 1)

            nc.scalar.preload_act_table_set("natural_log_exp_and_others")
            for r, c0, v in ((0, V_N1, norm1_g), (0, V_N2, norm2_g), (0, V_BGK, b_gk), (0, V_GLA, gla_norm_g),
                             (0, V_SUB, subln_g), (0, V_CW0, conv_w[:, 0]), (1, V_CW1 - 90, conv_w[:, 1]),
                             (1, V_CW2 - 90, conv_w[:, 2]), (2, 0, conv_b)):
                n = v.shape[-1] // P
                act.dma_start(rows[c0:c0 + n, r, :], v[0].rearrange("(a b) -> a b", b=P)).then_inc(small_landed, 16)
            act.dma_start(wup[0:GLA_RANK, :], w_gk_up[0]).then_inc(small_landed, 16)
            act.dma_start(qk_g[:, 0], q_norm_g.broadcast_to([P, P])).then_inc(small_landed, 16)
            act.dma_start(qk_g[:, 1], k_norm_g.broadcast_to([P, P])).then_inc(small_landed, 16)
            for k, v in enumerate((lambda_q1, lambda_k1, lambda_q2, lambda_k2)):
                act.dma_start(lam_v[:, k], v.broadcast_to([P, P])).then_inc(small_landed, 16)
            act.dma_start(pos_i.bitcast(I32), positions[0].rearrange("(t p) -> p t", p=P),
                          allow_slow_non_contiguous=True).then_inc(small_landed, 16)

            act.wait_ge(x_landed[0], 16)
            fn(normed[:, 0], resid[:, 0], ACT.Square, accum_out=ss_x[:, 0:1]).then_inc(sumsq_act, 1)
            act.wait_ge(consts_ready, 1)
            act.wait_ge(sumsq_dve, 1)
            rsqrt(ss_x, rs_x, D, eps_c, sumsq_act, norm_ln, norm_rs, 1)
            norm_rows(resid, normed, ss_x, 1)
            act.wait_ge(cols_ready, 1)

            gla(0, None)
            with act.Fori(1, GLA_HEADS) as h:
                gla(h, h)
            diff(0, None, GLA_HEADS)
            with act.Fori(1, DIFF_PAIRS) as i:
                diff(i, i, None)
            branch(0, None, DIFF_PAIRS)
            with act.Fori(1, GROUPS) as g:
                branch(g, g, None)
            for j in range(4 * BLOCK):
                split_hi(OUT0, j)
                branch_tail(j, GROUPS)
                if j == 8:
                    nc.scalar.preload_act_table_set("natural_log_exp_and_others")
                if j % 8 == 4 and j > 4:
                    out_sumsq(j // 8 - 1)
            for j in range(2 * BLOCK):
                if j == 4:
                    norm_pair(6, V_N2, 2)
                    norm_pair(7, V_N2, 2)
                split_hi(FFN0, j)
                if j == 3:
                    out_sumsq(3)
                    rsqrt(ss_x, rs_x, D, eps_c, sumsq_dve, norm_ln, norm_rs, 2)
                    norm_rows(resid, xn2, ss_x, 2)
                    for pair in range(6):
                        norm_pair(pair, V_N2, 2)
                if j == 7:
                    nc.scalar.preload_act_table_set("silu_and_others")
                ffn_conv(j, 0)
            with act.Fori(1, LAST) as f:
                for j in range(FFN_N):
                    split_hi(ffn_base(f), j)
                    if j == 3:
                        hidden_hi(f, hid_hi)
                    ffn_conv(j, f)
            for j in range(FFN_N):
                split_hi(ffn_base(LAST), j)
                if j == 3:
                    hidden_hi(LAST, hid_hi)
                ffn_conv(j, LAST)
                if j == 19:
                    hidden_hi(FFN_GROUPS, last_hi)
            for j in range(BLOCK):
                split_hi(END0, j)

        @block.vector
        def _(dve):
            V = nc.vector

            def split_lo(first, j):
                slot = j % 4
                dve.wait_ge(hi_ready, first + j + 1)
                V.tensor_tensor(wlo[:, slot], raw[:, (j // 2) % 4, 2 * (j % 2):2 * (j % 2) + 2],
                                whi[:, slot].bitcast(F32), ALU.subtract).then_inc(lo_ready, 1)

            def norm_rows(src, dst, n):
                dve.wait_ge(norm_rs, n)
                for b in range(4):
                    V.tensor_scalar(dst[:, 1, b * NB:(b + 1) * NB], src[:, 1, b * NB:(b + 1) * NB], rs_x[:, 1:2], None,
                                    ALU.mult).then_inc(normed_dve, 1)

            def out_of(acc, dst):
                return V.tensor_reduce(dst, acc[:, :].rearrange("p (f s t) -> p f t s", f=2, s=2), AX.X, ALU.add)

            def norm_pair(pair, col, n):
                dve.wait_ge(norm_hi, 8 * (n - 1) + pair + 1)
                for k in (2 * pair, 2 * pair + 1):
                    last = V.scalar_tensor_tensor(out=hT[:, k, 1], in0=stage(pair)[:, (k % 2) * T:(k % 2 + 1) * T],
                                                  scalar=cols[:, col + k:col + k + 1], in1=hT[:, k, 0].bitcast(F32),
                                                  op0=ALU.mult, op1=ALU.subtract)
                last.then_inc(norm_lo, 1)

            def rope_and_lambda():
                n_rope = [0]

                def then(ins):
                    n_rope[0] += 1
                    ins.then_inc(rope_step, 1)
                    dve.wait_ge(rope_step, n_rope[0])

                pos, ang, turns, red = (rope_t[:, k] for k in range(4))
                then(V.tensor_copy(pos[:, :, 0], pos_i.bitcast(I32)))
                for t in range(TT):
                    ins = V.tensor_scalar(ang[:, t], inv_f, pos[:, t, 0:1], None, ALU.mult)
                then(ins)
                for unit in (4096.0, 1.0):
                    src = ang
                    then(V.tensor_scalar(turns, src, 1.0 / (2.0 * math.pi * unit), None, ALU.mult))
                    then(V.tensor_scalar(turns, turns, ROUND, None, ALU.add))
                    then(V.tensor_scalar(turns, turns, -ROUND, None, ALU.add))
                    for piece in TWO_PI:
                        then(V.scalar_tensor_tensor(out=ang, in0=turns, scalar=-piece * unit, in1=ang,
                                                    op0=ALU.mult, op1=ALU.add))
                pi = float(np.nextafter(np.float32(math.pi), np.float32(0)))
                V.tensor_scalar(red, ang, pi, -pi, ALU.min, ALU.max).then_inc(rope_arg, 1)
                for k in range(2):
                    ins = V.tensor_tensor_reduce(lam_p[:, k], lam_v[:, 2 * k], lam_v[:, 2 * k + 1], 1.0, 0.0,
                                                 ALU.mult, ALU.add, lam2[:, k:k + 1])
                ins.then_inc(lam_dot, 1)

            def rope_and_lambda_end():
                dve.wait_ge(rope_sin, 1)
                V.scalar_tensor_tensor(out=rope_t[:, 5], in0=rope_t[:, 5], scalar=-2.0, in1=rope_t[:, 5],
                                       op0=ALU.mult, op1=ALU.mult).then_inc(rope_ready, 1)
                dve.wait_ge(rope_ready, 1)
                V.tensor_scalar(rope_t[:, 5], rope_t[:, 5], 1.0, None, ALU.add).then_inc(rope_ready, 1)
                dve.wait_ge(lam_exp, 1)
                V.tensor_tensor(neg_lam, lam2[:, 1:2], lam2[:, 0:1], ALU.subtract).then_inc(lam_ready, 1)
                dve.wait_ge(lam_ready, 1)
                V.tensor_scalar(neg_lam, neg_lam, -LAMBDA_INIT, None, ALU.add).then_inc(lam_ready, 1)

            def cumulate(h, first_head):
                if not first_head:
                    dve.wait_ge(cum_ready, h)
                else:
                    dve.wait_ge(gkx_ready, 2)
                V.tensor_scalar(gmin[:, :, :], gkx[:, bass.ds(2 * h, 2), :], 0.0, None, ALU.min).then_inc(gk_min, 1)
                dve.wait_ge(gk_min, h + 1)
                dve.wait_ge(gk_ln, h + 1)
                V.tensor_tensor(gmin[:, :, :], gmin[:, :, :], dec[:, :, :], ALU.subtract).then_inc(gk_gate, 1)
                dve.wait_ge(gk_gate, h + 1)
                if not first_head:
                    dve.wait_ge(e_ready, h)
                for f in range(2):
                    last = V.tensor_tensor_scan(cum[:, f], reset[:, :], gmin[:, f], 0.0, ALU.mult, ALU.add)
                last.then_inc(cum_ready, 1)
                dve.wait_ge(cum_ready, h + 1)
                V.tensor_scalar(bl.rearrange("p (f c) -> p f c", f=2),
                                cum[:, :, :].rearrange("p f (c t) -> p f c t", t=C)[:, :, :, C - 1],
                                1.0 / GLA_NORMALIZER, None, ALU.mult).then_inc(bl_scaled, 1)
                dve.wait_ge(bl_scaled, h + 1)
                b4 = bl.rearrange("p (f c) -> p f c", f=2)
                V.tensor_tensor(bl01, b4[:, :, 0], b4[:, :, 1], ALU.add).then_inc(bl_ready, 1)

            def gla(h, tail):
                first = GLA_N * h + GLA0
                first_head = tail is None
                qp, kp = q_sum[:, :, :], k_sum[:, :, :]
                at_cum, at_operands, at_AT = (15, 16, 19) if first_head else (2, 11, 17)
                for j in range(GLA_N):
                    if first_head and j < HALF:
                        norm_pair(2 * j, V_N1, 1)
                        norm_pair(2 * j + 1, V_N1, 1)
                    split_lo(first, j)
                    if first_head and j == 2:
                        dve.wait_ge(wlr_hi_ready, 1)
                        V.tensor_tensor(wlr_lo[:, :, :], wlr_raw[:, :, :], wlr_hi[:, :, :].bitcast(F32), ALU.subtract)\
                         .then_inc(wlr_lo_ready, 1)
                    if j == at_cum:
                        cumulate(h, first_head)
                    if first_head and j == 7:
                        rope_and_lambda()
                    if j == 7:
                        dve.wait_ge(pieces_used, first + HALF)
                        if not first_head:
                            dve.wait_ge(operands_ready, h)
                        out_of(acc_a, q_sum[:, :, :]).then_inc(q_summed, 1)
                    if j == 11:
                        dve.wait_ge(pieces_used, first + BLOCK)
                        out_of(acc_b, k_sum[:, :, :]).then_inc(k_summed, 1)
                    if j == at_operands:
                        dve.wait_ge(q_summed, h + 1)
                        dve.wait_ge(k_summed, h + 1)
                        dve.wait_ge(e_ready, h + 1)
                        if not first_head:
                            dve.wait_ge(A_done, h)
                        V.scalar_tensor_tensor(out=q_dec[:, :, :], in0=qp, scalar=GLA_DK ** -0.5, in1=e_pos[:, :, :],
                                               op0=ALU.mult, op1=ALU.mult)
                        V.tensor_tensor(k_inv[:, :, :], kp, e_neg[:, :, :], ALU.mult)
                    if j == at_operands + 1:
                        def chunks(a, odd):
                            return a.rearrange("p f (c s t) -> p f c s t", s=2, t=C)[:, :, :, odd]
                        V.tensor_tensor(chunks(k_mix[:, :, :], 0), chunks(kp, 0), e_tail[:, :, :, :], ALU.mult)
                        V.tensor_tensor(chunks(k_mix[:, :, :], 1), chunks(kp, 1), chunks(e_neg[:, :, :], 1), ALU.mult)
                        V.tensor_tensor(k_tile[:, :, :], kp[:, :, 0:P], e_tile[:, :, :], ALU.mult)
                        V.scalar_tensor_tensor(out=q_3[:, :, :], in0=qp[:, :, 3 * C:4 * C], scalar=GLA_DK ** -0.5,
                                               in1=e_q3[:, :, :], op0=ALU.mult, op1=ALU.mult).then_inc(operands_ready, 1)
                    if first_head and j == 14:
                        rope_and_lambda_end()
                    if j == at_AT:
                        dve.wait_ge(A_done, h + 1)
                        if not first_head:
                            dve.wait_ge(go_done, h)
                        V.tensor_copy(AT[:, 2], mix[:, 2 * P:3 * P])
                        dve.wait_ge(consts_ready, 1)
                        for t in range(TT):
                            last = V.copy_predicated(AT[:, t], keep[:, :].bitcast(U32), mix[:, t * P:(t + 1) * P])
                        last.then_inc(AT_ready, 1)
                    if tail is not None:
                        gla_tail(j, tail)

            def gla_tail(j, n):
                if j == 3:
                    dve.wait_ge(gout_exp, n)
                    V.tensor_scalar(g_exp[:, :], g_exp[:, :], 1.0, None, ALU.add).then_inc(gout_one, 1)
                if j == 4:
                    dve.wait_ge(gout_one, n)
                    V.reciprocal(g_exp[:, :], g_exp[:, :]).then_inc(gout_inv, 1)
                if j == 5:
                    dve.wait_ge(gout_inv, n)
                    V.tensor_tensor(g_silu[:, :, :].rearrange("p t n -> p (t n)"), acc_c[:, :], g_exp[:, :],
                                    ALU.mult).then_inc(gout_silu, 1)
                if j == 13:
                    dve.wait_ge(glaT_hi_ready, n)
                    for f in range(4):
                        last = V.scalar_tensor_tensor(
                            out=glaT[:, bass.ds(4 * n - 4 + f, 1), 1].rearrange("p a t -> p (a t)"),
                            in0=mix[:, f * T:(f + 1) * T], scalar=cols[:, V_GLA + f:V_GLA + f + 1],
                            in1=glaT[:, bass.ds(4 * n - 4 + f, 1), 0].rearrange("p a t -> p (a t)").bitcast(F32),
                            op0=ALU.mult, op1=ALU.subtract)
                    last.then_inc(glaT_lo_ready, 1)

            def head_sums(sq_sem, out_ss, done, n):
                dve.wait_ge(sq_sem, n)
                V.tensor_reduce(out_ss, sq[:, :, :], AX.X, ALU.add).then_inc(done, 1)

            def head_scale(acc, dst, rs, rs_sem, done, n, free_sem, free_n):
                dve.wait_ge(rs_sem, n)
                if free_n is not None:
                    dve.wait_ge(free_sem, free_n)
                V.tensor_tensor(dst[:, :, :, :].rearrange("p t s d -> p (t s) d"),
                                acc[:, :].rearrange("p (s d) -> p s d", d=DH),
                                rs.unsqueeze(2).broadcast_to([P, 8, DH]), ALU.mult).then_inc(done, 1)

            def diff(i, tail, gtail):
                first = DIFF_N * i + DIFF0
                for j in range(DIFF_N):
                    split_lo(first, j)
                    if tail is not None:
                        diff_tail(j, tail)
                    if gtail is not None:
                        gla_tail(j, gtail)
                    if j == 11:
                        head_sums(q_sq, dq_ss, q_ss, i + 1)
                    if j == 13:
                        head_scale(acc_a, qn, dq_rs, q_rs, q_normed, i + 1, q_T, i if gtail is None else None)
                    if j == 19:
                        head_sums(k_sq, dk_ss, k_ss, i + 1)
                    if j == 21:
                        head_scale(acc_b, kn, dk_rs, k_rs, k_normed, i + 1, k_T, i if gtail is None else None)

            def diff_tail(j, n):
                if j in (5, 8):
                    half = (5, 8).index(j)
                    dve.wait_ge(consts_ready, 1)
                    dve.wait_ge(scores_done[half], n)
                    for s in (2 * half, 2 * half + 1):
                        ps = mix[:, (s % 2) * NB:(s % 2) * NB + 3 * P]
                        for t, (a, b) in enumerate(((0, P), (P, 3 * P))):
                            k = 2 * s + t
                            last = V.tensor_tensor_reduce(prob[:, s, a:b], ps[:, a:b], causal[:, T - (b - a):T], 1.0, -3.0e38,
                                                          ALU.add, ALU.max, s_max[:, k:k + 1])
                    last.then_inc(max_found[half], 1)
                    dve.wait_ge(max_found[half], n)
                    V.tensor_scalar(s_nmax[:, 4 * half:4 * half + 4], s_max[:, 4 * half:4 * half + 4], -DH ** -0.5, None,
                                    ALU.mult).then_inc(max_ready[half], 1)
                if j == 11:
                    dve.wait_ge(exp_ready[0], n)
                    dve.wait_ge(exp_ready[1], n)
                    V.reciprocal(p_inv, p_sum).then_inc(sums_inv, 1)
                    dve.wait_ge(sums_inv, n)
                    V.tensor_scalar(p_lam.rearrange("p (h t) -> p h t", h=2),
                                    p_inv.rearrange("p (h s t) -> p h s t", h=2, s=2)[:, :, 1], neg_lam, None,
                                    ALU.mult).then_inc(sums_lam, 1)
                    dve.wait_ge(sums_lam, n)
                    spans = [(hh, t, a, b) for hh in range(2) for t, (a, b) in enumerate(((0, P), (P, 3 * P)))]
                    for hh, t, a, b in spans:
                        last = V.tensor_scalar(prob[:, 2 * hh + 1, a:b], prob[:, 2 * hh + 1, a:b],
                                               p_lam[:, 2 * hh + t:2 * hh + t + 1], None, ALU.mult)
                    last.then_inc(att_second, 1)
                    dve.wait_ge(att_second, n)
                    for hh, t, a, b in spans:
                        k = 4 * hh + t
                        last = V.scalar_tensor_tensor(out=att[:, hh, a:b], in0=prob[:, 2 * hh, a:b], scalar=p_inv[:, k:k + 1],
                                                      in1=prob[:, 2 * hh + 1, a:b], op0=ALU.mult, op1=ALU.add)
                    last.then_inc(att_ready, 1)
                if j == 17:
                    dve.wait_ge(do_rs, n)
                    for hh in range(2):
                        last = V.tensor_tensor(d_on[:, :, hh * T:(hh + 1) * T],
                                               mix[:, hh * NB:(hh + 1) * NB].rearrange("p (t e) -> p t e", t=TT),
                                               o_rs[:, 2 * hh:2 * hh + 2].unsqueeze(2).broadcast_to([P, TT, T]), ALU.mult)
                    last.then_inc(do_normed, 1)
                if j == 22:
                    dve.wait_ge(diffT_hi_ready, n)
                    for f in range(4):
                        last = V.scalar_tensor_tensor(
                            out=diffT[:, bass.ds(4 * n - 4 + f, 1), 1].rearrange("p a t -> p (a t)"),
                            in0=mix[:, f * T:(f + 1) * T], scalar=cols[:, V_SUB + f % 2:V_SUB + f % 2 + 1],
                            in1=diffT[:, bass.ds(4 * n - 4 + f, 1), 0].rearrange("p a t -> p (a t)").bitcast(F32),
                            op0=ALU.mult, op1=ALU.subtract)
                    last.then_inc(diffT_lo_ready, 1)

            def branch(g, tail, dtail):
                first = BR_N * g + BR0
                for j in range(BR_N):
                    split_lo(first, j)
                    if dtail is not None:
                        diff_tail(j, dtail)
                    if tail is not None:
                        branch_tail(j, tail)
                    if j in (7, 11, 15, 19):
                        half = (7, 11, 15, 19).index(j)
                        dve.wait_ge(pieces_used, first + HALF * (half + 1))
                        if tail is not None:
                            dve.wait_ge(mixT_hi_ready, g)
                            dve.wait_ge(mixT_lo_ready, g)
                        out_of((acc_a, acc_b)[half % 2],
                               (gate_g, gate_d)[half // 2][:, 2 * (half % 2):2 * (half % 2) + 2]).then_inc(halves_summed, 1)
                    if j in (23, 27, 31):
                        branch_gate((23, 27, 31).index(j), first, g + 1, dtail is not None)

            def branch_gate(half, first, n, after_diff):
                if half == 0 and after_diff:
                    dve.wait_ge(do_T, DIFF_PAIRS)
                elif half >= 2 or not after_diff:
                    dve.wait_ge(y_gated, 4 * n - 5 + half)
                dve.wait_ge(pieces_used, first + HALF * (half + 5))
                y = y_sum[:, half % 2]
                out_of((acc_a, acc_b)[half % 2], y).then_inc(halves_summed, 1)
                gate = (gate_g, gate_d)[half // 2][:, 2 * (half % 2):2 * (half % 2) + 2]
                dve.wait_ge(gates_ready, n)
                dve.wait_ge(halves_summed, BR_HALVES * n - 3 + half)
                V.tensor_tensor(gate, y, gate, ALU.mult).then_inc(y_gated, 1)

            def branch_tail(j, n):
                if j == 3:
                    branch_gate(3, BR_N * n + (BR0 - BR_N), n, False)
                    dve.wait_ge(y_gated, 4 * n)
                    V.tensor_tensor(gate_g[:, :, :], gate_g[:, :, :], gate_d[:, :, :], ALU.add).then_inc(mixed_ready, 1)
                if j == 4:
                    dve.wait_ge(mixT_hi_ready, n)
                    V.tensor_tensor(mixT_lo[:, bass.ds(4 * n - 4, 4), :], gate_g[:, :, :],
                                    mixT_hi[:, bass.ds(4 * n - 4, 4), :].bitcast(F32), ALU.subtract).then_inc(mixT_lo_ready, 1)

            def add_x(b):
                dve.wait_ge(pieces_used, OUT0 + (b + 1) * BLOCK)
                dve.wait_ge(resid_landed, 16)
                dst = resid[:, :, b * NB:(b + 1) * NB]
                V.tensor_tensor(dst, (acc_a, acc_b)[b % 2][:, :].rearrange("p (t n) -> p t n", t=TT), dst,
                                ALU.add).then_inc(x1_ready, 1)

            def ffn_half(acc, first, i, n):
                half = i % 2
                dve.wait_ge(pieces_used, first)
                if i >= 2:
                    dve.wait_ge(conv_ready, 2 * n)
                elif not (isinstance(n, int) and n == 1):
                    dve.wait_ge(hid_ready, n - 1)
                out_of(acc, up_sum[:, 2 * half:2 * half + 2]).then_inc(halves_summed, 1)

            def ffn_conv(j, f):
                base = FFN0 if isinstance(f, int) and f == 0 else ffn_base(f)
                for half in range(2):
                    if j == 7 + 4 * half:
                        ffn_half((acc_a, acc_b)[half], base + HALF * (half + 1), half, f + 1)
                    if j == 9 + 4 * half:
                        dve.wait_ge(conv_first, 2 * f + (half + 1))
                        for k in (2 * half, 2 * half + 1):
                            last = V.scalar_tensor_tensor(out=conv[:, k, 1:T], in0=up_sum[:, k, 0:T - 1],
                                                          scalar=cols[:, bass.ds(f * 4 + (V_CW1 + k), 1)],
                                                          in1=conv[:, k, 1:T], op0=ALU.mult, op1=ALU.add)
                        last.then_inc(conv_second, 1)
                    if j == 10 + 4 * half:
                        dve.wait_ge(conv_second, 2 * f + (half + 1))
                        for k in (2 * half, 2 * half + 1):
                            last = V.scalar_tensor_tensor(out=conv[:, k, 2:T], in0=up_sum[:, k, 0:T - 2],
                                                          scalar=cols[:, bass.ds(f * 4 + (V_CW0 + k), 1)],
                                                          in1=conv[:, k, 2:T], op0=ALU.mult, op1=ALU.add)
                        last.then_inc(conv_ready, 1)

            def hidden(n, done, hi, lo):
                ffn_half(acc_b, done, 3, n)
                dve.wait_ge(conv_silu, 2 * n)
                dve.wait_ge(halves_summed, 4 * n + FFN_HALF0)
                V.tensor_tensor(conv[:, :, :], up_sum[:, :, :], conv[:, :, :], ALU.mult).then_inc(hid_ready, 1)
                dve.wait_ge(hid_hi_ready, n)
                V.tensor_tensor(lo[:, :, :], conv[:, :, :], hi[:, :, :].bitcast(F32), ALU.subtract)\
                 .then_inc(hid_lo_ready, 1)

            def add_down(first, q, n):
                dve.wait_ge(pieces_used, first + 2 * (q + 1))
                dst = resid[:, :, q * NB:(q + 1) * NB]
                V.tensor_tensor(dst, (acc_c, mix)[q % 2][:, :].rearrange("p (t n) -> p t n", t=TT), dst,
                                ALU.add).then_inc(down_added, 1)

            dve.wait_ge(x_landed[1], 16)
            V.tensor_tensor_reduce(normed[:, 1], resid[:, 1], resid[:, 1], 1.0, 0.0, ALU.mult, ALU.add,
                                   ss_x[:, 1:2]).then_inc(sumsq_dve, 1)
            dve.wait_ge(cols_T, 1)
            V.tensor_copy(cols[:, 0:90], mix[:, 0:90])
            V.tensor_copy(cols[:, 90:222], mix[:, 90:222]).then_inc(scale_ready, 1)
            dve.wait_ge(scale_ready, 1)
            V.tensor_scalar(cols[:, V_SUB:V_SUB + 2], cols[:, V_SUB:V_SUB + 2], 1.0 - LAMBDA_INIT, None,
                            ALU.mult).then_inc(cols_ready, 1)
            norm_rows(resid, normed, 1)

            gla(0, None)
            with dve.Fori(1, GLA_HEADS) as h:
                gla(h, h)
            diff(0, None, GLA_HEADS)
            with dve.Fori(1, DIFF_PAIRS) as i:
                diff(i, i, None)
            branch(0, None, DIFF_PAIRS)
            with dve.Fori(1, GROUPS) as g:
                branch(g, g, None)
            for j in range(4 * BLOCK):
                split_lo(OUT0, j)
                branch_tail(j, GROUPS)
                if j % 8 == 3 and j > 3:
                    add_x(j // 8 - 1)
            for j in range(2 * BLOCK):
                if j == 4:
                    norm_pair(6, V_N2, 2)
                    norm_pair(7, V_N2, 2)
                split_lo(FFN0, j)
                if j == 3:
                    add_x(3)
                    dve.wait_ge(x1_sumsq, 4)
                    V.tensor_reduce(ss_x, ss_out.rearrange("p (t b) -> p t b", t=TT), AX.X, ALU.add).then_inc(sumsq_dve, 1)
                    norm_rows(resid, xn2, 2)
                    for pair in range(6):
                        norm_pair(pair, V_N2, 2)
                ffn_conv(j, 0)
                if j == 15:
                    ffn_half(acc_a, FFN0 + 3 * HALF, 2, 1)
            with dve.Fori(1, LAST) as f:
                for j in range(FFN_N):
                    split_lo(ffn_base(f), j)
                    if j == 3:
                        hidden(f, ffn_base(f), hid_hi, hid_lo)
                    ffn_conv(j, f)
                    if j in (13, 15, 17, 19):
                        add_down(ffn_base(f) + BLOCK, (j - 13) // 2, f)
                    if j == 23:
                        ffn_half(acc_a, ffn_base(f) + 5 * HALF, 2, f + 1)
            for j in range(FFN_N):
                split_lo(ffn_base(LAST), j)
                if j == 3:
                    hidden(LAST, ffn_base(LAST), hid_hi, hid_lo)
                ffn_conv(j, LAST)
                if j == 15:
                    ffn_half(acc_a, ffn_base(LAST) + 3 * HALF, 2, FFN_GROUPS)
                if j == 19:
                    hidden(FFN_GROUPS, ffn_base(LAST) + 2 * BLOCK, last_hi, last_lo)
                if j in (21, 23):
                    add_down(ffn_base(LAST) + 2 * BLOCK, (j - 21) // 2, LAST)
            for j in range(BLOCK):
                split_lo(END0, j)
                if j in (1, 3):
                    add_down(ffn_base(LAST) + 2 * BLOCK, (j + 3) // 2, LAST)
                if j in (5, 7):
                    add_down(END0, (j - 5) // 2, FFN_GROUPS)
            add_down(END0, 2, FFN_GROUPS)
            add_down(END0, 3, FFN_GROUPS)

        @block.gpsimd
        def _(pool):
            G = nc.gpsimd
            G.memset(ident[:, :], 0.0)
            G.memset(keep[:, :], 1.0)
            G.memset(causal[:, :], 0.0)
            G.memset(AT[:, :, :], 0.0)
            G.memset(reset[:, :], 1.0)
            G.memset(cols[:, :], 0.0)
            G.memset(eps_c, EPS)
            G.memset(sub_eps_c, SUBLN_EPS)
            G.memset(one_c, 1.0)
            for k in range(ROPE // 2):
                f = float(np.float32(ROPE_THETA) ** (-np.float32(2 * k) / np.float32(ROPE)))
                last = G.memset(inv_f[:, k:k + 1], f)
            last.then_inc(const_step, 1)
            pool.wait_ge(const_step, 1)
            G.affine_select(out=ident[:, :], in_=ident[:, :], compare_op=ALU.not_equal, fill=1.0, base=0,
                            pattern=[[-1, P]], channel_multiplier=1)
            G.affine_select(out=keep[:, :], in_=keep[:, :], compare_op=ALU.is_ge, fill=0.0, base=0,
                            pattern=[[1, P]], channel_multiplier=-1)
            G.affine_select(out=causal[:, P:T], in_=causal[:, P:T], compare_op=ALU.is_ge, fill=-1.0e30, base=0,
                            pattern=[[-1, P]], channel_multiplier=1)
            G.memset(reset[:, :].rearrange("p (c t) -> p c t", t=C)[:, :, 0:1], 0.0).then_inc(consts_ready, 1)

            def gla_tail(n):
                pool.wait_ge(go_normed, n)
                pool.wait_ge(gout_silu, n)
                if not (isinstance(n, int) and n == 1):
                    pool.wait_ge(og_T, n - 1)
                G.tensor_tensor(g_og[:, :, :], g_on[:, :, :], g_silu[:, :, :], ALU.mult).then_inc(og_ready, 1)

            def turn(buf, which, normed_sem, scaled, turned, roped, n):
                v = buf[:, :, :, :].rearrange("p t s d -> p (t s) d")
                pool.wait_ge(normed_sem, n)
                G.tensor_tensor(v, v, qk_g[:, which].unsqueeze(1).broadcast_to([P, 8, DH]), ALU.mult).then_inc(scaled, 1)
                pool.wait_ge(scaled, n)
                H = ROPE // 2
                sin = rope_t[:, 4].unsqueeze(2).broadcast_to([P, TT, 4, H])
                cos = rope_t[:, 5].unsqueeze(2).broadcast_to([P, TT, 4, H])
                x1, x2 = buf[:, :, :, 0:H], buf[:, :, :, H:2 * H]
                r = [rot[:, k].rearrange("p (t s) h -> p t s h", t=TT) for k in range(4)]
                G.tensor_tensor(r[0], x1, cos, ALU.mult)
                G.tensor_tensor(r[1], x2, sin, ALU.mult)
                G.tensor_tensor(r[2], x2, cos, ALU.mult)
                G.tensor_tensor(r[3], x1, sin, ALU.mult).then_inc(turned, 1)
                pool.wait_ge(turned, n)
                G.tensor_tensor(x1, r[0], r[1], ALU.subtract)
                G.tensor_tensor(x2, r[2], r[3], ALU.add).then_inc(roped, 1)

            def diff(n):
                turn(qn, 0, q_normed, q_scaled, q_turned, q_roped, n)
                pool.wait_ge(q_roped, n)
                turn(kn, 1, k_normed, k_scaled, k_turned, k_roped, n)
                pool.wait_ge(k_roped, n)

            gla_tail(1)
            with pool.Fori(2, GLA_HEADS + 1) as n:
                gla_tail(n)
            pool.wait_ge(small_landed, 17 * 16)
            pool.wait_ge(rope_ready, 2)
            with pool.Fori(1, DIFF_PAIRS + 1) as n:
                diff(n)

        @block.tensor
        def _(pe):
            mm = nc.tensor.matmul

            def features(first, j, acc, a):
                slot, k0 = j % 4, 4 * (j % HALF)
                pe.wait_ge(lo_ready, first + j + 1)
                hi, lo = (w[:, slot].rearrange("p k (a n) -> p (k a) n", n=HB) for w in (whi, wlo))
                for k in range(4):
                    kt = k0 + k
                    for f in range(2):
                        dst = acc[:, f * NB:(f + 1) * NB]
                        mm(dst, hi[:, k, f * P:(f + 1) * P], a[:, kt].rearrange("p s t -> p (s t)"),
                           start=(kt == 0), stop=False, skip_group_check=True)
                        last = mm(dst[:, 0:T], lo[:, k, f * P:(f + 1) * P], a[:, kt, 0], start=False,
                                  stop=(kt == KT - 1), skip_group_check=True)
                last.then_inc(pieces_used, 1)

            def tokens(first, j, k0, n_kt, acc, a_hi, a_lo):
                slot = j % 4
                pe.wait_ge(lo_ready, first + j + 1)
                for k in range(PIECE_KT):
                    kt = k0 + k
                    for t in range(TT):
                        dst = acc[:, t * NB:(t + 1) * NB]
                        hi, lo = a_hi[:, kt, t * P:(t + 1) * P], a_lo[:, kt, t * P:(t + 1) * P]
                        mm(dst, hi, whi[:, slot, k], start=(kt == 0), stop=False)
                        mm(dst, hi, wlo[:, slot, k], start=False, stop=False)
                        last = mm(dst, lo, whi[:, slot, k], start=False, stop=(kt == n_kt - 1))
                last.then_inc(pieces_used, 1)

            def transpose(dst, src, n=P):
                return nc.tensor.transpose(dst, src, ident[0:n, 0:n])

            def norm_transposes(src, pair, n):
                pe.wait_ge(normed_act, 4 * (n - 1) + pair // 2 + 1)
                pe.wait_ge(normed_dve, 4 * (n - 1) + pair // 2 + 1)
                if pair >= 6:
                    pe.wait_ge(norm_lo, 8 * (n - 1) + pair - 5)
                for k in range(2):
                    for t in range(TT):
                        col = (2 * pair + k) * P
                        last = transpose(stage(pair)[:, k * T + t * P:k * T + (t + 1) * P], src[:, t, col:col + P])
                last.then_inc(norm_T, 1)

            def normed_block(src, j, n):
                if j == 0:
                    for pair in range(6):
                        norm_transposes(src, pair, n)
                if j == 1:
                    for pair in (6, 7):
                        norm_transposes(src, pair, n)
                if j < HALF:
                    pe.wait_ge(norm_lo, 8 * (n - 1) + 2 * j + 2)

            def decay_inputs(j):
                if j == 8:
                    pe.wait_ge(wlr_lo_ready, 1)
                    for k in range(KT):
                        mm(mix[:, 0:T], wlr_hi[:, k], hT[:, k, 0], start=(k == 0), stop=False)
                        mm(mix[:, 0:T], wlr_hi[:, k], hT[:, k, 1], start=False, stop=False)
                        last = mm(mix[:, 0:T], wlr_lo[:, k], hT[:, k, 0], start=False, stop=(k == KT - 1))
                    last.then_inc(lr_done, 1)
                if j == 10:
                    pe.wait_ge(lr_ready, 1)
                    for k in range(8):
                        last = mm((acc_c, mix)[k // 4][:, (k % 4) * T:(k % 4 + 1) * T], wup[0:GLA_RANK, k * P:(k + 1) * P],
                                  lrT[0:GLA_RANK, :], start=True, stop=True)
                        if k % 4 == 3:
                            last.then_inc(gk_done, 1)

            def gla(h, tail):
                first = GLA_N * h + GLA0
                first_head = tail is None
                at_A, at_o = (17, 20) if first_head else (13, 18)
                for j in range(GLA_N):
                    if tail is not None:
                        gla_tail(j, tail)
                    if first_head:
                        normed_block(normed, j, 1)
                        decay_inputs(j)
                        if j == 2 * BLOCK:
                            pe.wait_ge(gkx_ready, 1)
                    if j == at_A:
                        pe.wait_ge(operands_ready, h + 1)
                        if not first_head:
                            pe.wait_ge(glaT_lo_ready, h)
                        for dst, key, query in (
                                (0, k_inv[:, :, 0:P], q_dec[:, :, 0:C]), (C, k_mix[:, :, 0:P], q_dec[:, :, C:2 * C]),
                                (2 * C, k_inv[:, :, P:T], q_dec[:, :, 2 * C:3 * C]),
                                (3 * C, k_mix[:, :, P:T], q_dec[:, :, 3 * C:4 * C]),
                                (4 * C, k_tile[:, :, :], q_dec[:, :, 2 * C:3 * C]), (5 * C, k_tile[:, :, :], q_3[:, :, :])):
                            for f in range(2):
                                last = mm(mix[:, dst:dst + C], key[:, f], query[:, f], start=(f == 0), stop=(f == 1))
                        last.then_inc(A_done, 1)
                    if j == at_o:
                        pe.wait_ge(AT_ready, h + 1)
                        pe.wait_ge(gv_ready, h + 1)
                        mm(mix[:, NB:2 * NB], AT[:, 0], g_v[:, 0], start=True, stop=True)
                        mm(mix[:, 0:NB], AT[:, 1], g_v[:, 1], start=True, stop=False)
                        mm(mix[:, 0:NB], AT[:, 2], g_v[:, 0], start=False, stop=True).then_inc(go_done, 1)
                    if j < HALF:
                        if j == 0 and not first_head:
                            pe.wait_ge(gv_ready, h)
                        features(first, j, acc_a, hT)
                    elif j < BLOCK:
                        if j == HALF and not first_head:
                            pe.wait_ge(k_summed, h)
                        features(first, j, acc_b, hT)
                    elif j < 2 * BLOCK:
                        if j == BLOCK:
                            pe.wait_ge(q_summed, h + 1)
                        tokens(first, j, 2 * (j - BLOCK), KT, acc_a, hT[:, :, 0], hT[:, :, 1])
                    else:
                        if j == 2 * BLOCK and not first_head:
                            pe.wait_ge(gout_silu, h)
                        tokens(first, j, 2 * (j - 2 * BLOCK), KT, acc_c, hT[:, :, 0], hT[:, :, 1])

            def gla_tail(j, n):
                if j == 9:
                    pe.wait_ge(og_ready, n)
                    for f in range(4):
                        for t in range(TT):
                            last = transpose(mix[:, f * T + t * P:f * T + (t + 1) * P], g_og[:, t, f * P:(f + 1) * P])
                    last.then_inc(og_T, 1)

            def head_transposes(src):
                for s in range(4):
                    for t in range(TT):
                        last = transpose(mix[:, s * T + t * P:s * T + (t + 1) * P], src[:, t, s])
                return last

            def diff(i, tail, gtail):
                first = DIFF_N * i + DIFF0
                for j in range(DIFF_N):
                    if tail is not None:
                        diff_tail(j, tail, True, i)
                    if gtail is not None:
                        gla_tail(j, gtail)
                    if j == 17:
                        pe.wait_ge(q_roped, i + 1)
                        if tail is not None:
                            pe.wait_ge(do_normed, i)
                        else:
                            pe.wait_ge(glaT_lo_ready, GLA_HEADS)
                        head_transposes(qn).then_inc(q_T, 1)
                    if j == 22:
                        pe.wait_ge(k_roped, i + 1)
                        pe.wait_ge(qT_ready, i + 1)
                        if tail is not None:
                            pe.wait_ge(diffT_lo_ready, i)
                        head_transposes(kn).then_inc(k_T, 1)
                    b = j // BLOCK
                    if j == 0:
                        pe.wait_ge(gv_ready if gtail is not None else q_normed, GLA_HEADS if gtail is not None else i)
                    if j == BLOCK:
                        pe.wait_ge(k_summed if gtail is not None else k_normed, GLA_HEADS if gtail is not None else i)
                    if j == 2 * BLOCK:
                        pe.wait_ge(gout_silu if gtail is not None else dv_ready, GLA_HEADS if gtail is not None else i)
                    tokens(first, j, 2 * (j - b * BLOCK), KT, (acc_a, acc_b, acc_c)[b], hT[:, :, 0], hT[:, :, 1])

            def diff_tail(j, n, more, i):
                if j in (2, 5):
                    half = (2, 5).index(j)
                    if half == 0:
                        pe.wait_ge(qT_ready, n)
                        pe.wait_ge(kT_ready, n)
                    else:
                        pe.wait_ge(max_found[0], n)
                    for s in (2 * half, 2 * half + 1):
                        ps = mix[:, (s % 2) * NB:(s % 2) * NB + 3 * P]
                        mm(ps[:, 0:P], qT[:, s, 0:P], kT[:, s, 0:P], start=True, stop=True)
                        last = mm(ps[:, P:3 * P], qT[:, s, P:T], kT[:, s, :], start=True, stop=True)
                    last.then_inc(scores_done[half], 1)
                if j == 11:
                    pe.wait_ge(att_ready, n)
                    for hh in range(2):
                        for k in range(3):
                            last = transpose(mix[:, hh * NB + k * P:hh * NB + (k + 1) * P], att[:, hh, k * P:(k + 1) * P])
                    last.then_inc(att_T, 1)
                if j == 13:
                    pe.wait_ge(attT_ready, n)
                    pe.wait_ge(dv_ready, n)
                    for hh in range(2):
                        v = d_v[:, :, hh * T:(hh + 1) * T]
                        mm(mix[:, hh * NB:hh * NB + T], attT[:, hh, 0:P], v[:, 0], start=True, stop=True)
                        mm(mix[:, hh * NB + T:hh * NB + 2 * T], attT[:, hh, P:2 * P], v[:, 0], start=True, stop=False)
                        last = mm(mix[:, hh * NB + T:hh * NB + 2 * T], attT[:, hh, 2 * P:3 * P], v[:, 1],
                                  start=False, stop=True)
                    last.then_inc(pv_done, 1)
                if j == 19:
                    pe.wait_ge(do_normed, n)
                    if more:
                        pe.wait_ge(qT_ready, i + 1)
                    for f in range(4):
                        for t in range(TT):
                            last = transpose(mix[:, f * T + t * P:f * T + (t + 1) * P], d_on[:, t, f * P:(f + 1) * P])
                    last.then_inc(do_T, 1)

            def branch(g, tail, dtail):
                first = BR_N * g + BR0
                for j in range(BR_N):
                    if dtail is not None:
                        diff_tail(j, dtail, False, None)
                    half = j // HALF
                    if j % HALF == 0:
                        if dtail is not None and half < 2:
                            pe.wait_ge((q_normed, k_normed)[half], DIFF_PAIRS)
                        else:
                            pe.wait_ge(halves_summed, BR_HALVES * g + (half - 1))
                    if j == 3 * BLOCK and dtail is not None:
                        pe.wait_ge(diffT_lo_ready, DIFF_PAIRS)
                    features(first, j, (acc_a, acc_b)[half % 2], (hT, hT, glaT, diffT)[j // BLOCK])

            pe.wait_ge(consts_ready, 1)
            pe.wait_ge(small_landed, 17 * 16)
            transpose(mix[:, 0:90], rows[0:90, 0, :], 90)
            transpose(mix[:, 90:178], rows[0:88, 1, :], 88)
            transpose(mix[:, 178:222], rows[0:44, 2, :], 44).then_inc(cols_T, 1)
            pe.wait_ge(cols_ready, 1)

            gla(0, None)
            with pe.Fori(1, GLA_HEADS) as h:
                gla(h, h)
            diff(0, None, GLA_HEADS)
            with pe.Fori(1, DIFF_PAIRS) as i:
                diff(i, i, None)
            branch(0, None, DIFF_PAIRS)
            with pe.Fori(1, GROUPS) as g:
                branch(g, g, None)
            for j in range(4 * BLOCK):
                b = j // BLOCK
                if j in (0, BLOCK):
                    pe.wait_ge(halves_summed, FFN_HALF0 - 1 + b)
                if j == 6:
                    pe.wait_ge(mixT_lo_ready, GROUPS)
                if j in (2 * BLOCK, 3 * BLOCK):
                    pe.wait_ge(x1_ready, b - 1)
                tokens(OUT0, j, 2 * (j - b * BLOCK), KT, (acc_a, acc_b)[b % 2], mixT_hi, mixT_lo)
            for j in range(2 * BLOCK):
                normed_block(xn2, j, 2)
                if j in (2 * HALF, 3 * HALF):
                    pe.wait_ge(halves_summed, FFN_HALF0 + j // HALF - 1)
                features(FFN0, j, (acc_a, acc_b)[(j // HALF) % 2], hT)

            def down(first, j, q_first, n, a_hi, a_lo):
                q, k0 = (j - q_first) // 2, 2 * (j % 2)
                if j == q_first:
                    pe.wait_ge(hid_lo_ready, n)
                if j % 2 == 0 and (q >= 2 or a_hi is last_hi):
                    pe.wait_ge(down_added, 4 * n - 5 + q)
                tokens(first, j, k0, 4, (acc_c, mix)[q % 2], a_hi, a_lo)

            def up(first, j, half, f):
                if j % HALF == 0:
                    pe.wait_ge(halves_summed, 4 * f + (FFN_HALF0 + half - 1))
                features(first, j, (acc_a, acc_b)[half % 2], hT)

            with pe.Fori(1, LAST) as f:
                for j in range(FFN_N):
                    if j < BLOCK:
                        up(ffn_base(f), j, j // HALF, f)
                    elif j < 2 * BLOCK:
                        down(ffn_base(f), j, BLOCK, f, hid_hi, hid_lo)
                    else:
                        up(ffn_base(f), j, j // HALF - 2, f)
            for j in range(FFN_N):
                if j < 2 * BLOCK:
                    up(ffn_base(LAST), j, j // HALF, LAST)
                else:
                    down(ffn_base(LAST), j, 2 * BLOCK, LAST, hid_hi, hid_lo)
            for j in range(BLOCK):
                down(END0, j, 0, FFN_GROUPS, last_hi, last_lo)


_INS = ["x", "positions", "norm1_g", "w_in", "w_gk_up", "b_gk", "gla_norm_g", "q_norm_g", "k_norm_g",
        "lambda_q1", "lambda_k1", "lambda_q2", "lambda_k2", "subln_g", "w_branch", "w_out", "norm2_g",
        "w_ffn_up", "conv_w", "conv_b", "w_ffn_down"]


def kernel(**inputs):
    import numpy as _np
    import concourse.bacc as _bacc
    from concourse import mybir as _mybir
    from concourse.bass_utils import run_bass_kernel_spmd as _run

    nc = _bacc.Bacc("TRN2", target_bir_lowering=False, num_devices=1)
    arrays, args = {}, []
    for name in _INS:
        a = _np.ascontiguousarray(inputs[name])
        arrays[f"in_{name}_dram"] = a
        args.append(nc.dram_tensor(f"in_{name}_dram", a.shape, _mybir.dt.from_np(a.dtype), kind="ExternalInput").ap())
    out = nc.dram_tensor("out_0_dram", (1, T, D), F32, kind="ExternalOutput").ap()
    hybrid_block_kernel(nc, *args, out)
    r = _run(nc, [arrays], core_ids=[0])
    return r.results[0]["out_0_dram"]
```

```python
import math
from contextlib import ExitStack

import numpy as np

import concourse.bass as bass
from concourse import mybir

F32 = mybir.dt.float32
F32R = mybir.dt.float32r
I32 = mybir.dt.int32
U32 = mybir.dt.uint32
ALU = mybir.AluOpType
ACT = mybir.ActivationFunctionType
AX = mybir.AxisListType

P = 128
T = 256
TT = T // P
D = 2048
KT = D // P
NB = 512
CHUNK_KT = 4
PIECE_KT = 2
HB = NB // 2

GLA_HEADS = 4
GLA_DK = 256
GLA_DV = 512
GLA_RANK = 16
GLA_NORMALIZER = 16.0
C = 64
DIFF_PAIRS = 4
DH = 128
ROPE = 32
ROPE_THETA = 500000.0
FFN = 5632
FFN_GROUPS = FFN // NB
GROUPS = D // NB
EPS = 1e-6
SUBLN_EPS = 1e-5
LAMBDA_INIT = 0.8 - 0.6 * math.exp(-0.3 * 0)

C_GV = 2 * GLA_HEADS * GLA_DK
C_LR = C_GV + GLA_HEADS * GLA_DV
C_GOUT = C_LR + GLA_RANK
C_DQ = C_GOUT + D
C_DK = C_DQ + D
C_DV = C_DK + D
C_MG = C_DV + D
C_MD = C_MG + D

BLOCK = 8
HALF = BLOCK // 2
GLA0, GLA_N = 0, 3 * BLOCK
DIFF0, DIFF_N = GLA0 + GLA_HEADS * GLA_N, 3 * BLOCK
BR0, BR_N = DIFF0 + DIFF_PAIRS * DIFF_N, 4 * BLOCK
OUT0 = BR0 + GROUPS * BR_N
FFN0 = OUT0 + 4 * BLOCK
FFN_N = 3 * BLOCK
LAST = FFN_GROUPS - 1
END0 = FFN0 + FFN_GROUPS * FFN_N - BLOCK


BR_HALVES = 8
FFN_HALF0 = GROUPS * BR_HALVES


def ffn_base(f):
    return f * FFN_N + (FFN0 - BLOCK)


def two_pi_pieces(n):
    left, out = 2.0 * math.pi, []
    for _ in range(n - 1):
        step = 2.0 ** (math.floor(math.log2(left)) - 6)
        out.append(math.floor(left / step) * step)
        left -= out[-1]
    return out + [float(np.float32(left))]


TWO_PI = two_pi_pieces(5)
ROUND = 1.5 * 2.0 ** 23


def hybrid_block_kernel(nc, x, positions, norm1_g, w_in, w_gk_up, b_gk, gla_norm_g, q_norm_g, k_norm_g,
                        lambda_q1, lambda_k1, lambda_q2, lambda_k2, subln_g, w_branch, w_out,
                        norm2_g, w_ffn_up, conv_w, conv_b, w_ffn_down, out):
    with ExitStack() as ctx:
        KB = 1024
        base = -(-nc.sbuf_base // 64) * 64

        def at(name, offset, shape, dt=F32):
            return nc.alloc_sbuf_tensor_at(name, [P] + shape, dt, offset=base + int(offset))

        def sem(name):
            return ctx.enter_context(nc.semaphore(name))

        raw = at("raw", 0, [4, CHUNK_KT, NB])
        whi = at("whi", 32 * KB, [4, PIECE_KT, NB], F32R)
        wlo = at("wlo", 48 * KB, [4, PIECE_KT, NB], F32R)
        hT = at("hT", 64 * KB, [KT, 2, T], F32R)
        glaT = at("glaT", 96 * KB, [KT, 2, T], F32R)
        resid = at("resid", 96 * KB, [TT, D])
        normed = at("normed", 112 * KB, [TT, D])
        diffT = at("diffT", 128 * KB, [KT, 2, T], F32R)
        mixT_hi = at("mixT_hi", 160 * KB, [KT, T], F32R)
        mixT_lo = at("mixT_lo", 176 * KB, [KT, T], F32R)
        wlr_raw = at("wlr_raw", 128 * KB, [KT, P])
        wlr_hi = at("wlr_hi", 136 * KB, [KT, GLA_RANK], F32R)
        wlr_lo = at("wlr_lo", 137 * KB, [KT, GLA_RANK], F32R)
        gkx = at("gkx", 152 * KB, [8, T])
        g_exp = at("g_exp", 128 * KB, [TT * NB])
        g_silu = at("g_silu", 132 * KB, [TT, NB])
        g_on = at("g_on", 136 * KB, [TT, NB])
        g_og = at("g_og", 140 * KB, [TT, NB])
        gv_hi = at("gv_hi", 144 * KB, [TT, NB], F32R)
        gv_lo = at("gv_lo", 148 * KB, [TT, NB], F32R)
        q_sum = at("q_sum", 148 * KB, [2, T])
        k_sum = at("k_sum", 150 * KB, [2, T])
        o = 160 * KB
        dec = at("dec", o, [2, T])
        gmin = at("gmin", o + 2 * KB, [2, T])
        cum = at("cum", o + 4 * KB, [2, T])
        e_pos = at("e_pos", o + 6 * KB, [2, T])
        e_neg = at("e_neg", o + 8 * KB, [2, T])
        e_tail = at("e_tail", o + 10 * KB, [2, 2, C])
        e_tile = at("e_tile", o + 11 * KB, [2, P])
        e_q3 = at("e_q3", o + 12 * KB, [2, C])
        q_dec = at("q_dec", o + 12.5 * KB, [2, T])
        k_inv = at("k_inv", o + 14.5 * KB, [2, T])
        k_mix = at("k_mix", o + 16.5 * KB, [2, T])
        k_tile = at("k_tile", o + 18.5 * KB, [2, P])
        q_3 = at("q_3", o + 19.5 * KB, [2, C])
        AT = at("AT", o + 20 * KB, [3, P])
        AT_hi = at("AT_hi", o + 2 * KB, [3, P], F32R)
        AT_lo = at("AT_lo", o, [3, P], F32R)
        reset = at("reset", o + 21.5 * KB, [T])
        rows = at("rows", o + 22.5 * KB, [3, P])
        wup = at("wup", o + 24 * KB, [GLA_HEADS * GLA_DK])
        lam_v = at("lam_v", o + 28 * KB, [4, P])
        qk_g = at("qk_g", o + 30 * KB, [2, P])
        lam_p = at("lam_p", o + 31 * KB, [2, P])
        sq = at("sq", o, [8, DH])
        rot = at("rot", o + 4 * KB, [4, 8, ROPE // 2])
        qT = at("qT", o + 6 * KB, [4, T])
        kT = at("kT", o + 10 * KB, [4, T])
        dv_hi = at("dv_hi", o + 14 * KB, [TT, NB], F32R)
        dv_lo = at("dv_lo", o + 18 * KB, [TT, NB], F32R)
        prob = at("prob", o + 18 * KB, [4, 3 * P])
        att = at("att", o + 24 * KB, [2, 3 * P])
        attT_hi = at("attT_hi", o + 27 * KB, [2, 3 * P], F32R)
        attT_lo = at("attT_lo", o + 24 * KB, [2, 3 * P], F32R)
        o = 192 * KB
        lrT = at("lrT", o, [T])
        qn = at("qn", o, [TT, 4, DH])
        kn = at("kn", o + 4 * KB, [TT, 4, DH])
        gate_g = at("gate_g", o, [4, T])
        gate_d = at("gate_d", o + 4 * KB, [4, T])
        d_on = at("d_on", o + 8 * KB, [TT, NB])
        y_sum = at("y_sum", o + 8 * KB, [2, 2, T])
        o += 12 * KB
        ident = at("ident", o, [P])
        keep = at("keep", o + 512, [P])
        causal = at("causal", o + 1024, [T])
        cols = at("cols", o + 2048, [224])
        rope_t = at("rope_t", o + 2048 + 896, [6, TT, ROPE // 2])
        small = at("small", o + 2048 + 896 + 768, [44])
        assert base + o + 2048 + 896 + 768 + 176 <= nc.sbuf_usable_end
        rs_diag = at("rs_diag", 132 * KB, [TT, P])
        rs_row = at("rs_row", 133 * KB, [T])
        ones = at("ones", 134 * KB, [P])
        up_sum = at("up_sum", 112 * KB, [4, T])
        conv = at("conv", 144 * KB, [4, T])
        hid_hi = at("hid_hi", 148 * KB, [4, T], F32R)
        hid_lo = at("hid_lo", 152 * KB, [4, T], F32R)
        last_hi = at("last_hi", 156 * KB, [4, T], F32R)
        last_lo = at("last_lo", 128 * KB, [4, T], F32R)

        V_N1, V_N2, V_BGK, V_GLA, V_SUB, V_CW0 = 0, 16, 32, 40, 44, 46
        V_CW1, V_CW2, V_CB = 90, 134, 178
        ss_x, rs_x = small[:, 0:2], small[:, 2:4]
        eps_c, sub_eps_c = small[:, 4:5], small[:, 5:6]
        one_c, zero_c = small[:, 6:7], small[:, 7:8]
        neg_lam = small[:, 8:9]
        ss_half = small[:, 37:39]
        lam2 = small[:, 9:11]
        pos_i = small[:, 11:13]
        inv_f = small[:, 13:29]
        ss_out = small[:, 29:37]
        tiny = at("tiny", 31.5 * KB + 160 * KB, [96])
        bl = tiny[:, 0:8]
        bl01 = tiny[:, 8:10]
        g_ss, g_rs = tiny[:, 10:12], tiny[:, 12:14]
        dq_ss, dq_rs = tiny[:, 14:22], tiny[:, 22:30]
        dk_ss, dk_rs = tiny[:, 30:38], tiny[:, 38:46]
        s_max, s_nmax = tiny[:, 46:54], tiny[:, 54:62]
        p_sum, p_inv = tiny[:, 62:70], tiny[:, 70:78]
        p_lam = tiny[:, 78:82]
        o_ss, o_rs = tiny[:, 82:86], tiny[:, 86:90]

        acc_a, acc_b, acc_c, mix = (ctx.enter_context(nc.psum_tensor(n, [P, 2 * NB], F32))
                                    for n in ("acc_a", "acc_b", "acc_c", "mix"))

        def stage(pair):
            b = pair % 6
            return (acc_b, acc_c, mix)[b // 2][:, (b % 2) * NB:(b % 2 + 1) * NB]

        def stage2(pair):
            b = pair % 4
            return (acc_c, mix)[b // 2][:, (b % 2) * NB:(b % 2 + 1) * NB]

        raw_landed = [sem(f"raw_landed{i}") for i in range(4)]
        hi_ready = sem("hi_ready")
        lo_ready = sem("lo_ready")
        pieces_used = sem("pieces_used")
        x_landed = [sem("x_landed0"), sem("x_landed1")]
        wlr_landed, small_landed, rows_landed = sem("wlr_landed"), sem("small_landed"), sem("rows_landed")
        resid_landed = sem("resid_landed")
        out_stored = sem("out_stored")
        consts_ready, const_step, ones_ready = sem("consts_ready"), sem("const_step"), sem("ones_ready")
        cols_T, cols_ready = sem("cols_T"), sem("cols_ready")
        scale_ready = sem("scale_ready")
        wlr_hi_ready, wlr_lo_ready = sem("wlr_hi_ready"), sem("wlr_lo_ready")
        sumsq_act, sumsq_dve, sumsq_half = sem("sumsq_act"), sem("sumsq_dve"), sem("sumsq_half")
        norm_ln, norm_rs = sem("norm_ln"), sem("norm_rs")
        normed_act, normed_dve = sem("normed_act"), sem("normed_dve")
        norm_T, norm_hi, norm_lo = sem("norm_T"), sem("norm_hi"), sem("norm_lo")
        lr_done, lr_ready, gk_done, gkx_ready = sem("lr_done"), sem("lr_ready"), sem("gk_done"), sem("gkx_ready")
        rope_step, rope_arg, rope_sin, rope_ready = sem("rope_step"), sem("rope_arg"), sem("rope_sin"), sem("rope_ready")
        lam_dot, lam_exp, lam_ready = sem("lam_dot"), sem("lam_exp"), sem("lam_ready")
        gk_abs, gk_exp, gk_ln = sem("gk_abs"), sem("gk_exp"), sem("gk_ln")
        gk_min, gk_gate, cum_ready, bl_ready = sem("gk_min"), sem("gk_gate"), sem("cum_ready"), sem("bl_ready")
        bl_scaled = sem("bl_scaled")
        e_ready, operands_ready, A_done = sem("e_ready"), sem("operands_ready"), sem("A_done")
        AT_ready, AT_hi_ready, AT_lo_ready = sem("AT_ready"), sem("AT_hi_ready"), sem("AT_lo_ready")
        gv_hi_ready, gv_lo_ready, go_done = sem("gv_hi_ready"), sem("gv_lo_ready"), sem("go_done")
        go_sumsq, go_ln, go_rs, go_normed = sem("go_sumsq"), sem("go_ln"), sem("go_rs"), sem("go_normed")
        gout_exp, gout_one, gout_inv, gout_silu = sem("gout_exp"), sem("gout_one"), sem("gout_inv"), sem("gout_silu")
        og_ready, og_T, glaT_hi_ready, glaT_lo_ready = sem("og_ready"), sem("og_T"), sem("glaT_hi_ready"), sem("glaT_lo_ready")
        q_sq, q_ss, q_ln, q_rs, q_normed = (sem("q_" + n) for n in ("sq", "ss", "ln", "rs", "normed"))
        k_sq, k_ss, k_ln, k_rs, k_normed = (sem("k_" + n) for n in ("sq", "ss", "ln", "rs", "normed"))
        q_scaled, q_turned, q_roped = sem("q_scaled"), sem("q_turned"), sem("q_roped")
        k_scaled, k_turned, k_roped = sem("k_scaled"), sem("k_turned"), sem("k_roped")
        q_T, k_T, qT_ready, kT_ready, dv_hi_ready = sem("q_T"), sem("k_T"), sem("qT_ready"), sem("kT_ready"), sem("dv_hi_ready")
        dv_lo_ready, attT_lo_ready = sem("dv_lo_ready"), sem("attT_lo_ready")
        scores_done = [sem("scores01_done"), sem("scores23_done")]
        max_found = [sem("max01_found"), sem("max23_found")]
        max_ready = [sem("max01_ready"), sem("max23_ready")]
        exp_ready = [sem("exp01_ready"), sem("exp23_ready")]
        sums_inv, sums_lam, att_second, att_ready = sem("sums_inv"), sem("sums_lam"), sem("att_second"), sem("att_ready")
        att_T, attT_hi_ready, pv_done = sem("att_T"), sem("attT_hi_ready"), sem("pv_done")
        do_sumsq, do_ln, do_rs, do_normed = sem("do_sumsq"), sem("do_ln"), sem("do_rs"), sem("do_normed")
        do_T, diffT_hi_ready, diffT_lo_ready = sem("do_T"), sem("diffT_hi_ready"), sem("diffT_lo_ready")
        q_summed, k_summed = sem("q_summed"), sem("k_summed")
        halves_summed = sem("halves_summed")
        gates_ready, y_gated, mixed_ready = sem("gates_ready"), sem("y_gated"), sem("mixed_ready")
        mixT_hi_ready, mixT_lo_ready = sem("mixT_hi_ready"), sem("mixT_lo_ready")
        x1_ready, x1_sumsq = sem("x1_ready"), sem("x1_sumsq")
        diag_ready, rs_spread, rs_row_ready = sem("diag_ready"), sem("rs_spread"), sem("rs_row_ready")
        halves_scaled = sem("halves_scaled")
        last_tile_done = sem("last_tile_done")
        conv_first, conv_second, conv_ready, conv_silu = sem("conv_first"), sem("conv_second"), sem("conv_ready"), sem("conv_silu")
        hid_ready, hid_hi_ready, hid_lo_ready, down_added = sem("hid_ready"), sem("hid_hi_ready"), sem("hid_lo_ready"), sem("down_added")

        x_v = x[0].rearrange("(t p) n -> p t n", p=P)
        out_v = out[0].rearrange("(t p) n -> p t n", p=P)
        w_in_v = w_in[0].rearrange("(k p) n -> p k n", p=P)
        w_br_v = w_branch[0].rearrange("(k p) n -> p k n", p=P)
        w_out_v = w_out[0].rearrange("(k p) n -> p k n", p=P)
        w_up_v = w_ffn_up[0].rearrange("(k p) n -> p k n", p=P)
        w_down_v = w_ffn_down[0].rearrange("(g k p) n -> p g k n", k=4, p=P)

        block = ctx.enter_context(nc.Block())

        @block.sync
        def _(sp):
            def load(first, j, src, half=False):
                slot = j % 4
                if isinstance(first, int):
                    if first // 2 + j >= 4:
                        sp.wait_ge(lo_ready, first + 2 * j - 6)
                else:
                    split = sp.snap(sp.to_reg(first + 2 * j - 6))
                    sp.wait_ge(x_landed[0], 16)
                    sp.wait_ge(lo_ready, split)
                dst = raw[:, slot]
                if half:
                    dst = dst.rearrange("p k (a n) -> p (k a) n", n=HB)
                sp.dma_start(dst, src).then_inc(raw_landed[slot], 16)

            def load_block(first, b, view, col, k0=0):
                for q in range(4):
                    load(first, 4 * b + q, view[:, k0 + 4 * q:k0 + 4 * q + 4, bass.ds(col, NB)])

            def load_half(first, half, view, col, k0=0):
                for c in range(2):
                    load(first, 2 * half + c, view[:, k0 + 8 * c:k0 + 8 * c + 8, bass.ds(col, HB)], True)

            def load_features(first, b, view, col, k0=0):
                for i in range(2):
                    load_half(first, 2 * b + i, view, col + i * HB, k0)

            def gla(h):
                first = GLA_N * h + GLA0
                load_half(first, 0, w_in_v, h * GLA_DK)
                load_half(first, 1, w_in_v, h * GLA_DK + GLA_HEADS * GLA_DK)
                if isinstance(h, int):
                    sp.dma_start(wlr_raw[:, :, :], w_in_v[:, :, C_LR:C_LR + P]).then_inc(wlr_landed, 16)
                    sp.dma_start(wup[0:GLA_RANK, :], w_gk_up[0]).then_inc(small_landed, 16)
                    sp.dma_start(qk_g[:, 0], q_norm_g.broadcast_to([P, P])).then_inc(small_landed, 16)
                    sp.dma_start(qk_g[:, 1], k_norm_g.broadcast_to([P, P])).then_inc(small_landed, 16)
                    for k, v in enumerate((lambda_q1, lambda_k1, lambda_q2, lambda_k2)):
                        sp.dma_start(lam_v[:, k], v.broadcast_to([P, P])).then_inc(small_landed, 16)
                    sp.dma_start(pos_i.bitcast(I32), positions[0].rearrange("(t p) -> p t", p=P),
                                 allow_slow_non_contiguous=True).then_inc(small_landed, 16)
                load_block(first, 1, w_in_v, h * NB + C_GV)
                load_block(first, 2, w_in_v, h * NB + C_GOUT)

            def diff(i):
                first = DIFF_N * i + DIFF0
                load_block(first, 0, w_in_v, i * NB + C_DQ)
                load_block(first, 1, w_in_v, i * NB + C_DK)
                load_block(first, 2, w_in_v, i * NB + C_DV)

            def branch(g):
                first = BR_N * g + BR0
                load_features(first, 0, w_in_v, g * NB + C_MG)
                load_features(first, 1, w_in_v, g * NB + C_MD)
                load_features(first, 2, w_br_v, g * NB)
                load_features(first, 3, w_br_v, g * NB, KT)

            def down(first, b, f):
                for q in range(4):
                    load(first, 4 * b + q, w_down_v[:, bass.ds(f, 1), :, q * NB:(q + 1) * NB].rearrange("p g k n -> p (g k) n"))

            sp.dma_start(resid[:, 0], x_v[:, 0]).then_inc(x_landed[0], 16)
            for half in range(2):
                c = slice(half * D // 2, (half + 1) * D // 2)
                sp.dma_start(resid[:, 1, c], x_v[:, 1, c]).then_inc(x_landed[1], 16)
            for r, c0, v in ((0, V_N1, norm1_g), (0, V_N2, norm2_g), (0, V_BGK, b_gk), (0, V_GLA, gla_norm_g),
                             (0, V_SUB, subln_g), (0, V_CW0, conv_w[:, 0]), (1, V_CW1 - 90, conv_w[:, 1]),
                             (1, V_CW2 - 90, conv_w[:, 2]), (2, 0, conv_b)):
                n = v.shape[-1] // P
                sp.dma_start(rows[c0:c0 + n, r, :], v[0].rearrange("(a b) -> a b", b=P)).then_inc(rows_landed, 16)
            gla(0)
            with sp.Fori(1, GLA_HEADS) as h:
                gla(h)
            with sp.Fori(0, DIFF_PAIRS) as i:
                diff(i)
            with sp.Fori(0, GROUPS) as g:
                branch(g)
            load_block(OUT0, 0, w_out_v, 0)
            sp.wait_ge(pieces_used, OUT0 - BLOCK)
            sp.dma_start(resid[:, :, :], x_v).then_inc(resid_landed, 16)
            for b in range(1, 4):
                load_block(OUT0, b, w_out_v, b * NB)
            load_features(FFN0, 0, w_up_v, 0)
            load_features(FFN0, 1, w_up_v, FFN)
            with sp.Fori(1, LAST) as f:
                load_features(ffn_base(f), 0, w_up_v, f * NB)
                down(ffn_base(f), 1, f - 1)
                load_features(ffn_base(f), 2, w_up_v, f * NB + FFN)
            load_features(ffn_base(LAST), 0, w_up_v, LAST * NB)
            load_features(ffn_base(LAST), 1, w_up_v, LAST * NB + FFN)
            down(ffn_base(LAST), 2, LAST - 1)
            down(END0, 0, FFN_GROUPS - 1)
            for q in range(3):
                sp.wait_ge(down_added, 4 * (FFN_GROUPS - 1) + q + 1)
                sp.dma_start(out_v[:, :, q * NB:(q + 1) * NB], resid[:, :, q * NB:(q + 1) * NB]).then_inc(out_stored, 16)
            for t in range(TT):
                sp.wait_ge(down_added, 4 * FFN_GROUPS + t)
                sp.dma_start(out_v[:, t, 3 * NB:4 * NB], resid[:, t, 3 * NB:4 * NB]).then_inc(out_stored, 16)
            sp.wait_ge(out_stored, 5 * 16)

        @block.scalar
        def _(act):
            def fn(o_, i_, f, **kw):
                return nc.scalar.activation(o_, i_, f, **kw)

            def split_hi(first, j):
                slot = j % 4
                if j % 2 == 0:
                    act.wait_ge(raw_landed[(j // 2) % 4], (first + 8 * (j // 8) + 8) * 2)
                if not (isinstance(first, int) and first + j < 4):
                    act.wait_ge(pieces_used, first + j - 3)
                fn(whi[:, slot], raw[:, (j // 2) % 4, 2 * (j % 2):2 * (j % 2) + 2], ACT.Copy).then_inc(hi_ready, 1)

            def rsqrt(src, dst, width, eps, ready, ln_sem, rs_sem, n):
                act.wait_ge(ready, n)
                fn(dst, src, ACT.Ln, scale=1.0 / width, bias=eps).then_inc(ln_sem, 1)
                act.wait_ge(ln_sem, n)
                fn(dst, dst, ACT.Exp, scale=-0.5).then_inc(rs_sem, 1)

            def norm_rows(blocks):
                act.wait_ge(norm_rs, 1)
                for b in blocks:
                    fn(normed[:, 0, b * NB:(b + 1) * NB], resid[:, 0, b * NB:(b + 1) * NB], ACT.Copy,
                       scale=rs_x[:, 0:1]).then_inc(normed_act, 1)

            def norm_pair(pair, col, n):
                act.wait_ge(norm_T, 8 * (n - 1) + pair + 1)
                for k in (2 * pair, 2 * pair + 1):
                    last = fn(hT[:, k, 0], (stage, stage2)[n - 1](pair)[:, (k % 2) * T:(k % 2 + 1) * T], ACT.Copy,
                              scale=cols[:, col + k:col + k + 1])
                last.then_inc(norm_hi, 1)

            def decay_inputs(j):
                if j == 5:
                    act.wait_ge(wlr_landed, 16)
                    fn(wlr_hi[:, :, :], wlr_raw[:, :, 0:GLA_RANK], ACT.Copy).then_inc(wlr_hi_ready, 1)
                if j == 11:
                    act.wait_ge(lr_done, 1)
                    fn(lrT[0:GLA_RANK, :], mix[0:GLA_RANK, 0:T], ACT.Copy).then_inc(lr_ready, 1)
                if j in (12, 13):
                    act.wait_ge(gk_done, j - 11)
                    for k in range(4 * (j - 12), 4 * (j - 12) + 4):
                        last = fn(gkx[:, k], (acc_c, mix)[k // 4][:, (k % 4) * T:(k % 4 + 1) * T], ACT.Identity,
                                  bias=cols[:, V_BGK + k:V_BGK + k + 1])
                    last.then_inc(gkx_ready, 1)

            def decays(h, n):
                if n is not None:
                    act.wait_ge(gk_gate, n - 1)
                fn(dec[:, :, :], gkx[:, bass.ds(2 * h, 2), :], ACT.Abs).then_inc(gk_abs, 1)
                act.wait_ge(gk_abs, h + 1)
                fn(dec[:, :, :], dec[:, :, :], ACT.Exp, scale=-1.0).then_inc(gk_exp, 1)
                act.wait_ge(gk_exp, h + 1)
                fn(dec[:, :, :], dec[:, :, :], ACT.Ln, bias=one_c).then_inc(gk_ln, 1)

            def exponentials(h, first_head):
                act.wait_ge(bl_ready, h + 1)
                if not first_head:
                    act.wait_ge(operands_ready, h)
                s = 1.0 / GLA_NORMALIZER
                fn(e_pos[:, :, :], cum[:, :, :], ACT.Exp, scale=s)
                fn(e_neg[:, :, :], cum[:, :, :], ACT.Exp, scale=-s)

            def exponentials_tail(h):
                s = 1.0 / GLA_NORMALIZER
                for f in range(2):
                    for c in range(2):
                        fn(e_tail[:, f, c], cum[:, f, 2 * c * C:(2 * c + 1) * C], ACT.Exp, scale=-s,
                           bias=bl[:, 4 * f + 2 * c:4 * f + 2 * c + 1])
                    fn(e_tile[:, f, 0:C], cum[:, f, 0:C], ACT.Exp, scale=-s, bias=bl01[:, f:f + 1])
                    fn(e_tile[:, f, C:P], cum[:, f, C:P], ACT.Exp, scale=-s, bias=bl[:, 4 * f + 1:4 * f + 2])
                    last = fn(e_q3[:, f], cum[:, f, 3 * C:4 * C], ACT.Exp, scale=s, bias=bl[:, 4 * f + 2:4 * f + 3])
                last.then_inc(e_ready, 1)

            def gla(h, tail):
                first = GLA_N * h + GLA0
                first_head = tail is None
                at_decays, at_exp, at_exp_tail = (14, 15, 16) if first_head else (0, 5, 6)
                at_AT = 20 if first_head else 18
                for j in range(GLA_N):
                    split_hi(first, j)
                    if first_head and j < HALF:
                        norm_pair(2 * j, V_N1, 1)
                        norm_pair(2 * j + 1, V_N1, 1)
                    if first_head and j < 2:
                        norm_rows((j + 2,))
                    if first_head:
                        decay_inputs(j)
                    if j == at_decays:
                        if first_head:
                            act.wait_ge(gkx_ready, 2)
                        decays(h, None if first_head else h + 1)
                    if j == at_exp:
                        exponentials(h, first_head)
                    if j == at_exp_tail:
                        exponentials_tail(h)
                    if first_head and j == 9:
                        rope_and_lambda()
                    if j == 19:
                        act.wait_ge(pieces_used, first + 2 * BLOCK)
                        if not first_head:
                            act.wait_ge(go_done, h)
                        fn(gv_hi[:, :, :], acc_a[:, :].rearrange("p (t n) -> p t n", t=TT), ACT.Copy).then_inc(gv_hi_ready, 1)
                    if j == at_AT:
                        act.wait_ge(AT_ready, h + 1)
                        fn(AT_hi[:, :, :], AT[:, :, :], ACT.Copy).then_inc(AT_hi_ready, 1)
                    if j == 22:
                        act.wait_ge(go_done, h + 1)
                        if not first_head:
                            act.wait_ge(og_ready, h)
                        for t, ps in enumerate((mix[:, NB:2 * NB], mix[:, 0:NB])):
                            last = fn(g_on[:, t], ps, ACT.Square, accum_out=g_ss[:, t:t + 1])
                        last.then_inc(go_sumsq, 1)
                        rsqrt(g_ss, g_rs, GLA_DV, eps_c, go_sumsq, go_ln, go_rs, h + 1)
                    if j == 23:
                        act.wait_ge(go_rs, h + 1)
                        for t, ps in enumerate((mix[:, NB:2 * NB], mix[:, 0:NB])):
                            last = fn(g_on[:, t], ps, ACT.Copy, scale=g_rs[:, t:t + 1])
                        last.then_inc(go_normed, 1)
                    if tail is not None:
                        gla_tail(j, tail)

            def gla_tail(j, n):
                if j == 3:
                    act.wait_ge(pieces_used, GLA_N * n + GLA0)
                    fn(g_exp[:, :], acc_c[:, :], ACT.Exp, scale=-1.0).then_inc(gout_exp, 1)
                if j == 13:
                    act.wait_ge(og_T, n)
                    for f in range(4):
                        last = fn(glaT[:, bass.ds(4 * n - 4 + f, 1), 0].rearrange("p a t -> p (a t)"),
                                  mix[:, f * T:(f + 1) * T], ACT.Copy, scale=cols[:, V_GLA + f:V_GLA + f + 1])
                    last.then_inc(glaT_hi_ready, 1)

            def rope_and_lambda():
                nc.scalar.preload_act_table_set("trig_and_small")
                act.wait_ge(rope_arg, 1)
                fn(rope_t[:, 4], rope_t[:, 3], ACT.Sin)
                fn(rope_t[:, 5], rope_t[:, 3], ACT.Sin, scale=0.5).then_inc(rope_sin, 1)
                nc.scalar.preload_act_table_set("natural_log_exp_and_others")
                act.wait_ge(lam_dot, 1)
                fn(lam2, lam2, ACT.Exp).then_inc(lam_exp, 1)

            def diff(i, tail, gtail):
                first = DIFF_N * i + DIFF0
                for j in range(DIFF_N):
                    split_hi(first, j)
                    if tail is not None:
                        diff_tail(j, tail)
                    if gtail is not None:
                        gla_tail(j, gtail)
                    if j == 11:
                        act.wait_ge(pieces_used, first + BLOCK)
                        if gtail is None:
                            act.wait_ge(k_ss, i)
                        fn(sq[:, :, :], acc_a[:, :].rearrange("p (s d) -> p s d", d=DH), ACT.Square).then_inc(q_sq, 1)
                    if j == 12:
                        rsqrt(dq_ss, dq_rs, DH, eps_c, q_ss, q_ln, q_rs, i + 1)
                    if j == 20:
                        act.wait_ge(q_T, i + 1)
                        if gtail is None:
                            act.wait_ge(scores_done[1], i)
                        fn(qT[:, :, :], mix[:, :].rearrange("p (s t) -> p s t", t=T), ACT.Copy).then_inc(qT_ready, 1)
                    if j == 19:
                        act.wait_ge(pieces_used, first + 2 * BLOCK)
                        act.wait_ge(q_ss, i + 1)
                        fn(sq[:, :, :], acc_b[:, :].rearrange("p (s d) -> p s d", d=DH), ACT.Square).then_inc(k_sq, 1)
                    if j == 20:
                        rsqrt(dk_ss, dk_rs, DH, eps_c, k_ss, k_ln, k_rs, i + 1)

            def diff_tail(j, n):
                if j == 1:
                    act.wait_ge(k_T, n)
                    fn(kT[:, :, :], mix[:, :].rearrange("p (s t) -> p s t", t=T), ACT.Copy).then_inc(kT_ready, 1)
                if j == 3:
                    act.wait_ge(pieces_used, DIFF_N * n + DIFF0)
                    fn(dv_hi[:, :, :], acc_c[:, :].rearrange("p (t n) -> p t n", t=TT), ACT.Copy).then_inc(dv_hi_ready, 1)
                if j in (7, 10):
                    half = (7, 10).index(j)
                    act.wait_ge(max_ready[half], n)
                    for s in (2 * half, 2 * half + 1):
                        for t, a in enumerate((prob[:, s, 0:P], prob[:, s, P:3 * P])):
                            k = 2 * s + t
                            last = fn(a, a, ACT.Exp, scale=DH ** -0.5, bias=s_nmax[:, k:k + 1],
                                      accum_out=p_sum[:, k:k + 1])
                    last.then_inc(exp_ready[half], 1)
                if j == 14:
                    act.wait_ge(att_T, n)
                    for hh in range(2):
                        last = fn(attT_hi[:, hh], mix[:, hh * NB:hh * NB + 3 * P], ACT.Copy)
                    last.then_inc(attT_hi_ready, 1)
                if j == 16:
                    act.wait_ge(pv_done, n)
                    act.wait_ge(k_ss, n)
                    for k in range(4):
                        last = fn(d_on[:, k // 2, (k % 2) * T:(k % 2 + 1) * T], mix[:, k * T:(k + 1) * T], ACT.Square,
                                  accum_out=o_ss[:, k:k + 1])
                    last.then_inc(do_sumsq, 1)
                    rsqrt(o_ss, o_rs, 2 * DH, sub_eps_c, do_sumsq, do_ln, do_rs, n)
                if j == 22:
                    act.wait_ge(do_T, n)
                    for f in range(4):
                        last = fn(diffT[:, bass.ds(4 * n - 4 + f, 1), 0].rearrange("p a t -> p (a t)"),
                                  mix[:, f * T:(f + 1) * T], ACT.Copy, scale=cols[:, V_SUB + f % 2:V_SUB + f % 2 + 1])
                    last.then_inc(diffT_hi_ready, 1)

            def branch(g, tail, dtail):
                first = BR_N * g + BR0
                for j in range(BR_N):
                    split_hi(first, j)
                    if dtail is not None:
                        diff_tail(j, dtail)
                    if tail is not None:
                        branch_tail(j, tail)
                    if j == 23:
                        if dtail is not None:
                            nc.scalar.preload_act_table_set("sigmoid_and_others")
                        act.wait_ge(halves_summed, BR_HALVES * g + 4)
                        fn(gate_g[:, :, :], gate_g[:, :, :], ACT.Sigmoid)
                        fn(gate_d[:, :, :], gate_d[:, :, :], ACT.Sigmoid).then_inc(gates_ready, 1)

            def branch_tail(j, n):
                if j == 4:
                    act.wait_ge(mixed_ready, n)
                    fn(mixT_hi[:, bass.ds(4 * n - 4, 4), :], gate_g[:, :, :], ACT.Copy).then_inc(mixT_hi_ready, 1)

            def out_sumsq(b):
                act.wait_ge(x1_ready, b + 1)
                if b >= 1:
                    act.wait_ge(x1_sumsq, b)
                for t in range(TT):
                    last = fn(gate_g[:, 2 * t:2 * t + 2].rearrange("p a t -> p (a t)"), resid[:, t, b * NB:(b + 1) * NB],
                              ACT.Square, accum_out=ss_out[:, 4 * t + b:4 * t + b + 1])
                last.then_inc(x1_sumsq, 1)

            def norm2_block(b):
                norm_pair(2 * b, V_N2, 2)
                norm_pair(2 * b + 1, V_N2, 2)

            def ffn_conv(j, f):
                if j in (8, 12):
                    half = (8, 12).index(j)
                    act.wait_ge(halves_scaled, 4 * f + (half + 1))
                    if not (isinstance(f, int) and f == 0):
                        act.wait_ge(hid_lo_ready, f)
                    for k in (2 * half, 2 * half + 1):
                        last = fn(conv[:, k], up_sum[:, k], ACT.Identity,
                                  scale=cols[:, bass.ds(f * 4 + (V_CW2 + k), 1)],
                                  bias=cols[:, bass.ds(f * 4 + (V_CB + k), 1)])
                    last.then_inc(conv_first, 1)
                if j in (11, 15):
                    half = (11, 15).index(j)
                    act.wait_ge(conv_ready, 2 * f + (half + 1))
                    a = conv[:, 2 * half:2 * half + 2]
                    fn(a, a, ACT.Silu).then_inc(conv_silu, 1)

            def hidden_hi(n, dst):
                act.wait_ge(hid_ready, n)
                if dst is hid_hi:
                    act.wait_ge(pieces_used, ffn_base(n) - BLOCK)
                fn(dst[:, :, :], conv[:, :, :], ACT.Copy).then_inc(hid_hi_ready, 1)

            nc.scalar.preload_act_table_set("natural_log_exp_and_others")
            act.wait_ge(x_landed[0], 16)
            fn(normed[:, 0], resid[:, 0], ACT.Square, accum_out=ss_x[:, 0:1]).then_inc(sumsq_act, 1)
            act.wait_ge(x_landed[1], 32)
            fn(normed[:, 1, 0:D // 2], resid[:, 1, 0:D // 2], ACT.Square, accum_out=ss_half[:, 0:1]).then_inc(sumsq_act, 1)
            act.wait_ge(consts_ready, 1)
            act.wait_ge(sumsq_dve, 1)
            rsqrt(ss_x, rs_x, D, eps_c, sumsq_dve, norm_ln, norm_rs, 1)
            norm_rows((0, 1))
            act.wait_ge(cols_ready, 1)

            gla(0, None)
            with act.Fori(1, GLA_HEADS) as h:
                gla(h, h)
            diff(0, None, GLA_HEADS)
            with act.Fori(1, DIFF_PAIRS) as i:
                diff(i, i, None)
            branch(0, None, DIFF_PAIRS)
            with act.Fori(1, GROUPS) as g:
                branch(g, g, None)
            for j in range(4 * BLOCK):
                split_hi(OUT0, j)
                branch_tail(j, GROUPS)
                if j == 8:
                    nc.scalar.preload_act_table_set("natural_log_exp_and_others")
                if j % 8 == 4 and j > 4:
                    out_sumsq(j // 8 - 1)
                if j % 8 == 6 and j > 8:
                    norm2_block(j // 8 - 1)
            for j in range(2 * BLOCK):
                if j == 4:
                    norm2_block(3)
                split_hi(FFN0, j)
                if j == 3:
                    out_sumsq(3)
                if j == 5:
                    rsqrt(ss_x, rs_x, D, eps_c, sumsq_dve, norm_ln, norm_rs, 2)
                if j == 7:
                    nc.scalar.preload_act_table_set("silu_and_others")
                ffn_conv(j, 0)
            with act.Fori(1, LAST) as f:
                for j in range(FFN_N):
                    split_hi(ffn_base(f), j)
                    if j == 4:
                        hidden_hi(f, hid_hi)
                    ffn_conv(j, f)
            for j in range(FFN_N):
                split_hi(ffn_base(LAST), j)
                if j == 4:
                    hidden_hi(LAST, hid_hi)
                ffn_conv(j, LAST)
                if j == 21:
                    hidden_hi(FFN_GROUPS, last_hi)
            for j in range(BLOCK):
                split_hi(END0, j)

        @block.vector
        def _(dve):
            V = nc.vector

            def split_lo(first, j):
                slot = j % 4
                dve.wait_ge(hi_ready, first + j + 1)
                V.tensor_tensor(wlo[:, slot], raw[:, (j // 2) % 4, 2 * (j % 2):2 * (j % 2) + 2],
                                whi[:, slot].bitcast(F32), ALU.subtract).then_inc(lo_ready, 1)

            def norm_rows():
                dve.wait_ge(norm_rs, 1)
                for b in range(4):
                    V.tensor_scalar(normed[:, 1, b * NB:(b + 1) * NB], resid[:, 1, b * NB:(b + 1) * NB], rs_x[:, 1:2], None,
                                    ALU.mult).then_inc(normed_dve, 1)

            def out_of(acc, dst):
                return V.tensor_reduce(dst, acc[:, :].rearrange("p (f s t) -> p f t s", f=2, s=2), AX.X, ALU.add)

            def norm_pair(pair, col, n):
                dve.wait_ge(norm_hi, 8 * (n - 1) + pair + 1)
                for k in (2 * pair, 2 * pair + 1):
                    src = (stage, stage2)[n - 1](pair)[:, (k % 2) * T:(k % 2 + 1) * T]
                    last = V.scalar_tensor_tensor(out=hT[:, k, 1], in0=src,
                                                  scalar=cols[:, col + k:col + k + 1], in1=hT[:, k, 0].bitcast(F32),
                                                  op0=ALU.mult, op1=ALU.subtract)
                last.then_inc(norm_lo, 1)

            def rope_and_lambda():
                n_rope = [0]
                dve.wait_ge(small_landed, 8 * 16)

                def then(ins):
                    n_rope[0] += 1
                    ins.then_inc(rope_step, 1)
                    dve.wait_ge(rope_step, n_rope[0])

                pos, ang, turns, red = (rope_t[:, k] for k in range(4))
                then(V.tensor_copy(pos[:, :, 0], pos_i.bitcast(I32)))
                for t in range(TT):
                    ins = V.tensor_scalar(ang[:, t], inv_f, pos[:, t, 0:1], None, ALU.mult)
                then(ins)
                for unit in (4096.0, 1.0):
                    src = ang
                    then(V.tensor_scalar(turns, src, 1.0 / (2.0 * math.pi * unit), None, ALU.mult))
                    then(V.tensor_scalar(turns, turns, ROUND, None, ALU.add))
                    then(V.tensor_scalar(turns, turns, -ROUND, None, ALU.add))
                    for piece in TWO_PI:
                        then(V.scalar_tensor_tensor(out=ang, in0=turns, scalar=-piece * unit, in1=ang,
                                                    op0=ALU.mult, op1=ALU.add))
                pi = float(np.nextafter(np.float32(math.pi), np.float32(0)))
                V.tensor_scalar(red, ang, pi, -pi, ALU.min, ALU.max).then_inc(rope_arg, 1)
                for k in range(2):
                    ins = V.tensor_tensor_reduce(lam_p[:, k], lam_v[:, 2 * k], lam_v[:, 2 * k + 1], 1.0, 0.0,
                                                 ALU.mult, ALU.add, lam2[:, k:k + 1])
                ins.then_inc(lam_dot, 1)

            def rope_and_lambda_end():
                dve.wait_ge(rope_sin, 1)
                V.scalar_tensor_tensor(out=rope_t[:, 5], in0=rope_t[:, 5], scalar=-2.0, in1=rope_t[:, 5],
                                       op0=ALU.mult, op1=ALU.mult).then_inc(rope_ready, 1)
                dve.wait_ge(rope_ready, 1)
                V.tensor_scalar(rope_t[:, 5], rope_t[:, 5], 1.0, None, ALU.add).then_inc(rope_ready, 1)
                dve.wait_ge(lam_exp, 1)
                V.tensor_tensor(neg_lam, lam2[:, 1:2], lam2[:, 0:1], ALU.subtract).then_inc(lam_ready, 1)
                dve.wait_ge(lam_ready, 1)
                V.tensor_scalar(neg_lam, neg_lam, -LAMBDA_INIT, None, ALU.add).then_inc(lam_ready, 1)

            def cumulate(h, first_head):
                if not first_head:
                    dve.wait_ge(cum_ready, h)
                    dve.wait_ge(go_done, h)
                else:
                    dve.wait_ge(gkx_ready, 2)
                V.tensor_scalar(gmin[:, :, :], gkx[:, bass.ds(2 * h, 2), :], 0.0, None, ALU.min).then_inc(gk_min, 1)
                dve.wait_ge(gk_min, h + 1)
                dve.wait_ge(gk_ln, h + 1)
                V.tensor_tensor(gmin[:, :, :], gmin[:, :, :], dec[:, :, :], ALU.subtract).then_inc(gk_gate, 1)
                dve.wait_ge(gk_gate, h + 1)
                if not first_head:
                    dve.wait_ge(e_ready, h)
                for f in range(2):
                    last = V.tensor_tensor_scan(cum[:, f], reset[:, :], gmin[:, f], 0.0, ALU.mult, ALU.add)
                last.then_inc(cum_ready, 1)
                dve.wait_ge(cum_ready, h + 1)
                V.tensor_scalar(bl.rearrange("p (f c) -> p f c", f=2),
                                cum[:, :, :].rearrange("p f (c t) -> p f c t", t=C)[:, :, :, C - 1],
                                1.0 / GLA_NORMALIZER, None, ALU.mult).then_inc(bl_scaled, 1)
                dve.wait_ge(bl_scaled, h + 1)
                b4 = bl.rearrange("p (f c) -> p f c", f=2)
                V.tensor_tensor(bl01, b4[:, :, 0], b4[:, :, 1], ALU.add).then_inc(bl_ready, 1)

            def gla(h, tail):
                first = GLA_N * h + GLA0
                first_head = tail is None
                qp, kp = q_sum[:, :, :], k_sum[:, :, :]
                at_cum, at_operands, at_AT = (15, 16, 19) if first_head else (2, 11, 17)
                for j in range(GLA_N):
                    split_lo(first, j)
                    if first_head and j < HALF:
                        norm_pair(2 * j, V_N1, 1)
                        norm_pair(2 * j + 1, V_N1, 1)
                    if first_head and j == 5:
                        dve.wait_ge(wlr_hi_ready, 1)
                        V.tensor_tensor(wlr_lo[:, :, :], wlr_raw[:, :, 0:GLA_RANK], wlr_hi[:, :, :].bitcast(F32), ALU.subtract)\
                         .then_inc(wlr_lo_ready, 1)
                    if j == at_cum:
                        cumulate(h, first_head)
                    if first_head and j == 7:
                        rope_and_lambda()
                    if j == 7:
                        dve.wait_ge(pieces_used, first + HALF)
                        if not first_head:
                            dve.wait_ge(go_done, h)
                        out_of(acc_a, q_sum[:, :, :]).then_inc(q_summed, 1)
                    if j == 11:
                        dve.wait_ge(pieces_used, first + BLOCK)
                        out_of(acc_b, k_sum[:, :, :]).then_inc(k_summed, 1)
                    if j == at_operands:
                        dve.wait_ge(q_summed, h + 1)
                        dve.wait_ge(k_summed, h + 1)
                        dve.wait_ge(e_ready, h + 1)
                        if not first_head:
                            dve.wait_ge(A_done, h)
                        V.scalar_tensor_tensor(out=q_dec[:, :, :], in0=qp, scalar=GLA_DK ** -0.5, in1=e_pos[:, :, :],
                                               op0=ALU.mult, op1=ALU.mult)
                        V.tensor_tensor(k_inv[:, :, :], kp, e_neg[:, :, :], ALU.mult)
                    if j == at_operands + 1:
                        def chunks(a, odd):
                            return a.rearrange("p f (c s t) -> p f c s t", s=2, t=C)[:, :, :, odd]
                        V.tensor_tensor(chunks(k_mix[:, :, :], 0), chunks(kp, 0), e_tail[:, :, :, :], ALU.mult)
                        V.tensor_tensor(chunks(k_mix[:, :, :], 1), chunks(kp, 1), chunks(e_neg[:, :, :], 1), ALU.mult)
                        V.tensor_tensor(k_tile[:, :, :], kp[:, :, 0:P], e_tile[:, :, :], ALU.mult)
                        V.scalar_tensor_tensor(out=q_3[:, :, :], in0=qp[:, :, 3 * C:4 * C], scalar=GLA_DK ** -0.5,
                                               in1=e_q3[:, :, :], op0=ALU.mult, op1=ALU.mult).then_inc(operands_ready, 1)
                    if first_head and j == 14:
                        rope_and_lambda_end()
                    if j == at_AT:
                        dve.wait_ge(A_done, h + 1)
                        if not first_head:
                            dve.wait_ge(AT_lo_ready, h)
                        V.tensor_copy(AT[:, 2], mix[:, 2 * P:3 * P])
                        dve.wait_ge(consts_ready, 1)
                        for t in range(TT):
                            last = V.copy_predicated(AT[:, t], keep[:, :].bitcast(U32), mix[:, t * P:(t + 1) * P])
                        last.then_inc(AT_ready, 1)
                    if j == at_AT + 1:
                        dve.wait_ge(AT_hi_ready, h + 1)
                        V.tensor_tensor(AT_lo[:, :, :], AT[:, :, :], AT_hi[:, :, :].bitcast(F32), ALU.subtract)\
                         .then_inc(AT_lo_ready, 1)
                    if j == 19:
                        dve.wait_ge(gv_hi_ready, h + 1)
                        dve.wait_ge(operands_ready, h + 1)
                        V.tensor_tensor(gv_lo[:, :, :], acc_a[:, :].rearrange("p (t n) -> p t n", t=TT),
                                        gv_hi[:, :, :].bitcast(F32), ALU.subtract).then_inc(gv_lo_ready, 1)
                    if tail is not None:
                        gla_tail(j, tail)

            def gla_tail(j, n):
                if j == 3:
                    dve.wait_ge(gout_exp, n)
                    V.tensor_scalar(g_exp[:, :], g_exp[:, :], 1.0, None, ALU.add).then_inc(gout_one, 1)
                if j == 4:
                    dve.wait_ge(gout_one, n)
                    V.reciprocal(g_exp[:, :], g_exp[:, :]).then_inc(gout_inv, 1)
                if j == 5:
                    dve.wait_ge(gout_inv, n)
                    V.tensor_tensor(g_silu[:, :, :].rearrange("p t n -> p (t n)"), acc_c[:, :], g_exp[:, :],
                                    ALU.mult).then_inc(gout_silu, 1)
                if j == 13:
                    dve.wait_ge(glaT_hi_ready, n)
                    for f in range(4):
                        last = V.scalar_tensor_tensor(
                            out=glaT[:, bass.ds(4 * n - 4 + f, 1), 1].rearrange("p a t -> p (a t)"),
                            in0=mix[:, f * T:(f + 1) * T], scalar=cols[:, V_GLA + f:V_GLA + f + 1],
                            in1=glaT[:, bass.ds(4 * n - 4 + f, 1), 0].rearrange("p a t -> p (a t)").bitcast(F32),
                            op0=ALU.mult, op1=ALU.subtract)
                    last.then_inc(glaT_lo_ready, 1)

            def head_sums(sq_sem, out_ss, done, n):
                dve.wait_ge(sq_sem, n)
                V.tensor_reduce(out_ss, sq[:, :, :], AX.X, ALU.add).then_inc(done, 1)

            def head_scale(acc, dst, rs, rs_sem, done, n, free_sem, free_n):
                dve.wait_ge(rs_sem, n)
                if free_n is not None:
                    dve.wait_ge(free_sem, free_n)
                V.tensor_tensor(dst[:, :, :, :].rearrange("p t s d -> p (t s) d"),
                                acc[:, :].rearrange("p (s d) -> p s d", d=DH),
                                rs.unsqueeze(2).broadcast_to([P, 8, DH]), ALU.mult).then_inc(done, 1)

            def diff(i, tail, gtail):
                first = DIFF_N * i + DIFF0
                for j in range(DIFF_N):
                    split_lo(first, j)
                    if tail is not None:
                        diff_tail(j, tail)
                    if gtail is not None:
                        gla_tail(j, gtail)
                    if j == 11:
                        head_sums(q_sq, dq_ss, q_ss, i + 1)
                    if j == 13:
                        head_scale(acc_a, qn, dq_rs, q_rs, q_normed, i + 1, q_T, i if gtail is None else None)
                    if j == 19:
                        head_sums(k_sq, dk_ss, k_ss, i + 1)
                    if j == 21:
                        head_scale(acc_b, kn, dk_rs, k_rs, k_normed, i + 1, k_T, i if gtail is None else None)

            def diff_tail(j, n):
                if j in (5, 8):
                    half = (5, 8).index(j)
                    dve.wait_ge(consts_ready, 1)
                    dve.wait_ge(scores_done[half], n)
                    for s in (2 * half, 2 * half + 1):
                        ps = mix[:, (s % 2) * NB:(s % 2) * NB + 3 * P]
                        for t, (a, b) in enumerate(((0, P), (P, 3 * P))):
                            k = 2 * s + t
                            last = V.tensor_tensor_reduce(prob[:, s, a:b], ps[:, a:b], causal[:, T - (b - a):T], 1.0, -3.0e38,
                                                          ALU.add, ALU.max, s_max[:, k:k + 1])
                    last.then_inc(max_found[half], 1)
                    dve.wait_ge(max_found[half], n)
                    V.tensor_scalar(s_nmax[:, 4 * half:4 * half + 4], s_max[:, 4 * half:4 * half + 4], -DH ** -0.5, None,
                                    ALU.mult).then_inc(max_ready[half], 1)
                if j == 11:
                    dve.wait_ge(exp_ready[0], n)
                    dve.wait_ge(exp_ready[1], n)
                    V.reciprocal(p_inv, p_sum).then_inc(sums_inv, 1)
                    dve.wait_ge(sums_inv, n)
                    V.tensor_scalar(p_lam.rearrange("p (h t) -> p h t", h=2),
                                    p_inv.rearrange("p (h s t) -> p h s t", h=2, s=2)[:, :, 1], neg_lam, None,
                                    ALU.mult).then_inc(sums_lam, 1)
                    dve.wait_ge(sums_lam, n)
                    spans = [(hh, t, a, b) for hh in range(2) for t, (a, b) in enumerate(((0, P), (P, 3 * P)))]
                    for hh, t, a, b in spans:
                        last = V.tensor_scalar(prob[:, 2 * hh + 1, a:b], prob[:, 2 * hh + 1, a:b],
                                               p_lam[:, 2 * hh + t:2 * hh + t + 1], None, ALU.mult)
                    last.then_inc(att_second, 1)
                    dve.wait_ge(att_second, n)
                    for hh, t, a, b in spans:
                        k = 4 * hh + t
                        last = V.scalar_tensor_tensor(out=att[:, hh, a:b], in0=prob[:, 2 * hh, a:b], scalar=p_inv[:, k:k + 1],
                                                      in1=prob[:, 2 * hh + 1, a:b], op0=ALU.mult, op1=ALU.add)
                    last.then_inc(att_ready, 1)
                if j == 12:
                    dve.wait_ge(att_ready, n)
                    dve.wait_ge(dv_hi_ready, n)
                    V.tensor_tensor(dv_lo[:, :, :], acc_c[:, :].rearrange("p (t n) -> p t n", t=TT),
                                    dv_hi[:, :, :].bitcast(F32), ALU.subtract).then_inc(dv_lo_ready, 1)
                if j == 14:
                    dve.wait_ge(attT_hi_ready, n)
                    for hh in range(2):
                        last = V.tensor_tensor(attT_lo[:, hh], mix[:, hh * NB:hh * NB + 3 * P],
                                               attT_hi[:, hh].bitcast(F32), ALU.subtract)
                    last.then_inc(attT_lo_ready, 1)
                if j == 17:
                    dve.wait_ge(do_rs, n)
                    for hh in range(2):
                        last = V.tensor_tensor(d_on[:, :, hh * T:(hh + 1) * T],
                                               mix[:, hh * NB:(hh + 1) * NB].rearrange("p (t e) -> p t e", t=TT),
                                               o_rs[:, 2 * hh:2 * hh + 2].unsqueeze(2).broadcast_to([P, TT, T]), ALU.mult)
                    last.then_inc(do_normed, 1)
                if j == 22:
                    dve.wait_ge(diffT_hi_ready, n)
                    for f in range(4):
                        last = V.scalar_tensor_tensor(
                            out=diffT[:, bass.ds(4 * n - 4 + f, 1), 1].rearrange("p a t -> p (a t)"),
                            in0=mix[:, f * T:(f + 1) * T], scalar=cols[:, V_SUB + f % 2:V_SUB + f % 2 + 1],
                            in1=diffT[:, bass.ds(4 * n - 4 + f, 1), 0].rearrange("p a t -> p (a t)").bitcast(F32),
                            op0=ALU.mult, op1=ALU.subtract)
                    last.then_inc(diffT_lo_ready, 1)

            def branch(g, tail, dtail):
                first = BR_N * g + BR0
                for j in range(BR_N):
                    split_lo(first, j)
                    if dtail is not None:
                        diff_tail(j, dtail)
                    if tail is not None:
                        branch_tail(j, tail)
                    if j in (7, 11, 15, 19):
                        half = (7, 11, 15, 19).index(j)
                        dve.wait_ge(pieces_used, first + HALF * (half + 1))
                        if tail is not None:
                            dve.wait_ge(mixT_hi_ready, g)
                            dve.wait_ge(mixT_lo_ready, g)
                        out_of((acc_a, acc_b)[half % 2],
                               (gate_g, gate_d)[half // 2][:, 2 * (half % 2):2 * (half % 2) + 2]).then_inc(halves_summed, 1)
                    if j in (23, 27, 31):
                        branch_gate((23, 27, 31).index(j), first, g + 1, dtail is not None)

            def branch_gate(half, first, n, after_diff):
                if half == 0 and after_diff:
                    dve.wait_ge(do_T, DIFF_PAIRS)
                elif half >= 2 or not after_diff:
                    dve.wait_ge(y_gated, 4 * n - 5 + half)
                dve.wait_ge(pieces_used, first + HALF * (half + 5))
                y = y_sum[:, half % 2]
                out_of((acc_a, acc_b)[half % 2], y).then_inc(halves_summed, 1)
                gate = (gate_g, gate_d)[half // 2][:, 2 * (half % 2):2 * (half % 2) + 2]
                dve.wait_ge(gates_ready, n)
                dve.wait_ge(halves_summed, BR_HALVES * n - 3 + half)
                V.tensor_tensor(gate, y, gate, ALU.mult).then_inc(y_gated, 1)

            def branch_tail(j, n):
                if j == 3:
                    branch_gate(3, BR_N * n + (BR0 - BR_N), n, False)
                    dve.wait_ge(y_gated, 4 * n)
                    V.tensor_tensor(gate_g[:, :, :], gate_g[:, :, :], gate_d[:, :, :], ALU.add).then_inc(mixed_ready, 1)
                if j == 4:
                    dve.wait_ge(mixT_hi_ready, n)
                    V.tensor_tensor(mixT_lo[:, bass.ds(4 * n - 4, 4), :], gate_g[:, :, :],
                                    mixT_hi[:, bass.ds(4 * n - 4, 4), :].bitcast(F32), ALU.subtract).then_inc(mixT_lo_ready, 1)

            def add_x(b):
                dve.wait_ge(pieces_used, OUT0 + (b + 1) * BLOCK)
                dve.wait_ge(resid_landed, 16)
                dst = resid[:, :, b * NB:(b + 1) * NB]
                V.tensor_tensor(dst, (acc_a, acc_b)[b % 2][:, :].rearrange("p (t n) -> p t n", t=TT), dst,
                                ALU.add).then_inc(x1_ready, 1)

            def ffn_half(acc, first, i, n):
                half = i % 2
                dve.wait_ge(pieces_used, first)
                if i >= 2:
                    dve.wait_ge(conv_ready, 2 * n)
                elif not (isinstance(n, int) and n == 1):
                    dve.wait_ge(hid_ready, n - 1)
                a = up_sum[:, 2 * half:2 * half + 2]
                out_of(acc, a).then_inc(halves_summed, 1)
                if isinstance(n, int) and n == 1:
                    dve.wait_ge(rs_row_ready, 1)
                dve.wait_ge(halves_summed, 4 * n + (FFN_HALF0 - 3 + i))
                V.tensor_tensor(a, a, rs_row[:, :].unsqueeze(1).broadcast_to([P, 2, T]), ALU.mult)\
                 .then_inc(halves_scaled, 1)

            def norm2_block(b):
                norm_pair(2 * b, V_N2, 2)
                norm_pair(2 * b + 1, V_N2, 2)

            def ffn_conv(j, f):
                base = FFN0 if isinstance(f, int) and f == 0 else ffn_base(f)
                for half in range(2):
                    if j == 7 + 4 * half:
                        ffn_half((acc_a, acc_b)[half], base + HALF * (half + 1), half, f + 1)
                    if j == 9 + 4 * half:
                        dve.wait_ge(halves_scaled, 4 * f + (half + 1))
                        dve.wait_ge(conv_first, 2 * f + (half + 1))
                        for k in (2 * half, 2 * half + 1):
                            last = V.scalar_tensor_tensor(out=conv[:, k, 1:T], in0=up_sum[:, k, 0:T - 1],
                                                          scalar=cols[:, bass.ds(f * 4 + (V_CW1 + k), 1)],
                                                          in1=conv[:, k, 1:T], op0=ALU.mult, op1=ALU.add)
                        last.then_inc(conv_second, 1)
                    if j == 10 + 4 * half:
                        dve.wait_ge(conv_second, 2 * f + (half + 1))
                        for k in (2 * half, 2 * half + 1):
                            last = V.scalar_tensor_tensor(out=conv[:, k, 2:T], in0=up_sum[:, k, 0:T - 2],
                                                          scalar=cols[:, bass.ds(f * 4 + (V_CW0 + k), 1)],
                                                          in1=conv[:, k, 2:T], op0=ALU.mult, op1=ALU.add)
                        last.then_inc(conv_ready, 1)

            def hidden(step, n, done, hi, lo):
                if step == 0:
                    ffn_half(acc_b, done, 3, n)
                if step == 1:
                    dve.wait_ge(conv_silu, 2 * n)
                    dve.wait_ge(halves_scaled, 4 * n)
                    V.tensor_tensor(conv[:, :, :], up_sum[:, :, :], conv[:, :, :], ALU.mult).then_inc(hid_ready, 1)
                if step == 2:
                    dve.wait_ge(hid_hi_ready, n)
                    V.tensor_tensor(lo[:, :, :], conv[:, :, :], hi[:, :, :].bitcast(F32), ALU.subtract)\
                     .then_inc(hid_lo_ready, 1)

            def add_down(first, q, n):
                dve.wait_ge(pieces_used, first + 2 * (q + 1))
                dst = resid[:, :, q * NB:(q + 1) * NB]
                V.tensor_tensor(dst, (acc_c, mix)[q % 2][:, :].rearrange("p (t n) -> p t n", t=TT), dst,
                                ALU.add).then_inc(down_added, 1)

            dve.wait_ge(x_landed[1], 32)
            V.tensor_tensor_reduce(normed[:, 1, D // 2:D], resid[:, 1, D // 2:D], resid[:, 1, D // 2:D], 1.0, 0.0,
                                   ALU.mult, ALU.add, ss_half[:, 1:2]).then_inc(sumsq_half, 1)
            dve.wait_ge(sumsq_half, 1)
            dve.wait_ge(sumsq_act, 2)
            V.tensor_tensor(ss_x[:, 1:2], ss_half[:, 0:1], ss_half[:, 1:2], ALU.add).then_inc(sumsq_dve, 1)
            dve.wait_ge(cols_T, 1)
            V.tensor_copy(cols[:, 0:90], mix[:, 0:90])
            V.tensor_copy(cols[:, 90:222], mix[:, 90:222]).then_inc(scale_ready, 1)
            dve.wait_ge(scale_ready, 1)
            V.tensor_scalar(cols[:, V_SUB:V_SUB + 2], cols[:, V_SUB:V_SUB + 2], 1.0 - LAMBDA_INIT, None,
                            ALU.mult).then_inc(cols_ready, 1)
            norm_rows()

            gla(0, None)
            with dve.Fori(1, GLA_HEADS) as h:
                gla(h, h)
            diff(0, None, GLA_HEADS)
            with dve.Fori(1, DIFF_PAIRS) as i:
                diff(i, i, None)
            branch(0, None, DIFF_PAIRS)
            with dve.Fori(1, GROUPS) as g:
                branch(g, g, None)
            for j in range(4 * BLOCK):
                split_lo(OUT0, j)
                branch_tail(j, GROUPS)
                if j % 8 == 3 and j > 3:
                    add_x(j // 8 - 1)
                if j % 8 == 6 and j > 8:
                    norm2_block(j // 8 - 1)
            for j in range(2 * BLOCK):
                if j == 4:
                    norm2_block(3)
                if j == 3:
                    add_x(3)
                split_lo(FFN0, j)
                if j == 4:
                    dve.wait_ge(x1_sumsq, 4)
                    V.tensor_reduce(ss_x, ss_out.rearrange("p (t b) -> p t b", t=TT), AX.X, ALU.add).then_inc(sumsq_dve, 1)
                if j == 5:
                    dve.wait_ge(norm_rs, 2)
                    for t in range(TT):
                        V.tensor_scalar(rs_diag[:, t], ident[:, :], rs_x[:, t:t + 1], None, ALU.mult).then_inc(diag_ready, 1)
                if j == 7:
                    dve.wait_ge(rs_spread, 1)
                    V.tensor_copy(rs_row[:, :], acc_c[:, 0:T]).then_inc(rs_row_ready, 1)
                ffn_conv(j, 0)
                if j == 15:
                    ffn_half(acc_a, FFN0 + 3 * HALF, 2, 1)
            with dve.Fori(1, LAST) as f:
                for j in range(FFN_N):
                    split_lo(ffn_base(f), j)
                    if j in (3, 4, 5):
                        hidden(j - 3, f, ffn_base(f), hid_hi, hid_lo)
                    ffn_conv(j, f)
                    if j in (13, 15, 17, 19):
                        add_down(ffn_base(f) + BLOCK, (j - 13) // 2, f)
                    if j == 23:
                        ffn_half(acc_a, ffn_base(f) + 5 * HALF, 2, f + 1)
            for j in range(FFN_N):
                split_lo(ffn_base(LAST), j)
                if j in (3, 4, 5):
                    hidden(j - 3, LAST, ffn_base(LAST), hid_hi, hid_lo)
                ffn_conv(j, LAST)
                if j == 15:
                    ffn_half(acc_a, ffn_base(LAST) + 3 * HALF, 2, FFN_GROUPS)
                if j in (19, 20, 22):
                    hidden((19, 20, 22).index(j), FFN_GROUPS, ffn_base(LAST) + 2 * BLOCK, last_hi, last_lo)
                if j in (21, 23):
                    add_down(ffn_base(LAST) + 2 * BLOCK, (j - 21) // 2, LAST)
            for j in range(BLOCK):
                split_lo(END0, j)
                if j in (1, 3):
                    add_down(ffn_base(LAST) + 2 * BLOCK, (j + 3) // 2, LAST)
                if j in (5, 7):
                    add_down(END0, (j - 5) // 2, FFN_GROUPS)
            add_down(END0, 2, FFN_GROUPS)
            for t in range(TT):
                dve.wait_ge(last_tile_done, t + 1)
                dst = resid[:, t, 3 * NB:4 * NB]
                V.tensor_tensor(dst, mix[:, t * NB:(t + 1) * NB], dst, ALU.add).then_inc(down_added, 1)

        @block.gpsimd
        def _(pool):
            G = nc.gpsimd
            G.memset(ident[:, :], 0.0)
            G.memset(keep[:, :], 1.0)
            G.memset(causal[:, :], 0.0)
            G.memset(AT[:, :, :], 0.0)
            G.memset(reset[:, :], 1.0)
            G.memset(cols[:, :], 0.0)
            G.memset(eps_c, EPS)
            G.memset(sub_eps_c, SUBLN_EPS)
            G.memset(one_c, 1.0)
            for k in range(ROPE // 2):
                f = float(np.float32(ROPE_THETA) ** (-np.float32(2 * k) / np.float32(ROPE)))
                last = G.memset(inv_f[:, k:k + 1], f)
            last.then_inc(const_step, 1)
            pool.wait_ge(const_step, 1)
            G.affine_select(out=ident[:, :], in_=ident[:, :], compare_op=ALU.not_equal, fill=1.0, base=0,
                            pattern=[[-1, P]], channel_multiplier=1)
            G.affine_select(out=keep[:, :], in_=keep[:, :], compare_op=ALU.is_ge, fill=0.0, base=0,
                            pattern=[[1, P]], channel_multiplier=-1)
            G.affine_select(out=causal[:, P:T], in_=causal[:, P:T], compare_op=ALU.is_ge, fill=-1.0e30, base=0,
                            pattern=[[-1, P]], channel_multiplier=1)
            G.memset(reset[:, :].rearrange("p (c t) -> p c t", t=C)[:, :, 0:1], 0.0).then_inc(consts_ready, 1)

            def gla_tail(n):
                pool.wait_ge(go_normed, n)
                pool.wait_ge(gout_silu, n)
                if not (isinstance(n, int) and n == 1):
                    pool.wait_ge(og_T, n - 1)
                G.tensor_tensor(g_og[:, :, :], g_on[:, :, :], g_silu[:, :, :], ALU.mult).then_inc(og_ready, 1)

            def turn(buf, which, normed_sem, scaled, turned, roped, n):
                v = buf[:, :, :, :].rearrange("p t s d -> p (t s) d")
                pool.wait_ge(normed_sem, n)
                G.tensor_tensor(v, v, qk_g[:, which].unsqueeze(1).broadcast_to([P, 8, DH]), ALU.mult).then_inc(scaled, 1)
                pool.wait_ge(scaled, n)
                H = ROPE // 2
                sin = rope_t[:, 4].unsqueeze(2).broadcast_to([P, TT, 4, H])
                cos = rope_t[:, 5].unsqueeze(2).broadcast_to([P, TT, 4, H])
                x1, x2 = buf[:, :, :, 0:H], buf[:, :, :, H:2 * H]
                r = [rot[:, k].rearrange("p (t s) h -> p t s h", t=TT) for k in range(4)]
                G.tensor_tensor(r[0], x1, cos, ALU.mult)
                G.tensor_tensor(r[1], x2, sin, ALU.mult)
                G.tensor_tensor(r[2], x2, cos, ALU.mult)
                G.tensor_tensor(r[3], x1, sin, ALU.mult).then_inc(turned, 1)
                pool.wait_ge(turned, n)
                G.tensor_tensor(x1, r[0], r[1], ALU.subtract)
                G.tensor_tensor(x2, r[2], r[3], ALU.add).then_inc(roped, 1)

            def diff(n):
                turn(qn, 0, q_normed, q_scaled, q_turned, q_roped, n)
                pool.wait_ge(q_roped, n)
                turn(kn, 1, k_normed, k_scaled, k_turned, k_roped, n)
                pool.wait_ge(k_roped, n)

            gla_tail(1)
            with pool.Fori(2, GLA_HEADS + 1) as n:
                gla_tail(n)
            pool.wait_ge(small_landed, 8 * 16)
            pool.wait_ge(rope_ready, 2)
            with pool.Fori(1, DIFF_PAIRS + 1) as n:
                diff(n)
            pool.wait_ge(pieces_used, OUT0)
            G.memset(ones[:, :], 1.0).then_inc(ones_ready, 1)

        @block.tensor
        def _(pe):
            mm = nc.tensor.matmul

            def features(first, j, acc, a):
                slot, k0 = j % 4, 4 * (j % HALF)
                pe.wait_ge(lo_ready, first + j + 1)
                hi, lo = (w[:, slot].rearrange("p k (a n) -> p (k a) n", n=HB) for w in (whi, wlo))
                for k in range(4):
                    kt = k0 + k
                    for f in range(2):
                        dst = acc[:, f * NB:(f + 1) * NB]
                        mm(dst, hi[:, k, f * P:(f + 1) * P], a[:, kt].rearrange("p s t -> p (s t)"),
                           start=(kt == 0), stop=False, skip_group_check=True)
                        last = mm(dst[:, 0:T], lo[:, k, f * P:(f + 1) * P], a[:, kt, 0], start=False,
                                  stop=(kt == KT - 1), skip_group_check=True)
                last.then_inc(pieces_used, 1)

            def tokens(first, j, k0, n_kt, acc, a_hi, a_lo):
                slot = j % 4
                pe.wait_ge(lo_ready, first + j + 1)
                for k in range(PIECE_KT):
                    kt = k0 + k
                    for t in range(TT):
                        dst = acc[:, t * NB:(t + 1) * NB]
                        hi, lo = a_hi[:, kt, t * P:(t + 1) * P], a_lo[:, kt, t * P:(t + 1) * P]
                        mm(dst, hi, whi[:, slot, k], start=(kt == 0), stop=False)
                        mm(dst, hi, wlo[:, slot, k], start=False, stop=False)
                        last = mm(dst, lo, whi[:, slot, k], start=False, stop=(kt == n_kt - 1))
                last.then_inc(pieces_used, 1)

            def product(dst, lhs, rhs, start, stop):
                mm(dst, lhs[0], rhs[0], start=start, stop=False)
                mm(dst, lhs[0], rhs[1], start=False, stop=False)
                return mm(dst, lhs[1], rhs[0], start=False, stop=stop)

            def transpose(dst, src, n=P):
                return nc.tensor.transpose(dst, src, ident[0:n, 0:n])

            def norm_transposes(pair):
                pe.wait_ge(normed_act, pair // 2 + 1)
                pe.wait_ge(normed_dve, pair // 2 + 1)
                if pair >= 6:
                    pe.wait_ge(norm_lo, pair - 5)
                for k in range(2):
                    for t in range(TT):
                        col = (2 * pair + k) * P
                        last = transpose(stage(pair)[:, k * T + t * P:k * T + (t + 1) * P], normed[:, t, col:col + P])
                last.then_inc(norm_T, 1)

            def normed_block(j):
                if j == 0:
                    for pair in range(6):
                        norm_transposes(pair)
                if j == 1:
                    for pair in (6, 7):
                        norm_transposes(pair)
                if j < HALF:
                    pe.wait_ge(norm_lo, 2 * j + 2)

            def norm2_transposes(b):
                if b == 0:
                    pe.wait_ge(dv_lo_ready, DIFF_PAIRS)
                    pe.wait_ge(diffT_lo_ready, DIFF_PAIRS)
                pe.wait_ge(x1_ready, b + 1)
                if b >= 2:
                    pe.wait_ge(norm_lo, KT // 2 + 2 * b - 2)
                for pair in (2 * b, 2 * b + 1):
                    for k in range(2):
                        for t in range(TT):
                            col = (2 * pair + k) * P
                            last = transpose(stage2(pair)[:, k * T + t * P:k * T + (t + 1) * P], resid[:, t, col:col + P])
                    last.then_inc(norm_T, 1)

            def decay_inputs(j):
                if j == 8:
                    pe.wait_ge(wlr_lo_ready, 1)
                    for k in range(KT):
                        mm(mix[0:GLA_RANK, 0:T], wlr_hi[:, k], hT[:, k, 0], start=(k == 0), stop=False)
                        mm(mix[0:GLA_RANK, 0:T], wlr_hi[:, k], hT[:, k, 1], start=False, stop=False)
                        last = mm(mix[0:GLA_RANK, 0:T], wlr_lo[:, k], hT[:, k, 0], start=False, stop=(k == KT - 1))
                    last.then_inc(lr_done, 1)
                if j == 10:
                    pe.wait_ge(lr_ready, 1)
                    pe.wait_ge(small_landed, 8 * 16)
                    for k in range(8):
                        last = mm((acc_c, mix)[k // 4][:, (k % 4) * T:(k % 4 + 1) * T], wup[0:GLA_RANK, k * P:(k + 1) * P],
                                  lrT[0:GLA_RANK, :], start=True, stop=True)
                        if k % 4 == 3:
                            last.then_inc(gk_done, 1)

            def gla(h, tail):
                first = GLA_N * h + GLA0
                first_head = tail is None
                at_A, at_o = (17, 20) if first_head else (13, 19)
                for j in range(GLA_N):
                    if tail is not None:
                        gla_tail(j, tail)
                    if first_head:
                        normed_block(j)
                        decay_inputs(j)
                        if j == 2 * BLOCK:
                            pe.wait_ge(gkx_ready, 1)
                    if j == at_A:
                        pe.wait_ge(operands_ready, h + 1)
                        if not first_head:
                            pe.wait_ge(glaT_lo_ready, h)
                        for dst, key, query in (
                                (0, k_inv[:, :, 0:P], q_dec[:, :, 0:C]), (C, k_mix[:, :, 0:P], q_dec[:, :, C:2 * C]),
                                (2 * C, k_inv[:, :, P:T], q_dec[:, :, 2 * C:3 * C]),
                                (3 * C, k_mix[:, :, P:T], q_dec[:, :, 3 * C:4 * C]),
                                (4 * C, k_tile[:, :, :], q_dec[:, :, 2 * C:3 * C]), (5 * C, k_tile[:, :, :], q_3[:, :, :])):
                            for f in range(2):
                                last = mm(mix[:, dst:dst + C], key[:, f], query[:, f], start=(f == 0), stop=(f == 1))
                        last.then_inc(A_done, 1)
                    if j == at_o:
                        pe.wait_ge(AT_lo_ready, h + 1)
                        pe.wait_ge(gv_lo_ready, h + 1)
                        a0, a1, a2 = ((AT_hi[:, k], AT_lo[:, k]) for k in range(3))
                        v0, v1 = ((gv_hi[:, t], gv_lo[:, t]) for t in range(TT))
                        product(mix[:, NB:2 * NB], a0, v0, True, True)
                        product(mix[:, 0:NB], a1, v1, True, False)
                        product(mix[:, 0:NB], a2, v0, False, True).then_inc(go_done, 1)
                    if j < HALF:
                        if j == 0 and not first_head:
                            pe.wait_ge(gv_lo_ready, h)
                        features(first, j, acc_a, hT)
                    elif j < BLOCK:
                        if j == HALF and not first_head:
                            pe.wait_ge(k_summed, h)
                        features(first, j, acc_b, hT)
                    elif j < 2 * BLOCK:
                        if j == BLOCK:
                            pe.wait_ge(q_summed, h + 1)
                        tokens(first, j, 2 * (j - BLOCK), KT, acc_a, hT[:, :, 0], hT[:, :, 1])
                    else:
                        if j == 2 * BLOCK and not first_head:
                            pe.wait_ge(gout_silu, h)
                        tokens(first, j, 2 * (j - 2 * BLOCK), KT, acc_c, hT[:, :, 0], hT[:, :, 1])

            def gla_tail(j, n):
                if j == 9:
                    pe.wait_ge(og_ready, n)
                    for f in range(4):
                        for t in range(TT):
                            last = transpose(mix[:, f * T + t * P:f * T + (t + 1) * P], g_og[:, t, f * P:(f + 1) * P])
                    last.then_inc(og_T, 1)

            def head_transposes(src):
                for s in range(4):
                    for t in range(TT):
                        last = transpose(mix[:, s * T + t * P:s * T + (t + 1) * P], src[:, t, s])
                return last

            def diff(i, tail, gtail):
                first = DIFF_N * i + DIFF0
                for j in range(DIFF_N):
                    if tail is not None:
                        diff_tail(j, tail, True, i)
                    if gtail is not None:
                        gla_tail(j, gtail)
                    if j == 17:
                        pe.wait_ge(q_roped, i + 1)
                        if tail is not None:
                            pe.wait_ge(do_normed, i)
                        else:
                            pe.wait_ge(glaT_lo_ready, GLA_HEADS)
                        head_transposes(qn).then_inc(q_T, 1)
                    if j == 22:
                        pe.wait_ge(k_roped, i + 1)
                        pe.wait_ge(qT_ready, i + 1)
                        if tail is not None:
                            pe.wait_ge(diffT_lo_ready, i)
                        head_transposes(kn).then_inc(k_T, 1)
                    b = j // BLOCK
                    if j == 0:
                        pe.wait_ge(gv_lo_ready if gtail is not None else q_normed, GLA_HEADS if gtail is not None else i)
                    if j == BLOCK:
                        pe.wait_ge(k_summed if gtail is not None else k_normed, GLA_HEADS if gtail is not None else i)
                    if j == 2 * BLOCK:
                        pe.wait_ge(gout_silu if gtail is not None else dv_lo_ready, GLA_HEADS if gtail is not None else i)
                    tokens(first, j, 2 * (j - b * BLOCK), KT, (acc_a, acc_b, acc_c)[b], hT[:, :, 0], hT[:, :, 1])

            def diff_tail(j, n, more, i):
                if j in (2, 5):
                    half = (2, 5).index(j)
                    if half == 0:
                        pe.wait_ge(qT_ready, n)
                        pe.wait_ge(kT_ready, n)
                    else:
                        pe.wait_ge(max_found[0], n)
                    for s in (2 * half, 2 * half + 1):
                        ps = mix[:, (s % 2) * NB:(s % 2) * NB + 3 * P]
                        mm(ps[:, 0:P], qT[:, s, 0:P], kT[:, s, 0:P], start=True, stop=True)
                        last = mm(ps[:, P:3 * P], qT[:, s, P:T], kT[:, s, :], start=True, stop=True)
                    last.then_inc(scores_done[half], 1)
                if j == 11:
                    pe.wait_ge(att_ready, n)
                    for hh in range(2):
                        for k in range(3):
                            last = transpose(mix[:, hh * NB + k * P:hh * NB + (k + 1) * P], att[:, hh, k * P:(k + 1) * P])
                    last.then_inc(att_T, 1)
                if j == 13:
                    pe.wait_ge(attT_lo_ready, n)
                    pe.wait_ge(dv_lo_ready, n)
                    for hh in range(2):
                        v0, v1 = ((dv_hi[:, t, hh * T:(hh + 1) * T], dv_lo[:, t, hh * T:(hh + 1) * T]) for t in range(TT))
                        a0, a1, a2 = ((attT_hi[:, hh, k * P:(k + 1) * P], attT_lo[:, hh, k * P:(k + 1) * P]) for k in range(3))
                        product(mix[:, hh * NB:hh * NB + T], a0, v0, True, True)
                        product(mix[:, hh * NB + T:hh * NB + 2 * T], a1, v0, True, False)
                        last = product(mix[:, hh * NB + T:hh * NB + 2 * T], a2, v1, False, True)
                    last.then_inc(pv_done, 1)
                if j == 19:
                    pe.wait_ge(do_normed, n)
                    if more:
                        pe.wait_ge(qT_ready, i + 1)
                    for f in range(4):
                        for t in range(TT):
                            last = transpose(mix[:, f * T + t * P:f * T + (t + 1) * P], d_on[:, t, f * P:(f + 1) * P])
                    last.then_inc(do_T, 1)

            def branch(g, tail, dtail):
                first = BR_N * g + BR0
                for j in range(BR_N):
                    if dtail is not None:
                        diff_tail(j, dtail, False, None)
                    half = j // HALF
                    if j % HALF == 0:
                        if dtail is not None and half < 2:
                            pe.wait_ge((q_normed, k_normed)[half], DIFF_PAIRS)
                        else:
                            pe.wait_ge(halves_summed, BR_HALVES * g + (half - 1))
                    if j == 3 * BLOCK and dtail is not None:
                        pe.wait_ge(diffT_lo_ready, DIFF_PAIRS)
                    features(first, j, (acc_a, acc_b)[half % 2], (hT, hT, glaT, diffT)[j // BLOCK])

            pe.wait_ge(consts_ready, 1)
            pe.wait_ge(rows_landed, 9 * 16)
            transpose(mix[:, 0:90], rows[0:90, 0, :], 90)
            transpose(mix[:, 90:178], rows[0:88, 1, :], 88)
            transpose(mix[:, 178:222], rows[0:44, 2, :], 44).then_inc(cols_T, 1)
            pe.wait_ge(cols_ready, 1)

            gla(0, None)
            with pe.Fori(1, GLA_HEADS) as h:
                gla(h, h)
            diff(0, None, GLA_HEADS)
            with pe.Fori(1, DIFF_PAIRS) as i:
                diff(i, i, None)
            branch(0, None, DIFF_PAIRS)
            with pe.Fori(1, GROUPS) as g:
                branch(g, g, None)
            for j in range(4 * BLOCK):
                b = j // BLOCK
                if j in (0, BLOCK):
                    pe.wait_ge(halves_summed, FFN_HALF0 - 1 + b)
                if j == 6:
                    pe.wait_ge(mixT_lo_ready, GROUPS)
                if j in (2 * BLOCK, 3 * BLOCK):
                    pe.wait_ge(x1_ready, b - 1)
                if j % BLOCK == 2 and b >= 1:
                    norm2_transposes(b - 1)
                tokens(OUT0, j, 2 * (j - b * BLOCK), KT, (acc_a, acc_b)[b % 2], mixT_hi, mixT_lo)
            for j in range(2 * BLOCK):
                if j == 0:
                    pe.wait_ge(x1_ready, 3)
                if j == 1:
                    norm2_transposes(3)
                if j < HALF:
                    pe.wait_ge(norm_lo, KT // 2 + 2 * j + 2)
                if j == 4:
                    pe.wait_ge(diag_ready, TT)
                    pe.wait_ge(ones_ready, 1)
                    for t in range(TT):
                        last = mm(acc_c[:, t * P:(t + 1) * P], ones[:, :], rs_diag[:, t], start=True, stop=True)
                    last.then_inc(rs_spread, 1)
                if j in (2 * HALF, 3 * HALF):
                    pe.wait_ge(halves_summed, FFN_HALF0 + j // HALF - 1)
                features(FFN0, j, (acc_a, acc_b)[(j // HALF) % 2], hT)

            def down(first, j, q_first, n, a_hi, a_lo):
                q, k0 = (j - q_first) // 2, 2 * (j % 2)
                if j == q_first:
                    pe.wait_ge(hid_lo_ready, n)
                if j % 2 == 0 and (q >= 2 or a_hi is last_hi):
                    pe.wait_ge(down_added, 4 * n - 5 + q)
                tokens(first, j, k0, 4, (acc_c, mix)[q % 2], a_hi, a_lo)

            def up(first, j, half, f):
                if j % HALF == 0:
                    pe.wait_ge(halves_summed, 4 * f + (FFN_HALF0 + half - 1))
                features(first, j, (acc_a, acc_b)[half % 2], hT)

            with pe.Fori(1, LAST) as f:
                for j in range(FFN_N):
                    if j < BLOCK:
                        up(ffn_base(f), j, j // HALF, f)
                    elif j < 2 * BLOCK:
                        down(ffn_base(f), j, BLOCK, f, hid_hi, hid_lo)
                    else:
                        up(ffn_base(f), j, j // HALF - 2, f)
            for j in range(FFN_N):
                if j < 2 * BLOCK:
                    up(ffn_base(LAST), j, j // HALF, LAST)
                else:
                    down(ffn_base(LAST), j, 2 * BLOCK, LAST, hid_hi, hid_lo)
            for j in range(BLOCK - 1):
                down(END0, j, 0, FFN_GROUPS, last_hi, last_lo)
            slot = (BLOCK - 1) % 4
            pe.wait_ge(lo_ready, END0 + BLOCK)
            for t in range(TT):
                for k in range(PIECE_KT):
                    dst = mix[:, t * NB:(t + 1) * NB]
                    hi, lo = (a[:, 2 + k, t * P:(t + 1) * P] for a in (last_hi, last_lo))
                    mm(dst, hi, whi[:, slot, k], start=False, stop=False)
                    mm(dst, hi, wlo[:, slot, k], start=False, stop=False)
                    last = mm(dst, lo, whi[:, slot, k], start=False, stop=(k == 1))
                last.then_inc(last_tile_done, 1)


_INS = ["x", "positions", "norm1_g", "w_in", "w_gk_up", "b_gk", "gla_norm_g", "q_norm_g", "k_norm_g",
        "lambda_q1", "lambda_k1", "lambda_q2", "lambda_k2", "subln_g", "w_branch", "w_out", "norm2_g",
        "w_ffn_up", "conv_w", "conv_b", "w_ffn_down"]


def kernel(**inputs):
    import numpy as _np
    import concourse.bacc as _bacc
    from concourse import mybir as _mybir
    from concourse.bass_utils import run_bass_kernel_spmd as _run

    nc = _bacc.Bacc("TRN2", target_bir_lowering=False, num_devices=1)
    arrays, args = {}, []
    for name in _INS:
        a = _np.ascontiguousarray(inputs[name])
        arrays[f"in_{name}_dram"] = a
        args.append(nc.dram_tensor(f"in_{name}_dram", a.shape, _mybir.dt.from_np(a.dtype), kind="ExternalInput").ap())
    out = nc.dram_tensor("out_0_dram", (1, T, D), F32, kind="ExternalOutput").ap()
    hybrid_block_kernel(nc, *args, out)
    r = _run(nc, [arrays], core_ids=[0])
    return r.results[0]["out_0_dram"]
```
